# Optimizing a Trainium2 kernel written in Bass

```python
import jax
import jax.numpy as jnp
from jax import lax
import numpy as np

D_MODEL = 1024
BATCH = 1
SEQ = 512
DEPTH = 2

GRID_W = 64
CTX_LEN = 256
NORM_EPS = 1e-6
ROPE_BASE = 10000.0
Q_BLOCK = 128

MLA_HEADS = 8
MLA_NOPE = 64
MLA_ROPE = 32
MLA_QK = MLA_NOPE + MLA_ROPE
MLA_V = 64
MLA_Q_RANK = 384
MLA_KV_RANK = 256

RET_HEADS = 4
RET_DK = 64
RET_DV = 64
RET_CHUNK = 128
RET_EPS = 1e-5

RWKV_HEADS = 4
RWKV_N = 64
RWKV_DECAY_LORA = 64
RWKV_A_LORA = 64
RWKV_G_LORA = 128
RWKV_EPS = 64e-5
RWKV_DECAY_SCALE = 0.606531

N_EXPERTS = 16
EC_FACTOR = 2
EXPERT_FF = 1024

MLA_W = MLA_HEADS * MLA_V
RET_W = RET_HEADS * RET_DV
RWKV_W = RWKV_HEADS * RWKV_N
MIX_W = MLA_W + RET_W + RWKV_W

MLA_COLS = MLA_Q_RANK + MLA_KV_RANK + MLA_ROPE
RET_COLS = 2 * RET_HEADS * RET_DK + 2 * RET_W
RWKV_COLS = 3 * RWKV_W + 2 * RWKV_DECAY_LORA + RWKV_A_LORA + RWKV_G_LORA
IN_COLS = MLA_COLS + RET_COLS + RWKV_COLS
RWKV_SPLITS = [RWKV_W, 2 * RWKV_W, 3 * RWKV_W, 3 * RWKV_W + RWKV_DECAY_LORA,
               3 * RWKV_W + 2 * RWKV_DECAY_LORA, 3 * RWKV_W + 2 * RWKV_DECAY_LORA + RWKV_A_LORA]

kernel_name = 'hybrid_mla_retention_rwkv7_ecmoe_dit'

def rms_norm(x, w, eps=NORM_EPS):
    xf = x.astype(jnp.float32)
    y = xf * lax.rsqrt(jnp.mean(xf * xf, axis=-1, keepdims=True) + eps)
    return (y * w.astype(jnp.float32)).astype(x.dtype)

def head_layer_norm(y, w, n_heads, eps):
    shp = y.shape
    yf = y.astype(jnp.float32).reshape(shp[:-1] + (n_heads, shp[-1] // n_heads))
    mu = jnp.mean(yf, axis=-1, keepdims=True)
    var = jnp.mean(jnp.square(yf - mu), axis=-1, keepdims=True)
    yf = ((yf - mu) * lax.rsqrt(var + eps)).reshape(shp)
    return (yf * w.astype(jnp.float32)).astype(y.dtype)

def rotate_half_pairs(x, cos, sin):
    p = x.shape[-1] // 2
    c = cos[:, None, :].astype(x.dtype)
    s = sin[:, None, :].astype(x.dtype)
    x1, x2 = x[..., :p], x[..., p:]
    return jnp.concatenate([x1 * c - x2 * s, x1 * s + x2 * c], axis=-1)

def axial_rope_tables(rows):
    row = jnp.repeat(jnp.arange(rows, dtype=jnp.float32), GRID_W)
    col = jnp.tile(jnp.arange(GRID_W, dtype=jnp.float32), rows)
    n_freq = MLA_ROPE // 4
    inv = ROPE_BASE ** (-jnp.arange(n_freq, dtype=jnp.float32) / n_freq)
    ang = jnp.concatenate([row[:, None] * inv, col[:, None] * inv], axis=-1)
    return jnp.cos(ang), jnp.sin(ang)

def seq_rope_tables(pos):
    inv = ROPE_BASE ** (-jnp.linspace(0.0, 1.0, RET_DK // 2, dtype=jnp.float32))
    ang = pos.astype(jnp.float32)[:, None] * inv
    return jnp.cos(ang), jnp.sin(ang)

def token_shift(p, mu):
    zero = jnp.zeros_like(p[:, :1])
    prev = jnp.concatenate([zero, p[:, :-1]], axis=1)
    nxt = jnp.concatenate([p[:, 1:], zero], axis=1)
    return p + (0.5 * (prev + nxt) - p) * mu.astype(p.dtype)

def mla_project(cq, ckv, k_rope, q_norm_w, w_uq, kv_norm_w, w_ukv, q_gain, k_gain, rope):
    b, t, _ = cq.shape
    q = (rms_norm(cq, q_norm_w) @ w_uq).reshape(b, t, MLA_HEADS, MLA_QK)
    kv = (rms_norm(ckv, kv_norm_w) @ w_ukv).reshape(b, t, MLA_HEADS, MLA_NOPE + MLA_V)
    k_nope, v = kv[..., :MLA_NOPE], kv[..., MLA_NOPE:]
    k_r = jnp.broadcast_to(k_rope[:, :, None, :], (b, t, MLA_HEADS, MLA_ROPE))
    k = jnp.concatenate([k_nope, k_r], axis=-1)
    q = rms_norm(q, q_gain)
    k = rms_norm(k, k_gain)
    if rope is not None:
        cos, sin = rope
        q = jnp.concatenate([q[..., :MLA_NOPE], rotate_half_pairs(q[..., MLA_NOPE:], cos, sin)], axis=-1)
        k = jnp.concatenate([k[..., :MLA_NOPE], rotate_half_pairs(k[..., MLA_NOPE:], cos, sin)], axis=-1)
    return q, k, v

def attend_blocks(q, k, v):
    b, t, h, dq = q.shape
    qb = q.reshape(b, t // Q_BLOCK, Q_BLOCK, h, dq).transpose(1, 0, 2, 3, 4)
    scale = dq ** -0.5

    def one(qblk):
        s = jnp.einsum('bqhd,bkhd->bhqk', qblk, k).astype(jnp.float32) * scale
        pr = jax.nn.softmax(s, axis=-1).astype(v.dtype)
        return jnp.einsum('bhqk,bkhd->bqhd', pr, v)

    o = lax.map(one, qb)
    return o.transpose(1, 0, 2, 3, 4).reshape(b, t, h * v.shape[-1])

def retention_scan(q, k, v, log_g, r0):
    b, h, t, _ = q.shape
    n = t // RET_CHUNK

    def chunks(a):
        return a.reshape(b, h, n, RET_CHUNK, a.shape[-1]).transpose(2, 0, 1, 3, 4)

    i = jnp.arange(RET_CHUNK, dtype=jnp.float32)
    diff = i[:, None] - i[None, :]
    dmat = jnp.where(diff >= 0, jnp.exp(log_g[:, None, None] * jnp.maximum(diff, 0.0)), 0.0)
    xi = jnp.exp(log_g[:, None] * (i + 1.0))[..., None]
    zeta = jnp.exp(log_g[:, None] * (RET_CHUNK - 1.0 - i))[..., None]
    g_chunk = jnp.exp(log_g * RET_CHUNK)[:, None, None]

    def step(r, blk):
        qc, kc, vc = blk
        att = jnp.einsum('bhid,bhjd->bhij', qc, kc) * dmat
        o = jnp.einsum('bhij,bhjv->bhiv', att, vc) + jnp.einsum('bhid,bhdv->bhiv', qc, r) * xi
        r = g_chunk * r + jnp.einsum('bhjd,bhjv->bhdv', kc * zeta, vc)
        return r, o

    r, o = lax.scan(step, r0, (chunks(q), chunks(k), chunks(v)))
    return o.transpose(1, 2, 0, 3, 4).reshape(b, h, t, -1), r

def retention_prep(p, rope):
    q, k, v, g = jnp.split(p, [RET_HEADS * RET_DK, 2 * RET_HEADS * RET_DK,
                               2 * RET_HEADS * RET_DK + RET_W], axis=-1)
    b, t, _ = q.shape
    cos, sin = rope
    q = rotate_half_pairs(q.reshape(b, t, RET_HEADS, RET_DK), cos, sin)
    k = rotate_half_pairs(k.reshape(b, t, RET_HEADS, RET_DK), cos, sin) * (RET_DK ** -0.5)
    v = v.reshape(b, t, RET_HEADS, RET_DV)
    heads = lambda a: jnp.transpose(a, (0, 2, 1, 3)).astype(jnp.float32)
    return heads(q), heads(k), heads(v), g

def retention_mixer(p_lat, p_ctx, need_ctx, decay_logits, gn_w, rope_lat, rope_ctx):
    ql, kl, vl, gl = retention_prep(p_lat, rope_lat)
    qc, kc, vc, gc = retention_prep(p_ctx, rope_ctx)
    log_g = jax.nn.log_sigmoid(decay_logits.astype(jnp.float32))
    r0 = jnp.zeros((ql.shape[0], RET_HEADS, RET_DK, RET_DV), jnp.float32)
    flip = lambda a: jnp.flip(a, axis=2)
    oc_f, rc_f = retention_scan(qc, kc, vc, log_g[0], r0)
    ol_f, _ = retention_scan(ql, kl, vl, log_g[0], rc_f)
    oc_b, rc_b = retention_scan(flip(qc), flip(kc), flip(vc), log_g[1], r0)
    ol_b, _ = retention_scan(flip(ql), flip(kl), flip(vl), log_g[1], rc_b)

    def finish(o, g):
        b, h, t, dv = o.shape
        o = jnp.transpose(o, (0, 2, 1, 3)).reshape(b, t, h * dv).astype(g.dtype)
        return head_layer_norm(o, gn_w, RET_HEADS, RET_EPS) * jax.nn.silu(g)

    out_lat = finish(ol_f + flip(ol_b), gl)
    out_ctx = finish(oc_f + flip(oc_b), gc) if need_ctx else None
    return out_lat, out_ctx

def rwkv_features(p, mu, w0, w2, a0, a2, g2, k_k, k_a):
    f32 = jnp.float32
    p = token_shift(p, mu)
    r, k, v, wdf, wdb, ad, gd = jnp.split(p, RWKV_SPLITS, axis=-1)
    b, t, _ = r.shape
    heads = lambda z: z.reshape(b, t, RWKV_HEADS, RWKV_N)
    w0f = w0.astype(f32)
    w2f = w2.astype(f32)
    w_fwd = jnp.exp(-RWKV_DECAY_SCALE * jax.nn.sigmoid(w0f[0] + jnp.tanh(wdf.astype(f32)) @ w2f[0]))
    w_bwd = jnp.exp(-RWKV_DECAY_SCALE * jax.nn.sigmoid(w0f[1] + jnp.tanh(wdb.astype(f32)) @ w2f[1]))
    a = jax.nn.sigmoid(a0.astype(f32) + ad.astype(f32) @ a2.astype(f32))
    g = jax.nn.sigmoid(gd) @ g2
    kf = k.astype(f32)
    kk = heads(kf * k_k.astype(f32))
    kk = kk / jnp.maximum(jnp.sqrt(jnp.sum(kk * kk, axis=-1, keepdims=True)), 1e-12)
    kf = kf * (1.0 + (a - 1.0) * k_a.astype(f32))
    return (heads(r.astype(f32)), heads(w_fwd), heads(w_bwd), heads(kf), heads(v.astype(f32)), kk, heads(a), g)

def rwkv_scan(r, w, k, v, kk, a, s0):
    xs = tuple(jnp.moveaxis(z, 1, 0) for z in (r, w, k, v, kk, a))

    def step(s, inp):
        rt, wt, kt, vt, kkt, at = inp
        skk = jnp.einsum('bhvk,bhk->bhv', s, kkt)
        s = s * wt[:, :, None, :] - skk[..., None] * (kkt * at)[:, :, None, :] + vt[..., None] * kt[:, :, None, :]
        return s, jnp.einsum('bhvk,bhk->bhv', s, rt)

    s, y = lax.scan(step, s0, xs)
    return jnp.moveaxis(y, 0, 1), s

def rwkv_mixer(p_lat, p_ctx, need_ctx, mu, w0, w2, a0, a2, g2, k_k, k_a, r_k, ln_w):
    rl, wfl, wbl, kl, vl, kkl, al, gl = rwkv_features(p_lat, mu, w0, w2, a0, a2, g2, k_k, k_a)
    rc, wfc, wbc, kc, vc, kkc, ac, gc = rwkv_features(p_ctx, mu, w0, w2, a0, a2, g2, k_k, k_a)
    s0 = jnp.zeros((rl.shape[0], RWKV_HEADS, RWKV_N, RWKV_N), jnp.float32)
    flip = lambda z: jnp.flip(z, axis=1)
    yc_f, sc_f = rwkv_scan(rc, wfc, kc, vc, kkc, ac, s0)
    yl_f, _ = rwkv_scan(rl, wfl, kl, vl, kkl, al, sc_f)
    yc_b, sc_b = rwkv_scan(flip(rc), flip(wbc), flip(kc), flip(vc), flip(kkc), flip(ac), s0)
    yl_b, _ = rwkv_scan(flip(rl), flip(wbl), flip(kl), flip(vl), flip(kkl), flip(al), sc_b)

    def finish(y, r, k, v, g):
        b, t = y.shape[:2]
        o = head_layer_norm(y.reshape(b, t, RWKV_W), ln_w, RWKV_HEADS, RWKV_EPS)
        bonus = (jnp.sum(r * k * r_k.astype(jnp.float32), axis=-1, keepdims=True) * v).reshape(b, t, RWKV_W)
        return ((o + bonus) * g.astype(jnp.float32)).astype(g.dtype)

    out_lat = finish(yl_f + flip(yl_b), rl, kl, vl, gl)
    out_ctx = finish(yc_f + flip(yc_b), rc, kc, vc, gc) if need_ctx else None
    return out_lat, out_ctx

def hybrid_mixer(u, uc, rope_axial, rope_ret_lat, rope_ret_ctx, need_ctx, w_in,
                 mla_q_norm_w, mla_w_uq, mla_kv_norm_w, mla_w_ukv, mla_q_gain, mla_k_gain,
                 ret_decay, ret_gn_w, rwkv_mu, rwkv_w0, rwkv_w2, rwkv_a0, rwkv_a2, rwkv_g2,
                 rwkv_k_k, rwkv_k_a, rwkv_r_k, rwkv_ln_w, w_out):
    b, t, _ = u.shape
    p = u @ w_in
    pc = uc @ w_in

    def mla_parts(z):
        return jnp.split(z[..., :MLA_COLS], [MLA_Q_RANK, MLA_Q_RANK + MLA_KV_RANK], axis=-1)

    ql, kl, vl = mla_project(*mla_parts(p), mla_q_norm_w, mla_w_uq, mla_kv_norm_w, mla_w_ukv,
                             mla_q_gain, mla_k_gain, rope_axial)
    qc, kc, vc = mla_project(*mla_parts(pc), mla_q_norm_w, mla_w_uq, mla_kv_norm_w, mla_w_ukv,
                             mla_q_gain, mla_k_gain, None)
    mla_lat = attend_blocks(ql, jnp.concatenate([kc, kl], axis=1), jnp.concatenate([vc, vl], axis=1))

    ret_lat, ret_ctx = retention_mixer(p[..., MLA_COLS:MLA_COLS + RET_COLS], pc[..., MLA_COLS:MLA_COLS + RET_COLS],
                                       need_ctx, ret_decay, ret_gn_w, rope_ret_lat, rope_ret_ctx)
    rwkv_lat, rwkv_ctx = rwkv_mixer(p[..., MLA_COLS + RET_COLS:], pc[..., MLA_COLS + RET_COLS:], need_ctx,
                                    rwkv_mu, rwkv_w0, rwkv_w2, rwkv_a0, rwkv_a2, rwkv_g2,
                                    rwkv_k_k, rwkv_k_a, rwkv_r_k, rwkv_ln_w)
    y = jnp.concatenate([mla_lat, ret_lat.astype(mla_lat.dtype), rwkv_lat.astype(mla_lat.dtype)], axis=-1) @ w_out
    if not need_ctx:
        return y, None
    mla_ctx = attend_blocks(qc, kc, vc)
    yc = jnp.concatenate([mla_ctx, ret_ctx.astype(mla_ctx.dtype), rwkv_ctx.astype(mla_ctx.dtype)], axis=-1) @ w_out
    return y, yc

def expert_choice_ffn(h, router_w, w_gate, w_up, w_down):
    b, n, d = h.shape
    cap = max(1, EC_FACTOR * n // N_EXPERTS)
    aff = jax.nn.softmax((h @ router_w).astype(jnp.float32), axis=-1)
    gate, idx = lax.top_k(jnp.swapaxes(aff, 1, 2), cap)
    xe = jax.vmap(lambda hb, ib: hb[ib])(h, idx)
    hid = jax.nn.silu(jnp.einsum('becd,edf->becf', xe, w_gate)) * jnp.einsum('becd,edf->becf', xe, w_up)
    ye = jnp.einsum('becf,efd->becd', hid, w_down) * gate[..., None].astype(h.dtype)
    scatter = lambda yb, ib: jnp.zeros((n, d), yb.dtype).at[ib.reshape(-1)].add(yb.reshape(-1, d))
    return jax.vmap(scatter)(ye, idx)

def setup_inputs(seed: int = 0) -> dict:
    key = jax.random.key(seed)
    ks = jax.random.split(key, 32)
    f32 = jnp.float32
    nrm = lambda k, shape, s: jax.random.normal(k, shape, f32) * s
    L = DEPTH
    ret_logit = np.log(2.0 ** (5.0 + np.arange(RET_HEADS)) - 1.0).astype(np.float32)
    return {
        'x': nrm(ks[0], (BATCH, SEQ, D_MODEL), 1.0),
        'c': nrm(ks[1], (BATCH, D_MODEL), 1.0),
        'ctx': nrm(ks[2], (BATCH, CTX_LEN, D_MODEL), 1.0),
        'c_ctx': nrm(ks[3], (D_MODEL,), 1.0),
        'mod_w': nrm(ks[4], (L, D_MODEL, 6 * D_MODEL), 0.5 * D_MODEL ** -0.5),
        'mod_b': nrm(ks[5], (L, 6 * D_MODEL), 0.02),
        'norm1_w': 1.0 + nrm(ks[6], (L, D_MODEL), 0.02),
        'norm2_w': 1.0 + nrm(ks[7], (L, D_MODEL), 0.02),
        'w_in': nrm(ks[8], (L, D_MODEL, IN_COLS), D_MODEL ** -0.5),
        'mla_q_norm_w': 1.0 + nrm(ks[9], (L, MLA_Q_RANK), 0.02),
        'mla_w_uq': nrm(ks[10], (L, MLA_Q_RANK, MLA_HEADS * MLA_QK), MLA_Q_RANK ** -0.5),
        'mla_kv_norm_w': 1.0 + nrm(ks[11], (L, MLA_KV_RANK), 0.02),
        'mla_w_ukv': nrm(ks[12], (L, MLA_KV_RANK, MLA_HEADS * (MLA_NOPE + MLA_V)), MLA_KV_RANK ** -0.5),
        'mla_q_gain': 1.0 + nrm(ks[13], (L, MLA_QK), 0.02),
        'mla_k_gain': 1.0 + nrm(ks[14], (L, MLA_QK), 0.02),
        'ret_decay': jnp.asarray(ret_logit)[None, None, :] + nrm(ks[15], (L, 2, RET_HEADS), 0.05),
        'ret_gn_w': 1.0 + nrm(ks[16], (L, RET_W), 0.02),
        'rwkv_mu': jax.random.uniform(ks[17], (L, RWKV_COLS), f32),
        'rwkv_w0': jax.random.uniform(ks[18], (L, 2, RWKV_W), f32, minval=-4.0, maxval=1.0),
        'rwkv_w2': nrm(ks[19], (L, 2, RWKV_DECAY_LORA, RWKV_W), 0.5 * RWKV_DECAY_LORA ** -0.5),
        'rwkv_a0': nrm(ks[20], (L, RWKV_W), 0.5),
        'rwkv_a2': nrm(ks[21], (L, RWKV_A_LORA, RWKV_W), 0.5 * RWKV_A_LORA ** -0.5),
        'rwkv_g2': nrm(ks[22], (L, RWKV_G_LORA, RWKV_W), RWKV_G_LORA ** -0.5),
        'rwkv_k_k': 0.85 + nrm(ks[23], (L, RWKV_W), 0.02),
        'rwkv_k_a': 1.0 + nrm(ks[24], (L, RWKV_W), 0.02),
        'rwkv_r_k': nrm(ks[25], (L, RWKV_HEADS, RWKV_N), 0.1),
        'rwkv_ln_w': 1.0 + nrm(ks[26], (L, RWKV_W), 0.02),
        'w_out': nrm(ks[27], (L, MIX_W, D_MODEL), MIX_W ** -0.5),
        'router_w': nrm(ks[28], (L, D_MODEL, N_EXPERTS), D_MODEL ** -0.5),
        'exp_w_gate': nrm(ks[29], (L, N_EXPERTS, D_MODEL, EXPERT_FF), D_MODEL ** -0.5),
        'exp_w_up': nrm(ks[30], (L, N_EXPERTS, D_MODEL, EXPERT_FF), D_MODEL ** -0.5),
        'exp_w_down': nrm(ks[31], (L, N_EXPERTS, EXPERT_FF, D_MODEL), EXPERT_FF ** -0.5),
    }

def reference(x, c, ctx, c_ctx, mod_w, mod_b, norm1_w, norm2_w, w_in,
              mla_q_norm_w, mla_w_uq, mla_kv_norm_w, mla_w_ukv, mla_q_gain, mla_k_gain,
              ret_decay, ret_gn_w, rwkv_mu, rwkv_w0, rwkv_w2, rwkv_a0, rwkv_a2, rwkv_g2,
              rwkv_k_k, rwkv_k_a, rwkv_r_k, rwkv_ln_w, w_out, router_w,
              exp_w_gate, exp_w_up, exp_w_down):
    n_lat = x.shape[1]
    n_ctx = ctx.shape[1]
    ROWS = n_lat // GRID_W
    rope_axial = axial_rope_tables(ROWS)
    rope_ret_ctx = seq_rope_tables(jnp.arange(n_ctx))
    rope_ret_lat = seq_rope_tables(n_ctx + jnp.arange(n_lat))
    silu_c = jax.nn.silu(c)
    silu_cc = jax.nn.silu(c_ctx)
    xc = ctx
    for l in range(DEPTH):
        need_ctx = l < DEPTH - 1
        mod = (silu_c @ mod_w[l] + mod_b[l])[:, None, :]
        mod_c = (silu_cc @ mod_w[l] + mod_b[l])[None, None, :]
        sh1, sc1, ga1, sh2, sc2, ga2 = jnp.split(mod, 6, axis=-1)
        csh1, csc1, cga1, csh2, csc2, cga2 = jnp.split(mod_c, 6, axis=-1)
        u = rms_norm(x, norm1_w[l]) * (1.0 + sc1) + sh1
        uc = rms_norm(xc, norm1_w[l]) * (1.0 + csc1) + csh1
        y, yc = hybrid_mixer(u, uc, rope_axial, rope_ret_lat, rope_ret_ctx, need_ctx, w_in[l],
                             mla_q_norm_w[l], mla_w_uq[l], mla_kv_norm_w[l], mla_w_ukv[l],
                             mla_q_gain[l], mla_k_gain[l], ret_decay[l], ret_gn_w[l],
                             rwkv_mu[l], rwkv_w0[l], rwkv_w2[l], rwkv_a0[l], rwkv_a2[l], rwkv_g2[l],
                             rwkv_k_k[l], rwkv_k_a[l], rwkv_r_k[l], rwkv_ln_w[l], w_out[l])
        x = x + ga1 * y
        h = rms_norm(x, norm2_w[l]) * (1.0 + sc2) + sh2
        x = x + ga2 * expert_choice_ffn(h, router_w[l], exp_w_gate[l], exp_w_up[l], exp_w_down[l])
        if need_ctx:
            xc = xc + cga1 * yc
            hc = rms_norm(xc, norm2_w[l]) * (1.0 + csc2) + csh2
            xc = xc + cga2 * expert_choice_ffn(hc, router_w[l], exp_w_gate[l], exp_w_up[l], exp_w_down[l])
    return x


_drawn_inputs = setup_inputs


def setup_inputs(seed=0):
    import zlib

    import numpy as np

    out = dict(_drawn_inputs(seed))
    spreads = {}
    factors = {'norm1_w': 6.72,
     'norm2_w': 19.018,
     'mla_q_norm_w': 8.0,
     'mla_kv_norm_w': 29.426,
     'mla_q_gain': 23.675,
     'mla_k_gain': 24.539,
     'ret_gn_w': 45.241,
     'rwkv_w2': 6.089,
     'rwkv_k_k': 200.0,
     'rwkv_k_a': 8.0,
     'rwkv_ln_w': 200.0}
    for name, (base, spread) in spreads.items():
        noise = np.random.default_rng([zlib.crc32(name.encode()), seed]).standard_normal(out[name].shape)
        drawn = base * np.exp(spread * noise) if base else spread * noise
        out[name] = jnp.asarray(drawn.astype(out[name].dtype))
    for name, factor in factors.items():
        out[name] = (out[name] * factor).astype(out[name].dtype)
    return out
```

```python
from contextlib import ExitStack

import numpy as np

import concourse.bass as bass
from concourse import mybir

P = 128
D = 1024
KD = D // P
LAT, CTX = 512, 256
TOK = LAT + CTX
CT, NT = CTX // P, TOK // P
DEPTH = 2
EPS = 1e-6

HEADS, NOPE, ROPE, QK, VD = 8, 64, 32, 96, 64
QR, KVR = 384, 256
MLA_COLS = QR + KVR + ROPE
RET_COLS = 1024
RWKV_COLS = 1088
IN_COLS = MLA_COLS + RET_COLS + RWKV_COLS
C = 64
NCH = TOK // C
CCH = CTX // C
DECAY = -0.606531
E_N, CAP_L, CAP_C = 16, 64, 32
LEVELS = (2, 4, 8, 16, 32)

F32 = mybir.dt.float32
ALU = mybir.AluOpType
ACT = mybir.ActivationFunctionType
AX = mybir.AxisListType.X


def packed(widths):
    at, out = 0, {}
    for name, n in widths:
        out[name] = (at, at + n)
        at += n
    return out, at


BASE, BASE_N = packed([
    ("ident", 128), ("ones", 128), ("pair_ones", 128), ("ident64", 64), ("iota", 64),
    ("axial_cos", 4 * 16), ("axial_sin", 4 * 16)])
RETC, RETC_N = packed([
    ("seq_cos", 6 * 32), ("seq_sin", 6 * 32),
    ("dist", 896), ("after", 896), ("before", 896), ("dist_f", 640), ("dist_b", 640)])
RWKVC, RWKVC_N = packed([
    ("mask", 4 * 2 * 64), ("first", 4 * 64), ("first_t", 4 * 64), ("level", len(LEVELS) * 4 * 64),
    ("restart", TOK)])
COLS, COLS_N = packed([
    ("mod_b", 48), ("norm1", 8), ("norm2", 8), ("cn", 5), ("mu", 9), ("w0", 4), ("a0", 2),
    ("k_k", 2), ("k_a", 2), ("r_k", 2)])
ROWS, ROWS_N = packed([("qk_gain", 2 * 96), ("decay", 8), ("gn_w", 256), ("ln_w", 128)])


def constants():
    p = np.arange(P)[:, None]
    packs = [(names, np.zeros((P, n), np.float32)) for names, n in
             ((BASE, BASE_N), (RETC, RETC_N), (RWKVC, RWKVC_N))]

    def put(name, a):
        for names, out in packs:
            if name in names:
                lo, hi = names[name]
                out[:, lo:hi] = np.broadcast_to(np.asarray(a, np.float32).reshape(a.shape[0], -1), (P, hi - lo))

    put("ident", np.eye(P))
    put("ones", np.ones((P, P)))
    put("pair_ones", (p // 64 == np.arange(P) // 64))
    put("ident64", (p % 64 == np.arange(64)))
    put("iota", np.arange(64)[None])
    row = np.repeat(np.arange(LAT // 64, dtype=np.float32), 64)
    col = np.tile(np.arange(64, dtype=np.float32), LAT // 64)
    inv = (np.float32(10000.0) ** (-np.arange(8, dtype=np.float32) / 8)).astype(np.float32)
    ang = np.concatenate([row[:, None] * inv, col[:, None] * inv], -1)
    by_tile = lambda a: a.reshape(-1, P, a.shape[-1]).transpose(1, 0, 2)
    put("axial_cos", by_tile(np.cos(ang)))
    put("axial_sin", by_tile(np.sin(ang)))
    inv = (np.float32(10000.0) ** (-np.linspace(0.0, 1.0, 32, dtype=np.float32))).astype(np.float32)
    ang = np.arange(TOK, dtype=np.float32)[:, None] * inv
    put("seq_cos", by_tile(np.cos(ang)))
    put("seq_sin", by_tile(np.sin(ang)))
    d = np.arange(896)[None] - 384 - p
    put("dist", np.abs(d))
    put("after", d >= 0)
    put("before", d <= 0)
    d = np.arange(640)[None] - 128 - p
    put("dist_f", CTX + d)
    put("dist_b", LAT - d)
    s, t = (p % 64)[:, :, None], np.arange(64)[None, None]
    sign = np.array([1, 1, -1, -1])[None, :, None]
    gap = (t - s) * sign
    put("mask", np.stack([gap > 0, gap >= 0], 2))
    pairs = (s // 2 == t // 2) & (gap > 0)
    put("first_t", pairs)
    put("first", (s // 2 == t // 2) & (gap < 0))
    put("level", np.stack([(s // (2 * m) == t // (2 * m)) & (s // m != t // m) & (gap > 0)
                           for m in LEVELS], 1))
    put("restart", (np.arange(TOK) % C != 0)[None])
    return [out for _, out in packs]


def build(nc, io):
    with ExitStack() as kernel_scope:
        Program(nc, io, kernel_scope).run()


class Count:

    def __init__(self, sem, step=1):
        self.sem, self.step, self.base = sem, step, 0

    def __add__(self, k):
        return self.base + self.step * k

    def advance(self, k):
        self.base += self.step * k


class Chain:

    def __init__(self, sem):
        self.sem, self.n = sem, 0

    def on(self, eng):
        def link(ins):
            self.n += 1
            ins.then_inc(self.sem, 1)
            eng.wait_ge(self.sem, self.n)
        return link


def spread(ap, axis, n):
    a = ap.unsqueeze(axis)
    shape = list(a.shape)
    shape[axis] = n
    return a.broadcast_to(shape)


class Program:
    def __init__(self, nc, io, scope):
        self.nc, self.io, self.scope = nc, io, scope
        self.counts, self.n_tensors = {}, 0
        self.dve_chain = Chain(scope.enter_context(nc.semaphore("dve_chain")))
        self.act_chain = Chain(scope.enter_context(nc.semaphore("act_chain")))
        sb = lambda name, shape: self.sbuf(scope, name, shape)
        self.base = sb("base", [P, BASE_N])
        self.cols = sb("cols", [P, COLS_N])
        self.rows = sb("rows", [P, ROWS_N])
        self.x = sb("x_tokens", [P, NT, D])
        self.cvec = sb("cvec", [P, KD, 2])
        self.silu_c = sb("silu_c", [P, KD, 2])
        self.mod = sb("mod", [P, 48, 2])
        self.scale1 = sb("scale1", [P, KD, 2])
        self.scale2 = sb("scale2", [P, KD, 2])
        self.gates = sb("gates", [P, 2, 2, D])
        self.stat = sb("stat", [P, 64])
        self.psum = scope.enter_context(nc.psum_tensor("psum", [P, 8, 512], F32))
        self.flat = self.psum[:, :, :].rearrange("p b n -> p (b n)")

    def sbuf(self, scope, name, shape):
        self.n_tensors += 1
        return scope.enter_context(self.nc.sbuf_tensor(f"{name}_{self.n_tensors}", shape, F32))

    def count(self, name, step=1):
        if name not in self.counts:
            self.counts[name] = Count(self.scope.enter_context(self.nc.semaphore(name)), step)
        return self.counts[name]

    def c(self, name):
        lo, hi = BASE[name]
        return self.base[:, lo:hi]

    def col(self, name):
        lo, hi = COLS[name]
        return self.cols[:, lo:hi]

    def row(self, name):
        lo, hi = ROWS[name]
        return self.rows[:, lo:hi]

    def run(self):
        self.load_inputs()
        for layer in range(DEPTH):
            last = layer == DEPTH - 1
            self.modulation(layer)
            tiles = list(range(CT if last else 0, NT))
            with ExitStack() as mixer_scope:
                self.mix_t = self.sbuf(mixer_scope, "mix_t", [P, KD, TOK])
                with ExitStack() as scope:
                    self.u_t = self.sbuf(scope, "u_t", [P, KD, TOK])
                    with ExitStack() as inner:
                        self.xn = self.sbuf(inner, "xn", [P, NT, D])
                        self.normalise(layer, "norm1", self.scale1, 0, list(range(NT)))
                    self.attention(layer, last)
                    self.retention(layer, last)
                    self.rwkv(layer, last)
                self.project_out(layer, last, tiles)
            with ExitStack() as scope:
                self.xn = self.sbuf(scope, "xn", [P, NT, D])
                self.slot = self.sbuf(scope, "slot", [P, NT, E_N + 1])
                self.aff = self.sbuf(scope, "aff", [P, NT, E_N])
                with ExitStack() as inner:
                    self.u_t = self.sbuf(inner, "h_t", [P, KD, TOK])
                    self.normalise(layer, "norm2", self.scale2, 24, tiles)
                    self.route(layer, last, tiles)
                self.y_lat = self.sbuf(scope, "y_lat", [P, E_N // 2, D])
                self.y_ctx = None if last else self.sbuf(scope, "y_ctx", [P, E_N // 4, D])
                self.experts(layer, last)
                self.combine(layer, last, tiles)
        self.store()

    def load_inputs(self):
        nc, io = self.nc, self.io
        landed, sig, done = self.count("inputs_landed", 16), self.count("silu_sigmoid"), self.count("silu_done")
        with nc.Block() as block:
            @block.sync
            def _(sp):
                sp.dma_start(self.cvec[:, :, :], io["cvec"]).then_inc(landed.sem, 16)
                sp.dma_start(self.base[:, :], io["base"]).then_inc(landed.sem, 16)
                sp.dma_start(self.x[:, 0:CT, :], io["ctx"].rearrange("(t p) d -> p t d", p=P)).then_inc(landed.sem, 16)
                sp.dma_start(self.x[:, CT:NT, :], io["x"].rearrange("(t p) d -> p t d", p=P)).then_inc(landed.sem, 16)
                sp.wait_ge(landed.sem, landed + 4)

            @block.scalar
            def _(act):
                act.wait_ge(landed.sem, landed + 4)
                act.activation(self.silu_c[:, :, :], self.cvec[:, :, :], ACT.Sigmoid).then_inc(sig.sem, 1)

            @block.vector
            def _(dve):
                dve.wait_ge(sig.sem, sig + 1)
                dve.tensor_tensor(self.silu_c[:, :, :], self.silu_c[:, :, :], self.cvec[:, :, :],
                                  ALU.mult).then_inc(done.sem, 1)

    def modulation(self, l):
        nc, io = self.nc, self.io
        small = self.count("layer_vectors_landed", 16)
        landed = [self.count(f"mod_w_landed{i}", 16) for i in range(3)]
        used, summed = self.count("mod_w_used"), self.count("mod_summed")
        diag_ready, spread_done, gate_copied = (self.count(n) for n in ("gate_diag", "gate_spread", "gate_copied"))
        loads = [sum(k % 3 == i for k in range(KD)) for i in range(3)]
        with ExitStack() as scope:
            w = self.sbuf(scope, "mod_w", [P, 3, 6 * D])
            diag = self.sbuf(scope, "gate_diagonals", [P, 2, 4, P])
            block = scope.enter_context(nc.Block())

            @block.sync
            def _(sp):
                sp.dma_start(self.cols[:, :], io["cols"][l]).then_inc(small.sem, 16)
                sp.dma_start(self.rows[:, :], io["rows"][l]).then_inc(small.sem, 16)
                for k in range(KD):
                    if k >= 3:
                        sp.wait_ge(used.sem, used + (k - 2))
                    sp.dma_start(w[:, k % 3, :], io["mod_w"][l, k * P:(k + 1) * P, :]).then_inc(landed[k % 3].sem, 16)
                sp.wait_ge(small.sem, small + 2)

            @block.tensor
            def _(pe):
                for k in range(KD):
                    pe.wait_ge(landed[k % 3].sem, landed[k % 3] + (k // 3 + 1))
                    for j in range(48):
                        mm = pe.matmul(self.flat[:, 2 * j:2 * j + 2], w[:, k % 3, j * P:(j + 1) * P],
                                       self.silu_c[:, k, :], start=(k == 0 and j == 0), stop=(k == KD - 1),
                                       skip_group_check=True)
                    if k == KD - 1:
                        mm.then_inc(summed.sem, 1)
                    else:
                        mm.then_inc(used.sem, 1)
                for n in range(8):
                    pe.wait_ge(diag_ready.sem, diag_ready + (n + 1))
                    if n >= 2:
                        pe.wait_ge(gate_copied.sem, gate_copied + (n - 1))
                    pe.matmul(self.psum[:, 1 + n % 2, :], self.c("ones"),
                              diag[:, n % 2, :, :].rearrange("p a b -> p (a b)"), start=True, stop=True
                              ).then_inc(spread_done.sem, 1)

            @block.scalar
            def _(act):
                for n in range(8):
                    g, s, half = n // 4, n // 2 % 2, n % 2
                    act.wait_ge(spread_done.sem, spread_done + (n + 1))
                    act.copy(self.gates[:, g, s, half * 512:(half + 1) * 512],
                             self.psum[:, 1 + n % 2, :]).then_inc(gate_copied.sem, 1)

            @block.vector
            def _(dve):
                link = self.dve_chain.on(dve)
                dve.wait_ge(small.sem, small + 2)
                dve.wait_ge(summed.sem, summed + 1)
                link(dve.tensor_tensor(self.mod[:, :, :], self.flat[:, 0:96].rearrange("p (j s) -> p j s", s=2),
                                       spread(self.col("mod_b"), 2, 2), ALU.add))
                for n in range(8):
                    g, s, half = n // 4, n // 2 % 2, n % 2
                    j = (16, 40)[g] + 4 * half
                    if n >= 2:
                        dve.wait_ge(spread_done.sem, spread_done + (n - 1))
                    dve.tensor_tensor(diag[:, n % 2, :, :], spread(self.c("ident"), 1, 4),
                                      spread(self.mod[:, j:j + 4, s], 2, P), ALU.mult).then_inc(diag_ready.sem, 1)
                for scale, j, name in ((self.scale1, 8, "norm1"), (self.scale2, 32, "norm2")):
                    link(dve.tensor_scalar(scale[:, :, :], self.mod[:, j:j + 8, :], 1.0, None, ALU.add))
                    link(dve.tensor_tensor(scale[:, :, :], scale[:, :, :], spread(self.col(name), 2, 2), ALU.mult))
        small.advance(2)
        used.advance(KD - 1)
        summed.advance(1)
        for i in range(3):
            landed[i].advance(loads[i])
        for s in (diag_ready, spread_done, gate_copied):
            s.advance(8)

    def normalise(self, l, name, scale, shift, tiles):
        nc = self.nc
        squares, mean, root, normed = (self.count(f"norm_{n}") for n in ("squares", "mean", "root", "rows"))
        turned, modulated = self.count("norm_turned"), self.count("norm_modulated")
        n = len(tiles)
        ss, rs = self.stat[:, 0:NT], self.stat[:, 8:8 + NT]
        groups = [(1, [t for t in tiles if t < CT]), (0, [t for t in tiles if t >= CT])]
        items = [(k, s, ts) for k in range(KD) for s, ts in groups if ts]
        with ExitStack() as scope:
            junk = self.sbuf(scope, "squares", [P, D])
            block = scope.enter_context(nc.Block())

            @block.scalar
            def _(act):
                for t in tiles:
                    self.act_chain.on(act)(act.activation(junk[:, :], self.x[:, t, :], ACT.Square,
                                                          accum_out=ss[:, t:t + 1]))
                act.copy(junk[:, 0:1], junk[:, 1:2]).then_inc(squares.sem, 1)
                act.wait_ge(mean.sem, mean + 1)
                act.activation(rs[:, tiles[0]:NT], ss[:, tiles[0]:NT], ACT.Sqrt).then_inc(root.sem, 1)
                for i, (k, s, ts) in enumerate(items):
                    if i % 2:
                        act.wait_ge(turned.sem, turned + (i + 1))
                        act.activation(self.u_t[:, k, ts[0] * P:(ts[-1] + 1) * P], self.psum[:, i % 4, 0:len(ts) * P],
                                       ACT.Identity, bias=self.mod[:, shift + k, s:s + 1],
                                       scale=scale[:, k, s:s + 1]).then_inc(modulated.sem, 1)
                    else:
                        act.wait_ge(modulated.sem, modulated + (i + 1))

            @block.vector
            def _(dve):
                link = self.dve_chain.on(dve)
                dve.wait_ge(squares.sem, squares + 1)
                dve.tensor_scalar(ss[:, tiles[0]:NT], ss[:, tiles[0]:NT], 1.0 / D, EPS, ALU.mult, ALU.add
                                  ).then_inc(mean.sem, 1)
                dve.wait_ge(root.sem, root + 1)
                link(dve.reciprocal(rs[:, tiles[0]:NT], rs[:, tiles[0]:NT]))
                for t in tiles:
                    dve.tensor_scalar(self.xn[:, t, :], self.x[:, t, :], rs[:, t:t + 1], None,
                                      ALU.mult).then_inc(normed.sem, 1)
                for i, (k, s, ts) in enumerate(items):
                    if i % 2 == 0:
                        dve.wait_ge(turned.sem, turned + (i + 1))
                        if i:
                            dve.wait_ge(modulated.sem, modulated + i)
                        dve.tensor_scalar(self.u_t[:, k, ts[0] * P:(ts[-1] + 1) * P], self.psum[:, i % 4, 0:len(ts) * P],
                                          scale[:, k, s:s + 1], self.mod[:, shift + k, s:s + 1],
                                          ALU.mult, ALU.add).then_inc(modulated.sem, 1)

            @block.tensor
            def _(pe):
                pe.wait_ge(normed.sem, normed + n)
                for i, (k, s, ts) in enumerate(items):
                    if i >= 4:
                        pe.wait_ge(modulated.sem, modulated + (i - 3))
                    for a, t in enumerate(ts):
                        mm = pe.transpose(self.psum[:, i % 4, a * P:(a + 1) * P], self.xn[:, t, k * P:(k + 1) * P],
                                          self.c("ident"))
                    mm.then_inc(turned.sem, 1)
        squares.advance(1)
        mean.advance(1)
        root.advance(1)
        normed.advance(n)
        turned.advance(len(items))
        modulated.advance(len(items))

    def attention(self, l, last):
        nc, io = self.nc, self.io
        landed = self.count("mla_weights_landed", 16)
        names = ("projected", "squares", "mean", "root", "latents", "latents_turned", "latents_t", "heads_made",
                 "heads_copied", "head_mean", "head_root", "heads_normed", "heads_turned", "heads_t")
        s = {n: self.count("mla_" + n) for n in names}
        with ExitStack() as att_scope:
            sb = lambda name, shape: self.sbuf(att_scope, name, shape)
            q_t, k_t = sb("q_t", [QK, HEADS, TOK]), sb("k_t", [QK, HEADS, TOK])
            v = sb("v", [P, NT, HEADS, VD])
            with ExitStack() as scope:
                sb = lambda name, shape: self.sbuf(scope, name, shape)
                w = sb("w_mla", [P, KD, MLA_COLS])
                spare = self.mix_t[:, :, :].rearrange("p k n -> p (k n)")
                wq = spare[:, 0:3 * 768].rearrange("p (k n) -> p k n", k=3)
                wkv = spare[:, 2304:2304 + 2048].rearrange("p (k n) -> p k n", k=2)
                junk, lat = sb("mla_junk", [P, QR]), sb("latents", [P, MLA_COLS])
                lat_t = sb("latents_t", [P, 5, P])
                qk = sb("qk_rows", [P, 2, HEADS, QK])
                sq = sb("qk_squares", [P, 2, HEADS, QK])
                turn = sb("rope_parts", [P, 4, 2 * HEADS, 16])
                st = self.stat
                block = scope.enter_context(nc.Block())
                pa, pt = self.flat[:, 0:MLA_COLS], self.flat[:, 1024:1024 + 640]
                pq, pkv = self.flat[:, 2048:2048 + 768], self.flat[:, 3072:4096].rearrange("p (h d) -> p h d", h=HEADS)
                ph = self.psum[0:QK, 4:8, :].rearrange("p b (a n) -> p (b a) n", n=P)

                @block.sync
                def _(sp):
                    sp.dma_start(w[:, :, :], io["w_in"][l, :, 0:MLA_COLS].rearrange("(k p) n -> p k n", p=P)).then_inc(landed.sem, 16)
                    sp.dma_start(wq, io["mla_w_uq"][l].rearrange("(k p) n -> p k n", p=P)).then_inc(landed.sem, 16)
                    sp.dma_start(wkv, io["mla_w_ukv"][l].rearrange("(k p) n -> p k n", p=P)).then_inc(landed.sem, 16)

                @block.tensor
                def _(pe):
                    def project(t):
                        if t >= 1:
                            pe.wait_ge(s["latents"].sem, s["latents"] + t)
                        for lo, hi in ((0, 512), (512, MLA_COLS)):
                            for k in range(KD):
                                mm = pe.matmul(pa[:, lo:hi], self.u_t[:, k, t * P:(t + 1) * P], w[:, k, lo:hi],
                                               start=(k == 0), stop=(k == KD - 1))
                        mm.then_inc(s["projected"].sem, 1)

                    pe.wait_ge(landed.sem, landed + 3)
                    project(0)
                    for t in range(NT):
                        pe.wait_ge(s["latents"].sem, s["latents"] + (t + 1))
                        for a in range(5):
                            mm = pe.transpose(pt[:, a * P:(a + 1) * P], lat[:, a * P:(a + 1) * P], self.c("ident"))
                        mm.then_inc(s["latents_turned"].sem, 1)
                        if t + 1 < NT:
                            project(t + 1)
                        pe.wait_ge(s["latents_t"].sem, s["latents_t"] + (t + 1))
                        if t >= 1:
                            pe.wait_ge(s["heads_t"].sem, s["heads_t"] + 2 * t)
                        for lo, hi in ((0, 512), (512, 768)):
                            for k in range(3):
                                pe.matmul(pq[:, lo:hi], lat_t[:, k, :], wq[:, k, lo:hi], start=(k == 0), stop=(k == 2))
                        for b in range(2):
                            for k in range(2):
                                mm = pe.matmul(self.psum[:, 6 + b, :], lat_t[:, 3 + k, :], wkv[:, k, b * 512:(b + 1) * 512],
                                               start=(k == 0), stop=(k == 1))
                        mm.then_inc(s["heads_made"].sem, 1)
                        pe.wait_ge(s["heads_normed"].sem, s["heads_normed"] + (t + 1))
                        for a in range(2):
                            for h in range(HEADS):
                                mm = pe.transpose(ph[:, a * HEADS + h, :], qk[:, a, h, :], self.c("ident"))
                            mm.then_inc(s["heads_turned"].sem, 1)

                @block.scalar
                def _(act):
                    link = self.act_chain.on(act)
                    for t in range(NT):
                        act.wait_ge(s["projected"].sem, s["projected"] + (t + 1))
                        link(act.activation(junk[:, 0:QR], pa[:, 0:QR], ACT.Square, accum_out=st[:, 0:1]))
                        link(act.activation(junk[:, 0:KVR], pa[:, QR:QR + KVR], ACT.Square, accum_out=st[:, 1:2]))
                        act.copy(junk[:, 0:1], junk[:, 1:2]).then_inc(s["squares"].sem, 1)
                        act.wait_ge(s["mean"].sem, s["mean"] + (t + 1))
                        act.activation(st[:, 4:6], st[:, 2:4], ACT.Sqrt).then_inc(s["root"].sem, 1)
                        act.wait_ge(s["heads_made"].sem, s["heads_made"] + (t + 1))
                        if t >= 1:
                            act.wait_ge(s["heads_turned"].sem, s["heads_turned"] + 2 * t)
                        act.copy(qk[:, 0, :, :].rearrange("p h d -> p (h d)"), pq)
                        act.copy(qk[:, 1, :, 0:NOPE], pkv[:, :, 0:NOPE])
                        act.copy(v[:, t, :, :], pkv[:, :, NOPE:NOPE + VD]).then_inc(s["heads_copied"].sem, 1)
                        act.wait_ge(s["head_mean"].sem, s["head_mean"] + (t + 1))
                        act.activation(st[:, 32:48], st[:, 16:32], ACT.Sqrt).then_inc(s["head_root"].sem, 1)
                        act.wait_ge(s["heads_turned"].sem, s["heads_turned"] + (2 * t + 1))
                        act.copy(q_t[:, :, t * P:(t + 1) * P], ph[:, 0:HEADS, :]).then_inc(s["heads_t"].sem, 1)

                @block.vector
                def _(dve):
                    link = self.dve_chain.on(dve)
                    for t in range(NT):
                        dve.wait_ge(s["squares"].sem, s["squares"] + (t + 1))
                        link(dve.tensor_scalar(st[:, 2:3], st[:, 0:1], 1.0 / QR, EPS, ALU.mult, ALU.add))
                        dve.tensor_scalar(st[:, 3:4], st[:, 1:2], 1.0 / KVR, EPS, ALU.mult, ALU.add).then_inc(s["mean"].sem, 1)
                        dve.wait_ge(s["root"].sem, s["root"] + (t + 1))
                        link(dve.reciprocal(st[:, 6:8], st[:, 4:6]))
                        link(dve.tensor_scalar(lat[:, 0:QR], pa[:, 0:QR], st[:, 6:7], None, ALU.mult))
                        link(dve.tensor_scalar(lat[:, QR:640], pa[:, QR:640], st[:, 7:8], None, ALU.mult))
                        dve.tensor_copy(lat[:, 640:MLA_COLS], pa[:, 640:MLA_COLS]).then_inc(s["latents"].sem, 1)
                        dve.wait_ge(s["latents_turned"].sem, s["latents_turned"] + (t + 1))
                        dve.tensor_tensor(lat_t[:, :, :], pt.rearrange("p (a n) -> p a n", n=P),
                                          spread(self.col("cn"), 2, P), ALU.mult).then_inc(s["latents_t"].sem, 1)
                        if t >= 1:
                            dve.wait_ge(s["heads_turned"].sem, s["heads_turned"] + 2 * t)
                        dve.wait_ge(s["latents"].sem, s["latents"] + (t + 1))
                        link(dve.tensor_copy(qk[:, 1, :, NOPE:QK], spread(lat[:, 640:MLA_COLS], 1, HEADS)))
                        dve.wait_ge(s["heads_copied"].sem, s["heads_copied"] + (t + 1))
                        rows = qk[:, :, :, :].rearrange("p a h d -> p (a h) d")
                        link(dve.tensor_tensor(sq[:, :, :, :], qk[:, :, :, :], qk[:, :, :, :], ALU.mult))
                        link(dve.tensor_reduce(st[:, 16:32], sq[:, :, :, :].rearrange("p a h d -> p (a h) d"), AX, ALU.add))
                        dve.tensor_scalar(st[:, 16:32], st[:, 16:32], 1.0 / QK, EPS, ALU.mult, ALU.add).then_inc(s["head_mean"].sem, 1)
                        dve.wait_ge(s["head_root"].sem, s["head_root"] + (t + 1))
                        link(dve.reciprocal(st[:, 48:64], st[:, 32:48]))
                        link(dve.tensor_tensor(rows, rows, spread(st[:, 48:64], 2, QK), ALU.mult))
                        gain = spread(self.row("qk_gain").rearrange("p (a d) -> p a d", a=2), 2, HEADS)
                        link(dve.tensor_tensor(qk[:, :, :, :], qk[:, :, :, :], gain, ALU.mult))
                        if t >= CT:
                            at = (t - CT) * 16
                            cos = spread(self.c("axial_cos")[:, at:at + 16], 1, 2 * HEADS)
                            sin = spread(self.c("axial_sin")[:, at:at + 16], 1, 2 * HEADS)
                            x1, x2 = rows[:, :, NOPE:NOPE + 16], rows[:, :, NOPE + 16:QK]
                            link(dve.tensor_tensor(turn[:, 0], x1, cos, ALU.mult))
                            link(dve.tensor_tensor(turn[:, 1], x2, sin, ALU.mult))
                            link(dve.tensor_tensor(turn[:, 2], x1, sin, ALU.mult))
                            link(dve.tensor_tensor(turn[:, 3], x2, cos, ALU.mult))
                            link(dve.tensor_tensor(x1, turn[:, 0], turn[:, 1], ALU.subtract))
                            dve.tensor_tensor(x2, turn[:, 2], turn[:, 3], ALU.add).then_inc(s["heads_normed"].sem, 1)
                        else:
                            dve.tensor_copy(turn[:, 0, 0, 0:1], rows[:, 0, 0:1]).then_inc(s["heads_normed"].sem, 1)
                        dve.wait_ge(s["heads_turned"].sem, s["heads_turned"] + (2 * t + 2))
                        dve.tensor_copy(k_t[:, :, t * P:(t + 1) * P], ph[:, HEADS:2 * HEADS, :]).then_inc(s["heads_t"].sem, 1)
            landed.advance(3)
            for n in names:
                s[n].advance(2 * NT if n in ("heads_turned", "heads_t") else NT)
            self.attend(l, last, q_t, k_t, v)

    def attend(self, l, last, q_t, k_t, v):
        nc = self.nc
        names = ("scores", "max", "exp", "turned", "probs_t", "values", "outs", "out_turned", "out_t")
        s = {n: self.count("att_" + n) for n in names}
        tiles = list(range(CT if last else 0, NT))
        items = [(h, t) for h in range(HEADS) for t in tiles]
        n_items = len(items)
        keys = [CT if t < CT else NT for _, t in items]
        with ExitStack() as scope:
            sb = lambda name, shape: self.sbuf(scope, name, shape)
            probs, probs_t = sb("probs", [P, 2, TOK]), sb("probs_t", [P, 2, NT, P])
            outs = sb("attended", [P, NT, HEADS * VD])
            stat = sb("softmax_stat", [P, 4, 4])
            block = scope.enter_context(nc.Block())
            scale = float(QK) ** -0.5
            score = lambda i: self.flat[:, 1024 * (i % 2):1024 * (i % 2) + TOK]
            turned = self.flat[:, 2048:2048 + TOK].rearrange("p (a n) -> p a n", n=P)

            @block.tensor
            def _(pe):
                def scores(i):
                    h, t = items[i]
                    if i >= 2:
                        pe.wait_ge(s["exp"].sem, s["exp"] + (i - 1))
                    for lo in range(0, keys[i] * P, 512):
                        hi = min(lo + 512, keys[i] * P)
                        mm = pe.matmul(score(i)[:, lo:hi], q_t[:, h, t * P:(t + 1) * P], k_t[:, h, lo:hi],
                                       start=True, stop=True)
                    mm.then_inc(s["scores"].sem, 1)

                def turn(i):
                    pe.wait_ge(s["exp"].sem, s["exp"] + (i + 1))
                    if i >= 1:
                        pe.wait_ge(s["probs_t"].sem, s["probs_t"] + i)
                    for k in range(keys[i]):
                        mm = pe.transpose(turned[:, k, :], probs[:, i % 2, k * P:(k + 1) * P], self.c("ident"))
                    mm.then_inc(s["turned"].sem, 1)

                def values(i):
                    h, t = items[i]
                    pe.wait_ge(s["probs_t"].sem, s["probs_t"] + (i + 1))
                    if i >= 2:
                        pe.wait_ge(s["outs"].sem, s["outs"] + (i - 1))
                    for k in range(keys[i]):
                        mm = pe.matmul(self.psum[:, 6 + i % 2, 0:VD], probs_t[:, i % 2, k, :], v[:, k, h, :],
                                       start=(k == 0), stop=(k == keys[i] - 1))
                    mm.then_inc(s["values"].sem, 1)

                for i in range(n_items + 2):
                    if i < n_items:
                        scores(i)
                    if 1 <= i <= n_items:
                        turn(i - 1)
                    if i >= 2:
                        values(i - 2)
                pe.wait_ge(s["outs"].sem, s["outs"] + n_items)
                for n, t in enumerate(tiles):
                    if n >= 2:
                        pe.wait_ge(s["out_t"].sem, s["out_t"] + (n - 1))
                    for a in range(4):
                        mm = pe.transpose(self.psum[:, n % 2, a * P:(a + 1) * P], outs[:, t, a * P:(a + 1) * P], self.c("ident"))
                    mm.then_inc(s["out_turned"].sem, 1)

            @block.scalar
            def _(act):
                for i in range(n_items):
                    act.wait_ge(s["max"].sem, s["max"] + (i + 1))
                    if i >= 2:
                        act.wait_ge(s["turned"].sem, s["turned"] + (i - 1))
                    n = keys[i] * P
                    act.activation(probs[:, i % 2, 0:n], score(i)[:, 0:n], ACT.Exp, bias=stat[:, i % 4, 1:2],
                                   scale=scale, accum_out=stat[:, i % 4, 2:3]).then_inc(s["exp"].sem, 1)
                for n, t in enumerate(tiles):
                    act.wait_ge(s["out_turned"].sem, s["out_turned"] + (n + 1))
                    act.copy(self.mix_t[:, 0:4, t * P:(t + 1) * P],
                             self.psum[:, n % 2, :].rearrange("p (a n) -> p a n", n=P)).then_inc(s["out_t"].sem, 1)

            @block.vector
            def _(dve):
                link = self.dve_chain.on(dve)
                for i in range(n_items + 2):
                    if i < n_items:
                        dve.wait_ge(s["scores"].sem, s["scores"] + (i + 1))
                        link(dve.tensor_reduce(stat[:, i % 4, 0:1], score(i)[:, 0:keys[i] * P], AX, ALU.max))
                        dve.tensor_scalar(stat[:, i % 4, 1:2], stat[:, i % 4, 0:1], -scale, None, ALU.mult).then_inc(s["max"].sem, 1)
                    if 1 <= i <= n_items:
                        j = i - 1
                        dve.wait_ge(s["turned"].sem, s["turned"] + (j + 1))
                        if j >= 2:
                            dve.wait_ge(s["values"].sem, s["values"] + (j - 1))
                        dve.tensor_copy(probs_t[:, j % 2, 0:keys[j], :], turned[:, 0:keys[j], :]).then_inc(s["probs_t"].sem, 1)
                    if i >= 2:
                        j = i - 2
                        h, t = items[j]
                        dve.wait_ge(s["values"].sem, s["values"] + (j + 1))
                        link(dve.reciprocal(stat[:, j % 4, 3:4], stat[:, j % 4, 2:3]))
                        dve.tensor_scalar(outs[:, t, h * VD:(h + 1) * VD], self.psum[:, 6 + j % 2, 0:VD],
                                          stat[:, j % 4, 3:4], None, ALU.mult).then_inc(s["outs"].sem, 1)
        for n in names:
            s[n].advance(len(tiles) if n.startswith("out_") else n_items)

    def retention(self, l, last):
        nc, io = self.nc, self.io
        landed = self.count("ret_weights_landed", 16)
        tiles = list(range(CT if last else 0, NT))
        names = ("projected", "rotated", "v_copied", "gate", "gated", "turned", "turned_t", "rows_read",
                 "decay_exp", "decay_ln", "log_decay", "powers", "strips",
                 "scores", "weighted", "head_done", "var", "root", "normed", "out_turned", "out_t")
        s = {n: self.count("ret_" + n) for n in names}
        n_scores = HEADS // 2 * NT
        with ExitStack() as scope:
            sb = lambda name, shape: self.sbuf(scope, name, shape)
            cst = sb("ret_const", [P, RETC_N])
            cc = lambda n: cst[:, RETC[n][0]:RETC[n][1]]
            w = sb("w_ret", [P, KD, RET_COLS])
            qk = sb("ret_qk", [P, 2, 8, 64])
            turn = sb("ret_turn", [P, 4, 8, 32])
            v, g = sb("ret_v", [P, NT, 256]), sb("ret_gate", [P, NT, 256])
            qk_t = sb("ret_qk_t", [P, 4, TOK])
            strip_a, strip_b = sb("strip_a", [P, 896]), sb("strip_b", [P, 640])
            part_a, part_b = sb("part_a", [P, 896]), sb("part_b", [P, 640])
            spare = w[:, :, :].rearrange("p k n -> p (k n)")
            att = spare[:, 0:NT * 512].rearrange("p (t n) -> p t n", t=NT)
            att_c = spare[:, 3072:3072 + CT * 256].rearrange("p (t n) -> p t n", t=CT)
            out = spare[:, 4096:4096 + NT * 256].rearrange("p (t n) -> p t n", t=NT)
            dec = sb("ret_decay", [P, 4, 8])
            st = sb("ret_stat", [P, 4, 24])
            block = scope.enter_context(nc.Block())
            proj = lambda t: self.flat[:, 1024 * (t % 2):1024 * (t % 2) + 1024]
            o = self.flat[:, 2048 + 512:2048 + 512 + NT * 256].rearrange("p (t n) -> p t n", t=NT)

            @block.sync
            def _(sp):
                sp.dma_start(cst[:, :], io["retc"]).then_inc(landed.sem, 16)
                sp.dma_start(w[:, :, :], io["w_in"][l, :, MLA_COLS:MLA_COLS + RET_COLS].rearrange("(k p) n -> p k n", p=P)).then_inc(landed.sem, 16)

            @block.tensor
            def _(pe):
                pe.wait_ge(landed.sem, landed + 2)

                def turn_tile(t):
                    pe.wait_ge(s["rotated"].sem, s["rotated"] + (t + 1))
                    if t >= 1:
                        pe.wait_ge(s["turned_t"].sem, s["turned_t"] + t)
                    for a in range(4):
                        mm = pe.transpose(self.psum[:, 4, a * P:(a + 1) * P],
                                          qk[:, t % 2, 2 * a:2 * a + 2, :].rearrange("p a d -> p (a d)"), self.c("ident"))
                    mm.then_inc(s["turned"].sem, 1)

                for t in range(NT):
                    if t >= 2:
                        pe.wait_ge(s["rotated"].sem, s["rotated"] + (t - 1))
                        pe.wait_ge(s["gated"].sem, s["gated"] + (t - 1))
                        pe.wait_ge(s["v_copied"].sem, s["v_copied"] + (t - 1))
                    for b in range(2):
                        for k in range(KD):
                            mm = pe.matmul(proj(t)[:, b * 512:(b + 1) * 512], self.u_t[:, k, t * P:(t + 1) * P],
                                           w[:, k, b * 512:(b + 1) * 512], start=(k == 0), stop=(k == KD - 1))
                    mm.then_inc(s["projected"].sem, 1)
                    if t >= 1:
                        turn_tile(t - 1)
                turn_tile(NT - 1)
                pe.wait_ge(s["turned_t"].sem, s["turned_t"] + NT)
                pe.wait_ge(s["gated"].sem, s["gated"] + NT)
                pe.wait_ge(s["v_copied"].sem, s["v_copied"] + NT)
                n = 0
                for h in range(4):
                    lo, f = 64 * (h % 2), h // 2
                    for j in range(NT):
                        if n >= 2:
                            pe.wait_ge(s["weighted"].sem, s["weighted"] + (n - 1))
                        key = qk_t[lo:lo + 64, 2 + f, j * P:(j + 1) * P]
                        if j < CT and not last:
                            pe.matmul(proj(n)[:, 0:CTX], key, qk_t[lo:lo + 64, f, 0:CTX], start=True, stop=True)
                        pe.matmul(proj(n)[:, 512:1024], key, qk_t[lo:lo + 64, f, CTX:TOK], start=True, stop=True
                                  ).then_inc(s["scores"].sem, 1)
                        n += 1
                    pe.wait_ge(s["weighted"].sem, s["weighted"] + n)
                    for t in tiles:
                        keys = list(range(CT if t < CT else NT))
                        for j in keys:
                            a = att_c[:, j, t * P:(t + 1) * P] if t < CT else att[:, j, (t - CT) * P:(t - CT + 1) * P]
                            mm = pe.matmul(o[:, t, h * 64:(h + 1) * 64], a, v[:, j, h * 64:(h + 1) * 64],
                                           start=(j == keys[0]), stop=(j == keys[-1]))
                    mm.then_inc(s["head_done"].sem, 1)
                pe.wait_ge(s["normed"].sem, s["normed"] + 1)
                for n, t in enumerate(tiles):
                    if n >= 2:
                        pe.wait_ge(s["out_t"].sem, s["out_t"] + (n - 1))
                    for a in range(2):
                        mm = pe.transpose(self.psum[:, n % 2, a * P:(a + 1) * P], out[:, t, a * P:(a + 1) * P], self.c("ident"))
                    mm.then_inc(s["out_turned"].sem, 1)

            @block.scalar
            def _(act):
                link = self.act_chain.on(act)
                for t in range(NT):
                    act.wait_ge(s["projected"].sem, s["projected"] + (t + 1))
                    act.copy(v[:, t, :], proj(t)[:, 512:768]).then_inc(s["v_copied"].sem, 1)
                    act.activation(g[:, t, :], proj(t)[:, 768:1024], ACT.Sigmoid).then_inc(s["gate"].sem, 1)
                act.wait_ge(s["log_decay"].sem, s["log_decay"] + 1)
                act.activation(dec[:, 1, :], dec[:, 0, :], ACT.Exp, scale=-1.0).then_inc(s["decay_exp"].sem, 1)
                act.wait_ge(s["decay_exp"].sem, s["decay_exp"] + 1)
                act.activation(dec[:, 2, :], dec[:, 1, :], ACT.Ln, bias=1.0).then_inc(s["decay_ln"].sem, 1)
                act.wait_ge(s["log_decay"].sem, s["log_decay"] + 2)
                for h in range(4):
                    if h >= 1:
                        act.wait_ge(s["strips"].sem, s["strips"] + h)
                        act.wait_ge(s["weighted"].sem, s["weighted"] + h * NT)
                    f, b = dec[:, 3, h:h + 1], dec[:, 3, 4 + h:5 + h]
                    act.activation(strip_a[:, :], cc("dist"), ACT.Exp, scale=f)
                    act.activation(part_a[:, :], cc("dist"), ACT.Exp, scale=b)
                    act.activation(strip_b[:, :], cc("dist_f"), ACT.Exp, scale=f)
                    act.activation(part_b[:, :], cc("dist_b"), ACT.Exp, scale=b).then_inc(s["powers"].sem, 1)
                act.wait_ge(s["var"].sem, s["var"] + 1)
                act.activation(st[:, 2, :], st[:, 1, :], ACT.Sqrt).then_inc(s["root"].sem, 1)
                for n, t in enumerate(tiles):
                    act.wait_ge(s["out_turned"].sem, s["out_turned"] + (n + 1))
                    act.copy(self.mix_t[:, 4:6, t * P:(t + 1) * P],
                             self.psum[:, n % 2, 0:256].rearrange("p (a n) -> p a n", n=P)).then_inc(s["out_t"].sem, 1)

            @block.vector
            def _(dve):
                link = self.dve_chain.on(dve)
                dve.wait_ge(landed.sem, landed + 2)
                link(dve.tensor_scalar(dec[:, 3, :], self.row("decay"), -1.0, None, ALU.mult))
                dve.tensor_tensor(dec[:, 0, :], dec[:, 3, :], self.row("decay"), ALU.max).then_inc(s["log_decay"].sem, 1)
                for t in range(NT):
                    dve.wait_ge(s["projected"].sem, s["projected"] + (t + 1))
                    rows = proj(t)[:, 0:512].rearrange("p (a d) -> p a d", d=64)
                    x1, x2 = rows[:, :, 0:32], rows[:, :, 32:64]
                    cos = spread(cc("seq_cos")[:, t * 32:(t + 1) * 32], 1, 8)
                    sin = spread(cc("seq_sin")[:, t * 32:(t + 1) * 32], 1, 8)
                    link(dve.tensor_tensor(turn[:, 0], x1, cos, ALU.mult))
                    link(dve.tensor_tensor(turn[:, 1], x2, sin, ALU.mult))
                    link(dve.tensor_tensor(turn[:, 2], x1, sin, ALU.mult))
                    link(dve.tensor_tensor(turn[:, 3], x2, cos, ALU.mult))
                    if t >= 2:
                        dve.wait_ge(s["turned"].sem, s["turned"] + (t - 1))
                    link(dve.tensor_tensor(qk[:, t % 2, :, 0:32], turn[:, 0], turn[:, 1], ALU.subtract))
                    dve.tensor_tensor(qk[:, t % 2, :, 32:64], turn[:, 2], turn[:, 3], ALU.add).then_inc(s["rotated"].sem, 1)
                    dve.wait_ge(s["gate"].sem, s["gate"] + (t + 1))
                    dve.tensor_tensor(g[:, t, :], g[:, t, :], proj(t)[:, 768:1024], ALU.mult).then_inc(s["gated"].sem, 1)
                    dve.wait_ge(s["turned"].sem, s["turned"] + (t + 1))
                    dve.tensor_copy(qk_t[:, :, t * P:(t + 1) * P],
                                    self.psum[:, 4, :].rearrange("p (a n) -> p a n", n=P)).then_inc(s["turned_t"].sem, 1)
                dve.wait_ge(s["decay_ln"].sem, s["decay_ln"] + 1)
                link(dve.tensor_scalar(dec[:, 3, :], self.row("decay"), 0.0, None, ALU.min))
                dve.tensor_tensor(dec[:, 3, :], dec[:, 3, :], dec[:, 2, :], ALU.subtract).then_inc(s["log_decay"].sem, 1)
                n = 0
                for h in range(4):
                    dve.wait_ge(s["powers"].sem, s["powers"] + (h + 1))
                    link(dve.tensor_tensor(strip_a[:, :], strip_a[:, :], cc("after"), ALU.mult))
                    link(dve.tensor_tensor(part_a[:, :], part_a[:, :], cc("before"), ALU.mult))
                    link(dve.tensor_tensor(strip_a[:, :], strip_a[:, :], part_a[:, :], ALU.add))
                    dve.tensor_tensor(strip_b[:, :], strip_b[:, :], part_b[:, :], ALU.add).then_inc(s["strips"].sem, 1)
                    dve.wait_ge(s["strips"].sem, s["strips"] + (h + 1))
                    if h >= 1:
                        dve.wait_ge(s["head_done"].sem, s["head_done"] + h)
                    for j in range(NT):
                        dve.wait_ge(s["scores"].sem, s["scores"] + (n + 1))
                        if j < CT:
                            if not last:
                                dve.scalar_tensor_tensor(att_c[:, j, :], proj(n)[:, 0:CTX], 0.125,
                                                         strip_a[:, 384 - j * P:384 - j * P + CTX], ALU.mult, ALU.mult)
                            strip = strip_b[:, P - j * P:P - j * P + LAT]
                        else:
                            strip = strip_a[:, 384 - (j - CT) * P:384 - (j - CT) * P + LAT]
                        dve.scalar_tensor_tensor(att[:, j, :], proj(n)[:, 512:1024], 0.125, strip,
                                                 ALU.mult, ALU.mult).then_inc(s["weighted"].sem, 1)
                        n += 1
                dve.wait_ge(s["head_done"].sem, s["head_done"] + 4)
                lo = tiles[0]
                rows = lambda a: a.rearrange("p t (h d) -> p (t h) d", d=64)
                src, dst = rows(o[:, lo:NT, :]), rows(out[:, lo:NT, :])
                a, b = lo * 4, NT * 4
                link(dve.memset(st[:, :, :], 1.0))
                link(dve.tensor_reduce(st[:, 0, a:b], src, AX, ALU.add))
                link(dve.tensor_scalar(st[:, 0, a:b], st[:, 0, a:b], 1.0 / 64, None, ALU.mult))
                link(dve.tensor_tensor(dst, src, spread(st[:, 0, a:b], 2, 64), ALU.subtract))
                sq = att[:, 0:3, :].rearrange("p a b -> p (a b)")[:, 0:(b - a) * 64].rearrange("p (r d) -> p r d", d=64)
                link(dve.tensor_tensor(sq, dst, dst, ALU.mult))
                link(dve.tensor_reduce(st[:, 1, a:b], sq, AX, ALU.add))
                dve.tensor_scalar(st[:, 1, a:b], st[:, 1, a:b], 1.0 / 64, 1e-5, ALU.mult, ALU.add).then_inc(s["var"].sem, 1)
                dve.wait_ge(s["root"].sem, s["root"] + 1)
                link(dve.reciprocal(st[:, 3, a:b], st[:, 2, a:b]))
                link(dve.tensor_tensor(dst, dst, spread(st[:, 3, a:b], 2, 64), ALU.mult))
                link(dve.tensor_tensor(out[:, lo:NT, :], out[:, lo:NT, :], spread(self.row("gn_w"), 1, NT - lo), ALU.mult))
                dve.tensor_tensor(out[:, lo:NT, :], out[:, lo:NT, :], g[:, lo:NT, :], ALU.mult).then_inc(s["normed"].sem, 1)
        landed.advance(2)
        once = {"decay_exp": 1, "decay_ln": 1, "log_decay": 2, "powers": 4, "strips": 4, "head_done": 4, "var": 1,
                "root": 1, "normed": 1, "scores": n_scores, "weighted": n_scores,
                "out_turned": len(tiles), "out_t": len(tiles)}
        for n in names:
            s[n].advance(once.get(n, NT))

    def rwkv(self, l, last):
        with ExitStack() as scope:
            sb = lambda name, shape: self.sbuf(scope, name, shape)
            cst = sb("rwkv_const", [P, RWKVC_N])
            self.cc = lambda n: cst[:, RWKVC[n][0]:RWKVC[n][1]]
            g, bonus = sb("rwkv_g", [P, 2, TOK]), sb("rwkv_bonus", [P, 2, TOK])
            v = sb("rwkv_v", [P, 2, TOK])
            queries = self.u_t[:, :, :].rearrange("p k n -> p (k n)").rearrange("p (q c a t) -> p q c a t", q=4, c=NCH, a=2)
            updates = sb("updates", [P, 4, NCH, 2, C])
            half = sb("half_decay", [P, 4, NCH])
            self.rwkv_features(l, cst, g, bonus, v, queries, updates, half)
            self.rwkv_chunks(l, last, g, bonus, v, queries, updates, half)

    def rwkv_features(self, l, cst, g, bonus, v, queries, updates, half):
        nc, io, cc = self.nc, self.io, self.cc
        landed = self.count("rwkv_weights_landed", 16)
        names = ("projected", "tile_read", "shifted", "wide", "wide_act", "wide_read", "table", "root",
                 "decay_exp", "decay_in")
        s = {n: self.count("rwkv_" + n) for n in names}
        order = (7, 8, 6, 0, 1, 2, 3, 4, 5)
        at = [(n * P, P) for n in range(7)] + [(896, 64), (960, P)]
        with ExitStack() as scope:
            sb = lambda name, shape: self.sbuf(scope, name, shape)
            feat = sb("rwkv_feat", [P, 4, TOK])
            low = sb("rwkv_low", [P, 3, TOK])
            raw = sb("rwkv_raw", [P, TOK + 4])
            lw = sb("log_w", [P, 4, TOK])
            a = sb("rwkv_a", [P, 2, TOK])
            small = sb("rwkv_small", [P, 3, 256])
            with ExitStack() as inner:
                w = self.sbuf(inner, "w_rwkv", [P, KD, 2, P])
                s_w = [self.count(f"rwkv_w_landed{i}", 16) for i in range(2)]
                block = inner.enter_context(nc.Block())

                @block.sync
                def _(sp):
                    sp.dma_start(cst[:, :], io["rwkvc"]).then_inc(landed.sem, 16)
                    sp.dma_start(small[:, 0, :], io["rwkv_w2"][l].rearrange("d k n -> (d k) n")).then_inc(landed.sem, 16)
                    sp.dma_start(small[0:64, 1, :], io["rwkv_a2"][l]).then_inc(landed.sem, 16)
                    sp.dma_start(small[:, 2, :], io["rwkv_g2"][l]).then_inc(landed.sem, 16)
                    for n, f in enumerate(order):
                        lo, width = at[f]
                        if n >= 2:
                            sp.wait_ge(s["projected"].sem, s["projected"] + (n - 1))
                        c0 = MLA_COLS + RET_COLS + lo
                        sp.dma_start(w[:, :, n % 2, 0:width], io["w_in"][l, :, c0:c0 + width].rearrange("(k p) n -> p k n", p=P)
                                     ).then_inc(s_w[n % 2].sem, 16)
                    sp.wait_ge(landed.sem, landed + 4)

                @block.tensor
                def _(pe):
                    for n, f in enumerate(order):
                        width = at[f][1]
                        pe.wait_ge(s_w[n % 2].sem, s_w[n % 2] + (n // 2 + 1))
                        if n >= 2:
                            pe.wait_ge(s["tile_read"].sem, s["tile_read"] + (n - 1))
                        for lo, hi in ((0, CTX), (CTX, TOK)):
                            b = 2 * (n % 2) + (lo > 0)
                            for k in range(KD):
                                mm = pe.matmul(self.psum[0:width, b, 0:hi - lo], w[:, k, n % 2, 0:width],
                                               self.u_t[:, k, lo:hi], start=(k == 0), stop=(k == KD - 1))
                        mm.then_inc(s["projected"].sem, 1)

                @block.vector
                def _(dve):
                    link = self.dve_chain.on(dve)
                    link(dve.memset(raw[:, :], 0.0))
                    for n, f in enumerate(order):
                        width = at[f][1]
                        dve.wait_ge(s["projected"].sem, s["projected"] + (n + 1))
                        link(dve.tensor_copy(raw[0:width, 1:1 + CTX], self.psum[0:width, 2 * (n % 2), 0:CTX]))
                        dve.tensor_copy(raw[0:width, 3 + CTX:3 + TOK], self.psum[0:width, 2 * (n % 2) + 1, 0:LAT]
                                        ).then_inc(s["tile_read"].sem, 1)
                        dve.wait_ge(s["tile_read"].sem, s["tile_read"] + (n + 1))
                        dst = {6: low[:, 0], 7: low[:, 1], 8: low[:, 2], 4: v[:, 0], 5: v[:, 1]}.get(f)
                        if dst is None:
                            dst = feat[:, f]
                        for lo, off in ((0, 1), (CTX, 3)):
                            width_t = CTX if lo == 0 else LAT
                            now = raw[0:width, lo + off:lo + off + width_t]
                            before, after = (raw[0:width, lo + off + d:lo + off + d + width_t] for d in (-1, 1))
                            to = dst[0:width, lo:lo + width_t]
                            link(dve.tensor_tensor(to, before, after, ALU.add))
                            link(dve.scalar_tensor_tensor(to, to, 0.5, now, ALU.mult, ALU.subtract))
                            link(dve.scalar_tensor_tensor(to, to, self.col("mu")[0:width, f:f + 1], now, ALU.mult, ALU.add))
            landed.advance(4)
            s["projected"].advance(9)
            s["tile_read"].advance(9)
            s_w[0].advance(5)
            s_w[1].advance(4)

            with ExitStack() as inner:
                sb = lambda name, shape: self.sbuf(inner, name, shape)
                kk, tmp = sb("kk", [P, 2, TOK]), raw[:, 0:TOK]
                inc, exc = sb("decay_x1", [P, TOK]), sb("decay_x2", [P, TOK])
                exps = low
                tot = sb("chunk_total", [P, NCH])
                block = inner.enter_context(nc.Block())
                halves = ((0, CTX), (CTX, TOK))
                wide = lambda n: self.psum[:, 2 * (n % 2):2 * (n % 2) + 2, :]
                jobs = [("w", q) for q in range(4)] + [("a", f) for f in range(2)] + [("g", f) for f in range(2)] + \
                       [("kk", f) for f in range(2)] + [("bonus", f) for f in range(2)]

                def each_half(n):
                    return [(wide(n)[:, b, 0:hi - lo], slice(lo, hi)) for b, (lo, hi) in enumerate(halves)]

                @block.tensor
                def _(pe):
                    pe.wait_ge(s["wide_act"].sem, s["wide_act"] + 1)
                    for n, (job, q) in enumerate(jobs):
                        if n >= 2:
                            pe.wait_ge(s["wide_read"].sem, s["wide_read"] + (n - 1))
                        if job in ("kk", "bonus"):
                            pe.wait_ge(s["table"].sem, s["table"] + (n - 7))
                        for b, (lo, hi) in enumerate(halves):
                            d, f = divmod(q, 2)
                            lhs, rhs = {
                                "w": lambda: (small[64 * d:64 * d + 64, 0, f * P:(f + 1) * P], low[64 * d:64 * d + 64, 0, lo:hi]),
                                "a": lambda: (small[0:64, 1, q * P:(q + 1) * P], low[0:64, 1, lo:hi]),
                                "g": lambda: (small[:, 2, q * P:(q + 1) * P], low[:, 2, lo:hi]),
                                "kk": lambda: (self.c("pair_ones"), tmp[:, lo:hi]),
                                "bonus": lambda: (self.c("pair_ones"), tmp[:, lo:hi])}[job]()
                            mm = pe.matmul(wide(n)[:, b, 0:hi - lo], lhs, rhs, start=True, stop=True)
                        mm.then_inc(s["wide"].sem, 1)

                @block.scalar
                def _(act):
                    act.activation(low[:, 0, :], low[:, 0, :], ACT.Tanh)
                    act.activation(low[:, 2, :], low[:, 2, :], ACT.Sigmoid).then_inc(s["wide_act"].sem, 1)
                    for n, (job, q) in enumerate(jobs[0:8]):
                        act.wait_ge(s["wide"].sem, s["wide"] + (n + 1))
                        for src, cut in each_half(n):
                            if job == "w":
                                ins = act.activation(lw[:, q, cut], src, ACT.Sigmoid, bias=self.col("w0")[:, q:q + 1])
                            elif job == "a":
                                ins = act.activation(a[:, q, cut], src, ACT.Sigmoid, bias=self.col("a0")[:, q:q + 1])
                            else:
                                ins = act.copy(g[:, q, cut], src)
                        ins.then_inc(s["wide_read"].sem, 1)
                    for f in range(2):
                        act.wait_ge(s["root"].sem, s["root"] + (2 * f + 1))
                        act.activation(tmp, tmp, ACT.Sqrt).then_inc(s["root"].sem, 1)
                    for q in range(4):
                        act.wait_ge(s["decay_in"].sem, s["decay_in"] + (q + 1))
                        sign = (1.0, -1.0)[q // 2]
                        by_query, by_update = (exc, inc) if q < 2 else (inc, exc)
                        act.activation(exps[:, 0, :], by_query[:, :], ACT.Exp, scale=sign)
                        act.activation(exps[:, 1, :], by_update[:, :], ACT.Exp, scale=sign)
                        act.activation(exps[:, 2, :], by_update[:, :], ACT.Exp, scale=-sign)
                        act.activation(half[:, q, :], tot[:, :], ACT.Exp, scale=0.5).then_inc(s["decay_exp"].sem, 1)

                @block.vector
                def _(dve):
                    link = self.dve_chain.on(dve)
                    dve.wait_ge(s["wide_read"].sem, s["wide_read"] + 8)
                    for q in range(4):
                        link(dve.tensor_scalar(lw[:, q, :], lw[:, q, :], DECAY, None, ALU.mult))
                    for f in range(2):
                        n = 8 + f
                        link(dve.tensor_scalar(kk[:, f, :], feat[:, 2 + f, :], self.col("k_k")[:, f:f + 1], None, ALU.mult))
                        dve.tensor_tensor(tmp, kk[:, f, :], kk[:, f, :], ALU.mult).then_inc(s["table"].sem, 1)
                        dve.wait_ge(s["wide"].sem, s["wide"] + (n + 1))
                        for src, cut in each_half(n):
                            ins = dve.tensor_scalar(tmp[:, cut], src, 1e-24, None, ALU.max)
                            if cut.start:
                                ins.then_inc(s["wide_read"].sem, 1)
                            else:
                                link(ins)
                        dve.wait_ge(s["wide_read"].sem, s["wide_read"] + (n + 1))
                        dve.tensor_copy(tot[:, 0:1], tmp[:, 0:1]).then_inc(s["root"].sem, 1)
                        dve.wait_ge(s["root"].sem, s["root"] + (2 * f + 2))
                        link(dve.reciprocal(tmp, tmp))
                        link(dve.tensor_tensor(kk[:, f, :], kk[:, f, :], tmp, ALU.mult))
                    for f in range(2):
                        link(dve.tensor_scalar(tmp, a[:, f, :], -1.0, self.col("k_a")[:, f:f + 1], ALU.add, ALU.mult))
                        link(dve.scalar_tensor_tensor(feat[:, 2 + f, :], tmp, 1.0, feat[:, 2 + f, :], ALU.add, ALU.mult))
                        link(dve.tensor_tensor(a[:, f, :], a[:, f, :], kk[:, f, :], ALU.mult))
                    for f in range(2):
                        n = 10 + f
                        dve.scalar_tensor_tensor(tmp, feat[:, f, :], self.col("r_k")[:, f:f + 1], feat[:, 2 + f, :],
                                                 ALU.mult, ALU.mult).then_inc(s["table"].sem, 1)
                        dve.wait_ge(s["wide"].sem, s["wide"] + (n + 1))
                        for src, cut in each_half(n):
                            ins = dve.tensor_tensor(bonus[:, f, cut], src, v[:, f, cut], ALU.mult)
                        ins.then_inc(s["wide_read"].sem, 1)
                    chunks = lambda ap: ap.rearrange("p (c t) -> p c t", t=C)
                    for q in range(4):
                        f = q % 2
                        link(dve.tensor_tensor_scan(inc[:, :], cc("restart"), lw[:, q, :], 0.0, ALU.mult, ALU.add))
                        link(dve.tensor_copy(tot[:, :], chunks(inc[:, :])[:, :, C - 1]))
                        link(dve.scalar_tensor_tensor(chunks(inc[:, :]), spread(tot[:, :], 2, C), -0.5, chunks(inc[:, :]),
                                                      ALU.mult, ALU.add))
                        dve.tensor_tensor(exc[:, :], inc[:, :], lw[:, q, :], ALU.subtract).then_inc(s["decay_in"].sem, 1)
                        dve.wait_ge(s["decay_exp"].sem, s["decay_exp"] + (q + 1))
                        e = lambda i: chunks(exps[:, i, :])
                        dve.tensor_tensor(queries[:, q, :, 0, :], chunks(kk[:, f, :]), e(0), ALU.mult)
                        dve.tensor_tensor(queries[:, q, :, 1, :], chunks(feat[:, f, :]), e(1), ALU.mult)
                        dve.scalar_tensor_tensor(updates[:, q, :, 0, :], chunks(a[:, f, :]), -1.0, e(2), ALU.mult, ALU.mult)
                        link(dve.tensor_tensor(updates[:, q, :, 1, :], chunks(feat[:, 2 + f, :]), e(2), ALU.mult))
            for n, k in (("wide", 12), ("wide_act", 1), ("wide_read", 12), ("table", 4), ("root", 4),
                         ("decay_exp", 4), ("decay_in", 4)):
                s[n].advance(k)

    def rwkv_chunks(self, l, last, g, bonus, v, queries, updates, half):
        nc, cc = self.nc, self.cc
        back = list(range(CCH - 1, -1, -1)) + list(range(NCH - 1, CCH - 1, -1))
        ch = lambda q, i: i if q < 2 else back[i]
        names = ("prep", "masked", "copied", "inner", "inner_copied", "grown", "added", "rest", "rest_copied",
                 "removed", "removed_copied", "moved", "state", "summed", "var", "root", "normed", "turned")
        s = {n: self.count("chunk_" + n) for n in names}
        NL = len(LEVELS)
        with ExitStack() as scope:
            sb = lambda name, shape: self.sbuf(scope, name, shape)
            m_b, m_k = sb("queries_b", [P, 2, 4, 2, C]), sb("queries_k", [P, 2, 4, 2, C])
            inv = sb("inverse", [P, 2, 2, 4, C])
            steps = sb("level_blocks", [P, NL, 4, C])
            inner = sb("inner", [P, 4, C])
            rows = sb("update_rows", [P, 2, 3, 4, C])
            state, rest, removed = sb("state", [P, 4, C]), sb("rest", [P, 4, C]), sb("removed", [P, 4, C])
            move = sb("state_decay", [P, 4])
            y = sb("rwkv_y", [P, 2, NCH, 2, C])
            st = sb("rwkv_stat", [P, 4, 2 * NCH])
            sq = sb("rwkv_squares", [P, 2 * NCH, C])
            block = scope.enter_context(nc.Block())
            ps = lambda bank, half_: self.psum[:, bank, 256 * half_:256 * half_ + 256].rearrange("p (q t) -> p q t", q=4)
            heads = [(q, slice(64 * e, 64 * e + 64)) for q in range(4) for e in range(2)]

            @block.tensor
            def _(pe):
                def prepare(i):
                    if i >= 1:
                        pe.wait_ge(s["masked"].sem, s["masked"] + i)
                        pe.wait_ge(s["copied"].sem, s["copied"] + i)
                    for q, r in heads:
                        c, f = ch(q, i), q % 2
                        rd, wb, wk = queries[r, q, c, :, :], updates[r, q, c, 0, :], updates[r, q, c, 1, :]
                        eye = self.c("ident64")[r, :]
                        both = rd.rearrange("p a t -> p (a t)")
                        pe.matmul(self.psum[r, 0, q * 128:q * 128 + 128], wb, both, start=True, stop=True)
                        pe.matmul(self.psum[r, 1, q * 128:q * 128 + 128], wk, both, start=True, stop=True)
                        pe.matmul(ps(2, 0)[r, q, :], rd[:, 0, :], wb, start=True, stop=True)
                        pe.matmul(ps(3, 0)[r, q, :], wb, eye, start=True, stop=True)
                        pe.matmul(ps(3, 1)[r, q, :], wk, eye, start=True, stop=True)
                        mm = pe.matmul(ps(2, 1)[r, q, :], v[r, f, c * C:(c + 1) * C], eye, start=True, stop=True)
                    mm.then_inc(s["prep"].sem, 1)

                def inner_part(i, n):
                    if n == 0:
                        pe.wait_ge(s["masked"].sem, s["masked"] + (i + 1))
                    else:
                        pe.wait_ge(s["added"].sem, s["added"] + (NL * i + n))
                    for q, r in heads:
                        mm = pe.matmul(ps(4, 0)[r, q, :], steps[r, n, q, :], inv[r, i % 2, 1, q, :], start=True, stop=True)
                    mm.then_inc(s["inner"].sem, 1)

                def grow(i, n):
                    pe.wait_ge(s["inner_copied"].sem, s["inner_copied"] + (NL * i + n + 1))
                    for q, r in heads:
                        mm = pe.matmul(ps(5, 0)[r, q, :], inner[r, q, :], inv[r, i % 2, 0, q, :], start=True, stop=True)
                        if n < NL - 1:
                            mm = pe.matmul(ps(5, 1)[r, q, :], inv[r, i % 2, 0, q, :], inner[r, q, :], start=True, stop=True)
                    mm.then_inc(s["grown"].sem, 1)

                def rest_part(i):
                    pe.wait_ge(s["state"].sem, s["state"] + (i + 1))
                    for q, r in heads:
                        pe.matmul(ps(6, 0)[r, q, :], queries[r, q, ch(q, i), 0, :], state[r, q, :], start=True, stop=False)
                        mm = pe.matmul(ps(6, 0)[r, q, :], m_k[r, i % 2, q, 0, :], rows[r, i % 2, 2, q, :], start=False, stop=True)
                    mm.then_inc(s["rest"].sem, 1)

                def removed_part(i):
                    pe.wait_ge(s["rest_copied"].sem, s["rest_copied"] + (i + 1))
                    pe.wait_ge(s["added"].sem, s["added"] + NL * (i + 1))
                    for q, r in heads:
                        mm = pe.matmul(ps(6, 1)[r, q, :], inv[r, i % 2, 0, q, :], rest[r, q, :], start=True, stop=True)
                    mm.then_inc(s["removed"].sem, 1)

                def move_part(i):
                    pe.wait_ge(s["removed_copied"].sem, s["removed_copied"] + (i + 1))
                    for q, r in heads:
                        pe.matmul(ps(7, 0)[r, q, :], queries[r, q, ch(q, i), 1, :], state[r, q, :], start=True, stop=False)
                        pe.matmul(ps(7, 0)[r, q, :], m_b[r, i % 2, q, 1, :], removed[r, q, :], start=False, stop=False)
                        pe.matmul(ps(7, 0)[r, q, :], m_k[r, i % 2, q, 1, :], rows[r, i % 2, 2, q, :], start=False, stop=True)
                        pe.matmul(ps(7, 1)[r, q, :], rows[r, i % 2, 0, q, :], removed[r, q, :], start=True, stop=False)
                        mm = pe.matmul(ps(7, 1)[r, q, :], rows[r, i % 2, 1, q, :], rows[r, i % 2, 2, q, :], start=False, stop=True)
                    mm.then_inc(s["moved"].sem, 1)

                for i in range(NCH + 1):
                    chain = (rest_part, removed_part, move_part)
                    if i < NCH:
                        prepare(i)
                    for n in range(NL):
                        if i < NCH:
                            inner_part(i, n)
                        if i >= 1 and n < len(chain):
                            chain[n](i - 1)
                        if i < NCH:
                            grow(i, n)
                pe.wait_ge(s["normed"].sem, s["normed"] + 1)
                for f in range(2):
                    for c in range(NCH):
                        for r in (slice(0, 64), slice(64, 128)):
                            mm = pe.matmul(self.flat[r, 1024 * f + c * C:1024 * f + (c + 1) * C], y[r, 0, c, f, :],
                                           self.c("ident64")[r, :], start=True, stop=True)
                mm.then_inc(s["turned"].sem, 1)

            @block.scalar
            def _(act):
                def copy_rows(i):
                    act.wait_ge(s["prep"].sem, s["prep"] + (i + 1))
                    if i >= 2:
                        act.wait_ge(s["moved"].sem, s["moved"] + (i - 1))
                    act.copy(rows[:, i % 2, 0:2].rearrange("p a q t -> p (a q t)"), self.psum[:, 3, :]).then_inc(s["copied"].sem, 1)

                for i in range(NCH + 1):
                    if i < NCH:
                        copy_rows(i)
                    for n in range(NL):
                        if i < NCH:
                            act.wait_ge(s["inner"].sem, s["inner"] + (NL * i + n + 1))
                            act.copy(inner[:, :, :], ps(4, 0)).then_inc(s["inner_copied"].sem, 1)
                        if i >= 1 and n == 0:
                            act.wait_ge(s["rest"].sem, s["rest"] + i)
                            act.copy(rest[:, :, :], ps(6, 0)).then_inc(s["rest_copied"].sem, 1)
                        if i >= 1 and n == 1:
                            act.wait_ge(s["removed"].sem, s["removed"] + i)
                            act.copy(removed[:, :, :], ps(6, 1)).then_inc(s["removed_copied"].sem, 1)
                act.wait_ge(s["var"].sem, s["var"] + 1)
                act.activation(st[:, 2, :], st[:, 1, :], ACT.Sqrt).then_inc(s["root"].sem, 1)

            @block.vector
            def _(dve):
                link = self.dve_chain.on(dve)

                def mask(i):
                    dve.wait_ge(s["prep"].sem, s["prep"] + (i + 1))
                    if i >= 2:
                        dve.wait_ge(s["moved"].sem, s["moved"] + (i - 1))
                    full = lambda b: self.psum[:, b, :].rearrange("p (q a t) -> p q a t", q=4, a=2)
                    m = cc("mask").rearrange("p (q a t) -> p q a t", q=4, a=2)
                    quarter = lambda ap: ap.rearrange("p (q t) -> p q t", q=4)
                    dve.tensor_copy(rows[:, i % 2, 2], ps(2, 1))
                    link(dve.tensor_tensor(m_b[:, i % 2], full(0), m, ALU.mult))
                    link(dve.tensor_tensor(m_k[:, i % 2], full(1), m, ALU.mult))
                    eye = spread(self.c("ident64"), 1, 4)
                    link(dve.tensor_tensor(inv[:, i % 2, 1], ps(2, 0), quarter(cc("first")), ALU.mult))
                    link(dve.tensor_tensor(inv[:, i % 2, 0], m_b[:, i % 2, :, 0, :], quarter(cc("first_t")), ALU.mult))
                    link(dve.tensor_tensor(inv[:, i % 2, 1], inv[:, i % 2, 1], eye, ALU.add))
                    link(dve.tensor_tensor(inv[:, i % 2, 0], inv[:, i % 2, 0], eye, ALU.add))
                    dve.tensor_tensor(steps[:, :, :, :], spread(m_b[:, i % 2, :, 0, :], 1, NL),
                                      cc("level").rearrange("p (n q t) -> p n q t", n=NL, q=4), ALU.mult).then_inc(s["masked"].sem, 1)

                def set_move(i):
                    for d in range(2):
                        now, then = ch(2 * d, i), ch(2 * d, min(i + 1, NCH - 1))
                        link(dve.tensor_tensor(move[:, 2 * d:2 * d + 2], half[:, 2 * d:2 * d + 2, now],
                                               half[:, 2 * d:2 * d + 2, then], ALU.mult))

                dve.memset(state[:, :, :], 0.0).then_inc(s["state"].sem, 1)
                for i in range(NCH + 1):
                    if i < NCH:
                        mask(i)
                    for n in range(NL):
                        if i < NCH:
                            dve.wait_ge(s["grown"].sem, s["grown"] + (NL * i + n + 1))
                            k = 2 if n < NL - 1 else 1
                            if n == 0:
                                dve.wait_ge(s["masked"].sem, s["masked"] + (i + 1))
                            else:
                                dve.wait_ge(s["added"].sem, s["added"] + (NL * i + n))
                            new = self.psum[:, 5, 0:256 * k].rearrange("p (a q t) -> p a q t", a=k, q=4)
                            dve.tensor_tensor(inv[:, i % 2, 0:k], inv[:, i % 2, 0:k], new, ALU.add).then_inc(s["added"].sem, 1)
                        if i >= 1 and n == 2:
                            j = i - 1
                            set_move(j)
                            dve.wait_ge(s["moved"].sem, s["moved"] + i)
                            link(dve.tensor_copy(y[:, 0, ch(0, j), :, :], ps(7, 0)[:, 0:2, :]))
                            link(dve.tensor_copy(y[:, 1, ch(2, j), :, :], ps(7, 0)[:, 2:4, :]))
                            link(dve.tensor_tensor(state[:, :, :], state[:, :, :], ps(7, 1), ALU.add))
                            dve.tensor_tensor(state[:, :, :], state[:, :, :], spread(move[:, :], 2, C), ALU.mult).then_inc(s["state"].sem, 1)
                y0 = y[:, 0, :, :, :].rearrange("p c f t -> p (c f) t")
                y1 = y[:, 1, :, :, :].rearrange("p c f t -> p (c f) t")
                link(dve.tensor_tensor(y0, y0, y1, ALU.add))
                link(dve.tensor_reduce(st[:, 0, :], y0, AX, ALU.add))
                link(dve.tensor_scalar(st[:, 0, :], st[:, 0, :], 1.0 / 64, None, ALU.mult))
                link(dve.tensor_tensor(y0, y0, spread(st[:, 0, :], 2, C), ALU.subtract))
                link(dve.tensor_tensor(sq[:, :, :], y0, y0, ALU.mult))
                link(dve.tensor_reduce(st[:, 1, :], sq[:, :, :], AX, ALU.add))
                dve.tensor_scalar(st[:, 1, :], st[:, 1, :], 1.0 / 64, 64e-5, ALU.mult, ALU.add).then_inc(s["var"].sem, 1)
                dve.wait_ge(s["root"].sem, s["root"] + 1)
                link(dve.reciprocal(st[:, 3, :], st[:, 2, :]))
                link(dve.tensor_tensor(y0, y0, spread(st[:, 3, :], 2, C), ALU.mult))
                lnw = spread(self.row("ln_w").rearrange("p (f t) -> p f t", f=2), 1, NCH)
                dve.tensor_tensor(y[:, 0, :, :, :], y[:, 0, :, :, :], lnw, ALU.mult).then_inc(s["normed"].sem, 1)
                dve.wait_ge(s["turned"].sem, s["turned"] + 1)
                for f in range(2):
                    to = self.mix_t[:, 6 + f, :]
                    link(dve.tensor_tensor(to, self.flat[:, 1024 * f:1024 * f + TOK], bonus[:, f, :], ALU.add))
                    link(dve.tensor_tensor(to, to, g[:, f, :], ALU.mult))
        per = {"state": NCH + 1, **{n: NL * NCH for n in ("inner", "inner_copied", "grown", "added")},
               **{n: 1 for n in ("summed", "var", "root", "normed", "turned")}}
        for n in names:
            s[n].advance(per.get(n, NCH))

    def project_out(self, l, last, tiles):
        nc, io = self.nc, self.io
        landed, made, added = self.count("w_out_landed", 16), self.count("out_made"), self.count("out_added")
        with ExitStack() as scope:
            w = self.sbuf(scope, "w_out", [P, KD, D])
            tmp = self.sbuf(scope, "gated", [P, D])
            block = scope.enter_context(nc.Block())

            @block.sync
            def _(sp):
                sp.dma_start(w[:, :, :], io["w_out"][l].rearrange("(k p) n -> p k n", p=P)).then_inc(landed.sem, 16)

            @block.tensor
            def _(pe):
                pe.wait_ge(landed.sem, landed + 1)
                for n, t in enumerate(tiles):
                    if n >= 2:
                        pe.wait_ge(added.sem, added + (n - 1))
                    for b in range(2):
                        for k in range(KD):
                            mm = pe.matmul(self.psum[:, 2 * (n % 2) + b, :], self.mix_t[:, k, t * P:(t + 1) * P],
                                           w[:, k, b * 512:(b + 1) * 512], start=(k == 0), stop=(k == KD - 1))
                    mm.then_inc(made.sem, 1)

            @block.vector
            def _(dve):
                self.add_gated(dve, tmp, 0, tiles, made, added)
        landed.advance(1)
        made.advance(len(tiles))
        added.advance(len(tiles))

    def add_gated(self, dve, tmp, which, tiles, made, added):
        link = self.dve_chain.on(dve)
        for n, t in enumerate(tiles):
            dve.wait_ge(made.sem, made + (n + 1))
            product = self.flat[:, 1024 * (n % 2):1024 * (n % 2) + D]
            if n >= 1:
                dve.wait_ge(added.sem, added + n)
            link(dve.tensor_tensor(tmp[:, :], product, self.gates[:, which, int(t < CT), :], ALU.mult))
            dve.tensor_tensor(self.x[:, t, :], self.x[:, t, :], tmp[:, :], ALU.add).then_inc(added.sem, 1)

    def route(self, l, last, tiles):
        nc, io = self.nc, self.io
        landed = self.count("router_landed", 16)
        names = ("logits", "shifted", "exp", "affinity", "turned", "placed", "back")
        s = {n: self.count("route_" + n) for n in names}
        lo = tiles[0]
        groups = [(CT, NT, CAP_L)] + ([] if last else [(0, CT, CAP_C)])
        with ExitStack() as scope:
            sb = lambda name, shape: self.sbuf(scope, name, shape)
            w = sb("router_w", [P, KD, E_N])
            st = sb("router_stat", [P, 3, NT])
            work, chosen = sb("affinity_left", [E_N, TOK]), sb("chosen", [E_N, TOK])
            place, ones = sb("place", [E_N, TOK]), sb("scan_ones", [E_N, LAT])
            best = sb("best", [E_N, 8])
            block = scope.enter_context(nc.Block())
            logits = self.psum[:, 0, 0:NT * E_N].rearrange("p (t e) -> p t e", e=E_N)
            back = self.psum[:, 3, 0:NT * E_N].rearrange("p (t e) -> p t e", e=E_N)
            turned = lambda a, b: self.psum[0:E_N, 1 if a < CT else 2, 0:(b - a) * P]

            @block.sync
            def _(sp):
                sp.dma_start(w[:, :, :], io["router_w"][l].rearrange("(k p) n -> p k n", p=P)).then_inc(landed.sem, 16)

            @block.tensor
            def _(pe):
                pe.wait_ge(landed.sem, landed + 1)
                for t in tiles:
                    for k in range(KD):
                        mm = pe.matmul(logits[:, t, :], self.u_t[:, k, t * P:(t + 1) * P], w[:, k, :],
                                       start=(k == 0), stop=(k == KD - 1))
                mm.then_inc(s["logits"].sem, 1)
                pe.wait_ge(s["affinity"].sem, s["affinity"] + 1)
                for a, b, _ in groups:
                    for t in range(a, b):
                        mm = pe.transpose(turned(a, b)[:, (t - a) * P:(t - a + 1) * P], self.aff[:, t, :], self.c("ident"))
                mm.then_inc(s["turned"].sem, 1)
                pe.wait_ge(s["placed"].sem, s["placed"] + 1)
                for t in tiles:
                    mm = pe.transpose(back[:, t, :], place[:, t * P:(t + 1) * P], self.c("ident")[0:E_N, 0:E_N])
                mm.then_inc(s["back"].sem, 1)

            @block.scalar
            def _(act):
                act.wait_ge(s["shifted"].sem, s["shifted"] + 1)
                act.activation(self.aff[:, lo:NT, :], self.aff[:, lo:NT, :], ACT.Exp).then_inc(s["exp"].sem, 1)

            @block.vector
            def _(dve):
                link = self.dve_chain.on(dve)
                link(dve.memset(ones[:, :], 1.0))
                dve.wait_ge(s["logits"].sem, s["logits"] + 1)
                aff = self.aff[:, lo:NT, :]
                link(dve.tensor_reduce(st[:, 0, lo:NT], logits[:, lo:NT, :], AX, ALU.max))
                dve.tensor_tensor(aff, logits[:, lo:NT, :], spread(st[:, 0, lo:NT], 2, E_N), ALU.subtract).then_inc(s["shifted"].sem, 1)
                dve.wait_ge(s["exp"].sem, s["exp"] + 1)
                link(dve.tensor_reduce(st[:, 1, lo:NT], aff, AX, ALU.add))
                link(dve.reciprocal(st[:, 2, lo:NT], st[:, 1, lo:NT]))
                dve.tensor_tensor(aff, aff, spread(st[:, 2, lo:NT], 2, E_N), ALU.mult).then_inc(s["affinity"].sem, 1)
                dve.wait_ge(s["turned"].sem, s["turned"] + 1)
                for n, (a, b, cap) in enumerate(groups):
                    cut = slice(a * P, b * P)
                    link(dve.tensor_copy(work[:, cut], turned(a, b)))
                    for _ in range(cap // 8):
                        link(dve.max(best[:, :], work[:, cut]))
                        link(dve.match_replace(work[:, cut], best[:, :], work[:, cut], -1.0))
                    link(dve.tensor_scalar(chosen[:, cut], work[:, cut], -1.0, None, ALU.is_equal))
                    link(dve.tensor_tensor_scan(place[:, cut], ones[:, 0:(b - a) * P], chosen[:, cut], 0.0, ALU.mult, ALU.add))
                    link(dve.tensor_tensor(place[:, cut], place[:, cut], chosen[:, cut], ALU.mult))
                    ins = dve.tensor_scalar(place[:, cut], place[:, cut], 1.0, None, ALU.subtract)
                    if n == len(groups) - 1:
                        ins.then_inc(s["placed"].sem, 1)
                    else:
                        link(ins)
                dve.wait_ge(s["back"].sem, s["back"] + 1)
                link(dve.memset(self.slot[:, :, :], -1.0))
                link(dve.tensor_copy(self.slot[:, lo:NT, 0:E_N], back[:, lo:NT, :]))
        landed.advance(1)
        for n in names:
            s[n].advance(1)

    def experts(self, l, last):
        nc, io = self.nc, self.io
        SLOTS, UNROLL = 4, 4
        landed = [self.count(f"expert_w_landed{i}", 16) for i in range(SLOTS)]
        used = [self.count(f"expert_w_used{i}") for i in range(SLOTS)]
        names = ("onehot", "gathered", "tokens", "gate", "up", "sigmoid", "hidden", "turned", "hidden_t", "down", "stored")
        s = {n: self.count("expert_" + n) for n in names}
        M = CAP_L + (0 if last else CAP_C)
        parts = ("exp_w_gate", 0), ("exp_w_gate", 1), ("exp_w_up", 0), ("exp_w_up", 1), ("exp_w_down", 0), ("exp_w_down", 1)
        rounds = UNROLL * len(parts) // SLOTS
        for first in (*used, s["hidden"], s["stored"]):
            first.advance(1)
        with ExitStack() as scope:
            sb = lambda name, shape: self.sbuf(scope, name, shape)
            w = sb("expert_w", [P, SLOTS, 4, D])
            hot = sb("onehot", [P, NT, CAP_L])
            xe = sb("expert_tokens", [P, KD, M])
            sig, hid = sb("expert_sigmoid", [M, D]), sb("expert_hidden", [M, D])
            hid_t = sb("expert_hidden_t", [P, KD, M])
            block = scope.enter_context(nc.Block())
            got_l = self.psum[:, 0, :].rearrange("p (k c) -> p k c", k=KD)
            got_c = self.psum[:, 1, 0:KD * CAP_C].rearrange("p (k c) -> p k c", k=KD)
            turned = self.psum[:, 6:8, 0:4 * M].rearrange("p b (a m) -> p b a m", a=4)

            @block.sync
            def _(sp):
                with sp.Fori(0, E_N // UNROLL) as i:
                    for n in range(UNROLL * len(parts)):
                        name, h = parts[n % len(parts)]
                        slot, turn_ = n % SLOTS, n // SLOTS
                        sp.wait_ge(used[slot].sem, used[slot] + (i * rounds + turn_))
                        expert = i * UNROLL + n // len(parts)
                        src = io[name][l].rearrange("e (h k p) n -> p (e h) k n", p=P, h=2)
                        sp.dma_start(w[:, slot, :, :], src[:, bass.ds(expert * 2 + h, 1), :, :].rearrange("p e k n -> p (e k) n")
                                     ).then_inc(landed[slot].sem, 16)

            @block.tensor
            def _(pe):
                def gather(n):
                    pe.wait_ge(s["onehot"].sem, s["onehot"] + (n + 1))
                    pe.wait_ge(s["tokens"].sem, s["tokens"] + n)
                    for k in range(KD):
                        for t in range(CT, NT):
                            mm = pe.matmul(got_l[:, k, :], self.xn[:, t, k * P:(k + 1) * P], hot[:, t, :],
                                           start=(t == CT), stop=(t == NT - 1))
                    if not last:
                        for k in range(KD):
                            for t in range(CT):
                                mm = pe.matmul(got_c[:, k, :], self.xn[:, t, k * P:(k + 1) * P], hot[:, t, 0:CAP_C],
                                               start=(t == 0), stop=(t == CT - 1))
                    mm.then_inc(s["gathered"].sem, 1)

                def small_product():
                    return pe.matmul(self.psum[0:1, 6, 511:512], self.c("ident")[:, 0:1], self.c("ident")[:, 0:1],
                                     start=True, stop=True)

                def product(i, m, bank, lhs, done):
                    for h in range(2):
                        slot, turn_ = (m + h) % SLOTS, (m + h) // SLOTS
                        pe.wait_ge(landed[slot].sem, landed[slot] + (i * rounds + (turn_ + 1)))
                        for b in range(2):
                            for k in range(4):
                                mm = pe.matmul(self.psum[0:M, bank + b, :], lhs[:, 4 * h + k, :],
                                               w[:, slot, k, b * 512:(b + 1) * 512],
                                               start=(h == 0 and k == 0), stop=(h == 1 and k == 3))
                        mm.then_inc(used[slot].sem, 1)
                    small_product().then_inc(done.sem, 1)

                for slot in range(SLOTS):
                    small_product().then_inc(used[slot].sem, 1)
                gather(0)
                with pe.Fori(0, E_N // UNROLL) as i:
                    for j in range(UNROLL):
                        n, m = i * UNROLL + j, j * len(parts)
                        pe.wait_ge(s["tokens"].sem, s["tokens"] + (n + 1))
                        pe.wait_ge(s["hidden"].sem, s["hidden"] + n)
                        product(i, m, 2, xe, s["gate"])
                        pe.wait_ge(s["stored"].sem, s["stored"] + n)
                        product(i, m + 2, 4, xe, s["up"])
                        gather(n + 1)
                        pe.wait_ge(s["hidden"].sem, s["hidden"] + (n + 1))
                        small_product()
                        for k in range(KD):
                            mm = pe.transpose(turned[:, k // 4, k % 4, :], hid[:, k * P:(k + 1) * P], self.c("ident")[0:M, 0:M])
                        mm.then_inc(s["turned"].sem, 1)
                        pe.wait_ge(s["hidden_t"].sem, s["hidden_t"] + (n + 1))
                        product(i, m + 4, 4, hid_t, s["down"])

            @block.scalar
            def _(act):
                act.copy(self.stat[0:1, 0:1], self.c("iota")[0:1, 0:1]).then_inc(s["stored"].sem, 1)
                with act.Fori(0, E_N // UNROLL) as i:
                    for j in range(UNROLL):
                        n = i * UNROLL + j
                        act.wait_ge(s["gate"].sem, s["gate"] + (n + 1))
                        act.wait_ge(s["hidden"].sem, s["hidden"] + n)
                        act.activation(sig[:, :], self.flat[0:M, 1024:2048], ACT.Sigmoid).then_inc(s["sigmoid"].sem, 1)
                        act.wait_ge(s["turned"].sem, s["turned"] + (n + 1))
                        act.copy(hid_t[:, :, :].rearrange("p (b a) m -> p b a m", a=4), turned).then_inc(s["hidden_t"].sem, 1)
                        act.wait_ge(s["down"].sem, s["down"] + (n + 1))
                        y = self.flat[:, 2048:3072]
                        e = j % 2
                        ins = act.copy(self.y_lat[64 * e:64 * e + 64, bass.ds(i * 2 + j // 2, 1), :].rearrange("p a n -> p (a n)"),
                                       y[0:CAP_L, :])
                        if not last:
                            ins = act.copy(self.y_ctx[32 * j:32 * j + 32, bass.ds(i, 1), :].rearrange("p a n -> p (a n)"),
                                           y[CAP_L:M, :])
                        ins.then_inc(s["stored"].sem, 1)

            @block.vector
            def _(dve):
                link = self.dve_chain.on(dve)

                def onehot(n):
                    cuts = [(CT, NT, CAP_L)] + ([] if last else [(0, CT, CAP_C)])
                    for a, b, cap in cuts:
                        place = self.slot[:, a:b, bass.ds(n, 1)].rearrange("p t e -> p (t e)") if not isinstance(n, int) \
                            else self.slot[:, a:b, n]
                        ins = dve.tensor_tensor(hot[:, a:b, 0:cap], spread(self.c("iota")[:, 0:cap], 1, b - a),
                                                spread(place, 2, cap), ALU.is_equal)
                    ins.then_inc(s["onehot"].sem, 1)

                def tokens(n):
                    dve.wait_ge(s["gathered"].sem, s["gathered"] + (n + 1))
                    cuts = [(got_l, 0, 0, CAP_L)] + ([] if last else [(got_c, 1, CAP_L, CAP_C)])
                    for got, v, at, cap in cuts:
                        to = xe[:, :, at:at + cap]
                        dve.tensor_tensor(to, got, spread(self.scale2[:, :, v], 2, cap), ALU.mult).then_inc(mid.sem, 1)
                        dve.wait_ge(mid.sem, mid + (len(cuts) * n + (1 if at == 0 else 2)))
                        ins = dve.tensor_tensor(to, to, spread(self.mod[:, 24:32, v], 2, cap), ALU.add)
                    ins.then_inc(s["tokens"].sem, 1)

                mid, gated = self.count("expert_scaled"), self.count("expert_gated")
                dve.memset(self.stat[0:1, 1:2], 0.0).then_inc(s["hidden"].sem, 1)
                onehot(0)
                tokens(0)
                with dve.Fori(0, E_N // UNROLL) as i:
                    for j in range(UNROLL):
                        n = i * UNROLL + j
                        onehot(n + 1)
                        dve.wait_ge(s["sigmoid"].sem, s["sigmoid"] + (n + 1))
                        dve.tensor_tensor(sig[:, :], sig[:, :], self.flat[0:M, 1024:2048], ALU.mult).then_inc(gated.sem, 1)
                        dve.wait_ge(gated.sem, gated + (n + 1))
                        dve.wait_ge(s["up"].sem, s["up"] + (n + 1))
                        dve.tensor_tensor(hid[:, :], sig[:, :], self.flat[0:M, 2048:3072], ALU.mult).then_inc(s["hidden"].sem, 1)
                        tokens(n + 1)
                mid.advance((E_N + 1) * (1 if last else 2))
                gated.advance(E_N)
        for slot in range(SLOTS):
            landed[slot].advance(rounds * E_N // UNROLL)
            used[slot].advance(rounds * E_N // UNROLL)
        for n in names:
            s[n].advance(E_N + (n in ("onehot", "gathered", "tokens")))

    def combine(self, l, last, tiles):
        nc = self.nc
        names = ("weights", "turned", "copied", "made", "added")
        s = {n: self.count("combine_" + n) for n in names}
        groups = [(CT, NT, g, 2, CAP_L) for g in range(E_N // 2)] + \
                 ([] if last else [(0, CT, g, 4, CAP_C) for g in range(E_N // 4)])
        with ExitStack() as scope:
            sb = lambda name, shape: self.sbuf(scope, name, shape)
            hot = sb("weighted_onehot", [P, 2, LAT])
            back_l, back_c = sb("scatter_lat", [P, E_N // 2, LAT]), sb("scatter_ctx", [P, E_N // 4, CTX])
            tmp = sb("gated_experts", [P, D])
            block = scope.enter_context(nc.Block())

            @block.tensor
            def _(pe):
                for n, (a, b, g, per, cap) in enumerate(groups):
                    pe.wait_ge(s["weights"].sem, s["weights"] + (n + 1))
                    if n >= 2:
                        pe.wait_ge(s["copied"].sem, s["copied"] + (n - 1))
                    for t in range(b - a):
                        mm = pe.transpose(self.psum[:, 4 + n % 2, t * P:(t + 1) * P], hot[:, n % 2, t * P:(t + 1) * P], self.c("ident"))
                    mm.then_inc(s["turned"].sem, 1)
                pe.wait_ge(s["copied"].sem, s["copied"] + len(groups))
                for n, t in enumerate(tiles):
                    if n >= 2:
                        pe.wait_ge(s["added"].sem, s["added"] + (n - 1))
                    back, y, k, t0 = (back_c, self.y_ctx, E_N // 4, t) if t < CT else (back_l, self.y_lat, E_N // 2, t - CT)
                    for b in range(2):
                        for g in range(k):
                            mm = pe.matmul(self.psum[:, 2 * (n % 2) + b, :], back[:, g, t0 * P:(t0 + 1) * P],
                                           y[:, g, b * 512:(b + 1) * 512], start=(g == 0), stop=(g == k - 1))
                    mm.then_inc(s["made"].sem, 1)

            @block.scalar
            def _(act):
                for n, (a, b, g, per, cap) in enumerate(groups):
                    act.wait_ge(s["turned"].sem, s["turned"] + (n + 1))
                    to = (back_c if a < CT else back_l)[:, g, :]
                    act.copy(to, self.psum[:, 4 + n % 2, 0:(b - a) * P]).then_inc(s["copied"].sem, 1)

            @block.vector
            def _(dve):
                link = self.dve_chain.on(dve)
                for n, (a, b, g, per, cap) in enumerate(groups):
                    if n >= 2:
                        dve.wait_ge(s["turned"].sem, s["turned"] + (n - 1))
                    to = hot[:, n % 2, 0:(b - a) * P].rearrange("p (t e c) -> p t e c", e=per, c=cap)
                    of = lambda x: spread(x[:, a:b, g * per:(g + 1) * per], 3, cap)
                    iota = spread(spread(self.c("iota")[:, 0:cap], 1, per), 1, b - a)
                    link(dve.tensor_tensor(to, iota, of(self.slot), ALU.is_equal))
                    dve.tensor_tensor(to, to, of(self.aff), ALU.mult).then_inc(s["weights"].sem, 1)
                self.add_gated(dve, tmp, 1, tiles, s["made"], s["added"])
        for n in names:
            s[n].advance(len(tiles) if n in ("made", "added") else len(groups))

    def store(self):
        nc, io = self.nc, self.io
        stored = self.count("output_stored", 16)
        with nc.Block() as block:
            @block.sync
            def _(sp):
                sp.dma_start(io["out"].rearrange("(t p) d -> p t d", p=P), self.x[:, CT:NT, :]).then_inc(stored.sem, 16)
                sp.wait_ge(stored.sem, stored + 1)


_WHOLE = ["mod_w", "w_in", "mla_w_uq", "mla_w_ukv", "rwkv_w2", "rwkv_a2", "rwkv_g2", "w_out", "router_w",
          "exp_w_gate", "exp_w_up", "exp_w_down"]


def _by_feature(a):
    return np.asarray(a).reshape(-1, P).T


def kernel(**inputs):
    import concourse.bacc as bacc
    from concourse.bass_utils import run_bass_kernel_spmd

    a = {k: np.asarray(v) for k, v in inputs.items()}
    cols, rows = [], []
    for l in range(DEPTH):
        mu = np.zeros(9 * P, np.float32)
        mu[0:896], mu[896:960], mu[1024:1152] = a["rwkv_mu"][l, 0:896], a["rwkv_mu"][l, 896:960], a["rwkv_mu"][l, 960:1088]
        cols.append(np.concatenate([_by_feature(x) for x in (
            a["mod_b"][l], a["norm1_w"][l], a["norm2_w"][l],
            np.concatenate([a["mla_q_norm_w"][l], a["mla_kv_norm_w"][l]]), mu, a["rwkv_w0"][l], a["rwkv_a0"][l],
            a["rwkv_k_k"][l], a["rwkv_k_a"][l], a["rwkv_r_k"][l])], 1))
        ln = a["rwkv_ln_w"][l].reshape(2, 2, 64)
        row = [a["mla_q_gain"][l], a["mla_k_gain"][l], a["ret_decay"][l].reshape(-1), a["ret_gn_w"][l]]
        rows.append(np.concatenate(
            [np.broadcast_to(np.concatenate(row), (P, ROWS_N - 128)),
             np.concatenate([np.broadcast_to(ln[:, e].reshape(-1), (64, 128)) for e in range(2)], 0)], 1))
    base, retc, rwkvc = constants()
    arrays = {"x": a["x"][0], "ctx": a["ctx"][0],
              "cvec": np.stack([_by_feature(a["c"][0]), _by_feature(a["c_ctx"])], 2),
              "cols": np.stack(cols), "rows": np.stack(rows), "base": base, "retc": retc, "rwkvc": rwkvc}
    for name in _WHOLE:
        arrays[name] = a[name]
    nc = bacc.Bacc("TRN2", target_bir_lowering=False, num_devices=1)
    io, fed = {}, {}
    for name, x in arrays.items():
        x = np.ascontiguousarray(x)
        fed[f"in_{name}"] = x
        io[name] = nc.dram_tensor(f"in_{name}", x.shape, mybir.dt.from_np(x.dtype), kind="ExternalInput").ap()
    io["out"] = nc.dram_tensor("out_0", (LAT, D), F32, kind="ExternalOutput").ap()
    build(nc, io)
    r = run_bass_kernel_spmd(nc, [fed], core_ids=[0])
    return r.results[0]["out_0"].reshape(1, LAT, D)
```

```python
from contextlib import ExitStack

import numpy as np

import concourse.bass as bass
from concourse import mybir

P = 128
D = 1024
KD = D // P
LAT, CTX = 512, 256
TOK = LAT + CTX
CT, NT = CTX // P, TOK // P
DEPTH = 2
EPS = 1e-6

HEADS, NOPE, ROPE, QK, VD = 8, 64, 32, 96, 64
QR, KVR = 384, 256
MLA_COLS = QR + KVR + ROPE
RET_COLS = 1024
RWKV_COLS = 1088
IN_COLS = MLA_COLS + RET_COLS + RWKV_COLS
C = 64
NCH = TOK // C
CCH = CTX // C
DECAY = -0.606531
E_N, CAP_L, CAP_C = 16, 64, 32
LEVELS = (2, 4, 8, 16, 32)
W_SLOTS, W_AHEAD = 3, 2
W_PARTS = tuple((name, half) for name in ("exp_w_gate", "exp_w_up", "exp_w_down") for half in range(2))

F32 = mybir.dt.float32
ALU = mybir.AluOpType
ACT = mybir.ActivationFunctionType
AX = mybir.AxisListType.X


def packed(widths):
    at, out = 0, {}
    for name, n in widths:
        out[name] = (at, at + n)
        at += n
    return out, at


BASE, BASE_N = packed([
    ("ident", 128), ("ones", 128), ("pair_ones", 128), ("ident64", 64), ("iota", 64),
    ("axial_cos", 4 * 16), ("axial_sin", 4 * 16)])
RETC, RETC_N = packed([
    ("seq_cos", 6 * 32), ("seq_sin", 6 * 32),
    ("dist", 896), ("after", 896), ("before", 896), ("dist_f", 640), ("dist_b", 640)])
RWKVC, RWKVC_N = packed([
    ("mask", 4 * 2 * 64), ("first_t", 4 * 64), ("level", len(LEVELS) * 4 * 64),
    ("restart", TOK)])
COLS, COLS_N = packed([
    ("mod_b", 48), ("norm1", 8), ("norm2", 8), ("cn", 5), ("mu", 9), ("w0", 4), ("a0", 2),
    ("k_k", 2), ("k_a", 2), ("r_k", 2)])
ROWS, ROWS_N = packed([("qk_gain", 2 * 96), ("decay", 8), ("gn_w", 256), ("ln_w", 128)])


def constants():
    p = np.arange(P)[:, None]
    packs = [(names, np.zeros((P, n), np.float32)) for names, n in
             ((BASE, BASE_N), (RETC, RETC_N), (RWKVC, RWKVC_N))]

    def put(name, a):
        for names, out in packs:
            if name in names:
                lo, hi = names[name]
                out[:, lo:hi] = np.broadcast_to(np.asarray(a, np.float32).reshape(a.shape[0], -1), (P, hi - lo))

    put("ident", np.eye(P))
    put("ones", np.ones((P, P)))
    put("pair_ones", (p // 64 == np.arange(P) // 64))
    put("ident64", (p % 64 == np.arange(64)))
    put("iota", np.arange(64)[None])
    row = np.repeat(np.arange(LAT // 64, dtype=np.float32), 64)
    col = np.tile(np.arange(64, dtype=np.float32), LAT // 64)
    inv = (np.float32(10000.0) ** (-np.arange(8, dtype=np.float32) / 8)).astype(np.float32)
    ang = np.concatenate([row[:, None] * inv, col[:, None] * inv], -1)
    by_tile = lambda a: a.reshape(-1, P, a.shape[-1]).transpose(1, 0, 2)
    put("axial_cos", by_tile(np.cos(ang)))
    put("axial_sin", by_tile(np.sin(ang)))
    inv = (np.float32(10000.0) ** (-np.linspace(0.0, 1.0, 32, dtype=np.float32))).astype(np.float32)
    ang = np.arange(TOK, dtype=np.float32)[:, None] * inv
    put("seq_cos", by_tile(np.cos(ang)))
    put("seq_sin", by_tile(np.sin(ang)))
    d = np.arange(896)[None] - 384 - p
    put("dist", np.abs(d))
    put("after", d >= 0)
    put("before", d <= 0)
    d = np.arange(640)[None] - 128 - p
    put("dist_f", CTX + d)
    put("dist_b", LAT - d)
    s, t = (p % 64)[:, :, None], np.arange(64)[None, None]
    sign = np.array([1, 1, -1, -1])[None, :, None]
    gap = (t - s) * sign
    put("mask", np.stack([gap > 0, gap >= 0], 2))
    pairs = (s // 2 == t // 2) & (gap > 0)
    put("first_t", pairs)
    put("level", np.stack([(s // (2 * m) == t // (2 * m)) & (s // m != t // m) & (gap > 0)
                           for m in LEVELS], 1))
    put("restart", (np.arange(TOK) % C != 0)[None])
    return [out for _, out in packs]


def build(nc, io):
    with ExitStack() as kernel_scope:
        Program(nc, io, kernel_scope).run()


class Count:

    def __init__(self, sem, step=1):
        self.sem, self.step, self.base = sem, step, 0

    def __add__(self, k):
        return self.base + self.step * k

    def advance(self, k):
        self.base += self.step * k


class Chain:

    def __init__(self, sem):
        self.sem, self.n = sem, 0

    def on(self, eng):
        def link(ins):
            self.n += 1
            ins.then_inc(self.sem, 1)
            eng.wait_ge(self.sem, self.n)
        return link


def spread(ap, axis, n):
    a = ap.unsqueeze(axis)
    shape = list(a.shape)
    shape[axis] = n
    return a.broadcast_to(shape)


class Program:
    def __init__(self, nc, io, scope):
        self.nc, self.io, self.scope = nc, io, scope
        self.counts, self.n_tensors = {}, 0
        self.dve_chain = Chain(scope.enter_context(nc.semaphore("dve_chain")))
        self.act_chain = Chain(scope.enter_context(nc.semaphore("act_chain")))
        sb = lambda name, shape: self.sbuf(scope, name, shape)
        self.base = sb("base", [P, BASE_N])
        self.cols = sb("cols", [P, COLS_N])
        self.rows = sb("rows", [P, ROWS_N])
        self.x = sb("x_tokens", [P, NT, D])
        self.cvec = sb("cvec", [P, KD, 2])
        self.silu_c = sb("silu_c", [P, KD, 2])
        self.mod = sb("mod", [P, 48, 2])
        self.scale1 = sb("scale1", [P, KD, 2])
        self.scale2 = sb("scale2", [P, KD, 2])
        self.gates = sb("gates", [P, 2, 2, D])
        self.stat = sb("stat", [P, 64])
        self.psum = scope.enter_context(nc.psum_tensor("psum", [P, 8, 512], F32))
        self.flat = self.psum[:, :, :].rearrange("p b n -> p (b n)")

    def sbuf(self, scope, name, shape):
        self.n_tensors += 1
        return scope.enter_context(self.nc.sbuf_tensor(f"{name}_{self.n_tensors}", shape, F32))

    def count(self, name, step=1):
        if name not in self.counts:
            self.counts[name] = Count(self.scope.enter_context(self.nc.semaphore(name)), step)
        return self.counts[name]

    def c(self, name):
        lo, hi = BASE[name]
        return self.base[:, lo:hi]

    def col(self, name):
        lo, hi = COLS[name]
        return self.cols[:, lo:hi]

    def row(self, name):
        lo, hi = ROWS[name]
        return self.rows[:, lo:hi]

    def run(self):
        self.load_inputs()
        for layer in range(DEPTH):
            last = layer == DEPTH - 1
            self.modulation(layer)
            tiles = list(range(CT if last else 0, NT))
            with ExitStack() as mixer_scope:
                self.mix_t = self.sbuf(mixer_scope, "mix_t", [P, KD, TOK])
                with ExitStack() as scope:
                    self.u_t = self.sbuf(scope, "u_t", [P, KD, TOK])
                    with ExitStack() as inner:
                        self.xn = self.sbuf(inner, "xn", [P, NT, D])
                        self.normalise(layer, "norm1", self.scale1, 0, list(range(NT)))
                    self.attention(layer, last)
                    self.retention(layer, last)
                    self.rwkv(layer, last)
                self.project_out(layer, last, tiles)
            with ExitStack() as scope:
                per_expert = CAP_L + (0 if last else CAP_C)
                self.slot = self.sbuf(scope, "slot", [P, NT, E_N])
                self.aff = self.sbuf(scope, "aff", [P, NT, E_N])
                self.chosen = self.sbuf(scope, "chosen_tokens", [P, E_N, KD, per_expert])
                with ExitStack() as loop_scope:
                    self.expert_w = self.sbuf(loop_scope, "expert_w", [P, W_SLOTS, KD, 512])
                    with ExitStack() as inner:
                        self.xn = self.sbuf(inner, "xn", [P, NT, D])
                        with ExitStack() as innermost:
                            self.u_t = self.sbuf(innermost, "h_t", [P, KD, TOK])
                            self.normalise(layer, "norm2", self.scale2, 24, tiles)
                            self.route(layer, last, tiles)
                        self.gather(layer, last)
                    self.y_lat = self.sbuf(loop_scope, "y_lat", [P, E_N // 2, D])
                    self.y_ctx = None if last else self.sbuf(loop_scope, "y_ctx", [P, E_N // 4, D])
                    with ExitStack() as inner:
                        self.experts(layer, last, inner)
                    self.combine(layer, last, tiles)
        self.store()

    def load_inputs(self):
        nc, io = self.nc, self.io
        landed, sig, done = self.count("inputs_landed", 16), self.count("silu_sigmoid"), self.count("silu_done")
        with nc.Block() as block:
            @block.sync
            def _(sp):
                sp.dma_start(self.cvec[:, :, :], io["cvec"]).then_inc(landed.sem, 16)
                sp.dma_start(self.base[:, :], io["base"]).then_inc(landed.sem, 16)
                sp.dma_start(self.x[:, 0:CT, :], io["ctx"].rearrange("(t p) d -> p t d", p=P)).then_inc(landed.sem, 16)
                sp.dma_start(self.x[:, CT:NT, :], io["x"].rearrange("(t p) d -> p t d", p=P)).then_inc(landed.sem, 16)
                sp.wait_ge(landed.sem, landed + 4)

            @block.scalar
            def _(act):
                act.wait_ge(landed.sem, landed + 4)
                act.activation(self.silu_c[:, :, :], self.cvec[:, :, :], ACT.Sigmoid).then_inc(sig.sem, 1)

            @block.vector
            def _(dve):
                dve.wait_ge(sig.sem, sig + 1)
                dve.tensor_tensor(self.silu_c[:, :, :], self.silu_c[:, :, :], self.cvec[:, :, :],
                                  ALU.mult).then_inc(done.sem, 1)

    def modulation(self, l):
        nc, io = self.nc, self.io
        small = self.count("layer_vectors_landed", 16)
        SLOTS, PARTS = 4, 12
        landed = [self.count(f"mod_w_landed{i}", 16) for i in range(SLOTS)]
        made, copied, turned = (self.count("mod_" + n) for n in ("made", "copied", "turned"))
        diag_ready, spread_done, gate_copied = (self.count(n) for n in ("gate_diag", "gate_spread", "gate_copied"))
        with ExitStack() as scope:
            w = self.sbuf(scope, "mod_w", [P, SLOTS, KD, 512])
            rows = self.sbuf(scope, "mod_rows", [2, PARTS, 512])
            diag = self.sbuf(scope, "gate_diagonals", [P, 2, 4, P])
            block = scope.enter_context(nc.Block())

            @block.sync
            def _(sp):
                for j in range(PARTS):
                    if j >= SLOTS:
                        sp.wait_ge(made.sem, made + (j - SLOTS + 1))
                    sp.dma_start(w[:, j % SLOTS, :, :], io["mod_w"][l, :, j * 512:(j + 1) * 512].rearrange("(k p) n -> p k n", p=P)
                                 ).then_inc(landed[j % SLOTS].sem, 16)
                    if j == SLOTS - 1:
                        sp.dma_start(self.cols[:, :], io["cols"][l]).then_inc(small.sem, 16)
                        sp.dma_start(self.rows[:, :], io["rows"][l]).then_inc(small.sem, 16)
                sp.wait_ge(small.sem, small + 2)

            @block.tensor
            def _(pe):
                for j in range(PARTS):
                    pe.wait_ge(landed[j % SLOTS].sem, landed[j % SLOTS] + (j // SLOTS + 1))
                    if j >= 2:
                        pe.wait_ge(copied.sem, copied + (j - 1))
                    for k in range(KD):
                        mm = pe.matmul(self.psum[0:2, 3 + j % 2, :], self.silu_c[:, k, :], w[:, j % SLOTS, k, :],
                                       start=(k == 0), stop=(k == KD - 1))
                    mm.then_inc(made.sem, 1)
                pe.wait_ge(copied.sem, copied + PARTS)
                for j in range(48):
                    mm = pe.transpose(self.flat[:, 2 * j:2 * j + 2], rows[:, j // 4, (j % 4) * P:(j % 4 + 1) * P],
                                      self.c("ident")[0:2, 0:2])
                mm.then_inc(turned.sem, 1)
                for n in range(8):
                    pe.wait_ge(diag_ready.sem, diag_ready + (n + 1))
                    if n >= 2:
                        pe.wait_ge(gate_copied.sem, gate_copied + (n - 1))
                    pe.matmul(self.psum[:, 1 + n % 2, :], self.c("ones"),
                              diag[:, n % 2, :, :].rearrange("p a b -> p (a b)"), start=True, stop=True
                              ).then_inc(spread_done.sem, 1)

            @block.scalar
            def _(act):
                for j in range(PARTS):
                    act.wait_ge(made.sem, made + (j + 1))
                    act.copy(rows[:, j, :], self.psum[0:2, 3 + j % 2, :]).then_inc(copied.sem, 1)
                for n in range(8):
                    g, s, half = n // 4, n // 2 % 2, n % 2
                    act.wait_ge(spread_done.sem, spread_done + (n + 1))
                    act.copy(self.gates[:, g, s, half * 512:(half + 1) * 512],
                             self.psum[:, 1 + n % 2, :]).then_inc(gate_copied.sem, 1)

            @block.vector
            def _(dve):
                link = self.dve_chain.on(dve)
                dve.wait_ge(small.sem, small + 2)
                dve.wait_ge(turned.sem, turned + 1)
                link(dve.tensor_tensor(self.mod[:, :, :], self.flat[:, 0:96].rearrange("p (j s) -> p j s", s=2),
                                       spread(self.col("mod_b"), 2, 2), ALU.add))
                for n in range(8):
                    g, s, half = n // 4, n // 2 % 2, n % 2
                    j = (16, 40)[g] + 4 * half
                    if n >= 2:
                        dve.wait_ge(spread_done.sem, spread_done + (n - 1))
                    dve.tensor_tensor(diag[:, n % 2, :, :], spread(self.c("ident"), 1, 4),
                                      spread(self.mod[:, j:j + 4, s], 2, P), ALU.mult).then_inc(diag_ready.sem, 1)
                for scale, j, name in ((self.scale1, 8, "norm1"), (self.scale2, 32, "norm2")):
                    link(dve.tensor_scalar(scale[:, :, :], self.mod[:, j:j + 8, :], 1.0, None, ALU.add))
                    link(dve.tensor_tensor(scale[:, :, :], scale[:, :, :], spread(self.col(name), 2, 2), ALU.mult))
        small.advance(2)
        made.advance(PARTS)
        copied.advance(PARTS)
        turned.advance(1)
        for slot in landed:
            slot.advance(PARTS // SLOTS)
        for s in (diag_ready, spread_done, gate_copied):
            s.advance(8)

    def normalise(self, l, name, scale, shift, tiles):
        nc = self.nc
        squares, mean, root, normed = (self.count(f"norm_{n}") for n in ("squares", "mean", "root", "rows"))
        turned, modulated = self.count("norm_turned"), self.count("norm_modulated")
        n = len(tiles)
        ss, rs = self.stat[:, 0:NT], self.stat[:, 8:8 + NT]
        groups = [(1, [t for t in tiles if t < CT]), (0, [t for t in tiles if t >= CT])]
        items = [(k, s, ts) for k in range(KD) for s, ts in groups if ts]
        with ExitStack() as scope:
            junk = self.sbuf(scope, "squares", [P, D])
            block = scope.enter_context(nc.Block())

            @block.scalar
            def _(act):
                for t in tiles:
                    self.act_chain.on(act)(act.activation(junk[:, :], self.x[:, t, :], ACT.Square,
                                                          accum_out=ss[:, t:t + 1]))
                act.copy(junk[:, 0:1], junk[:, 1:2]).then_inc(squares.sem, 1)
                act.wait_ge(mean.sem, mean + 1)
                act.activation(rs[:, tiles[0]:NT], ss[:, tiles[0]:NT], ACT.Sqrt).then_inc(root.sem, 1)
                for i, (k, s, ts) in enumerate(items):
                    if i % 2:
                        act.wait_ge(turned.sem, turned + (i + 1))
                        act.activation(self.u_t[:, k, ts[0] * P:(ts[-1] + 1) * P], self.psum[:, i % 4, 0:len(ts) * P],
                                       ACT.Identity, bias=self.mod[:, shift + k, s:s + 1],
                                       scale=scale[:, k, s:s + 1]).then_inc(modulated.sem, 1)
                    else:
                        act.wait_ge(modulated.sem, modulated + (i + 1))

            @block.vector
            def _(dve):
                link = self.dve_chain.on(dve)
                dve.wait_ge(squares.sem, squares + 1)
                dve.tensor_scalar(ss[:, tiles[0]:NT], ss[:, tiles[0]:NT], 1.0 / D, EPS, ALU.mult, ALU.add
                                  ).then_inc(mean.sem, 1)
                dve.wait_ge(root.sem, root + 1)
                link(dve.reciprocal(rs[:, tiles[0]:NT], rs[:, tiles[0]:NT]))
                for t in tiles:
                    dve.tensor_scalar(self.xn[:, t, :], self.x[:, t, :], rs[:, t:t + 1], None,
                                      ALU.mult).then_inc(normed.sem, 1)
                for i, (k, s, ts) in enumerate(items):
                    if i % 2 == 0:
                        dve.wait_ge(turned.sem, turned + (i + 1))
                        if i:
                            dve.wait_ge(modulated.sem, modulated + i)
                        dve.tensor_scalar(self.u_t[:, k, ts[0] * P:(ts[-1] + 1) * P], self.psum[:, i % 4, 0:len(ts) * P],
                                          scale[:, k, s:s + 1], self.mod[:, shift + k, s:s + 1],
                                          ALU.mult, ALU.add).then_inc(modulated.sem, 1)

            @block.tensor
            def _(pe):
                pe.wait_ge(normed.sem, normed + n)
                for i, (k, s, ts) in enumerate(items):
                    if i >= 4:
                        pe.wait_ge(modulated.sem, modulated + (i - 3))
                    for a, t in enumerate(ts):
                        mm = pe.transpose(self.psum[:, i % 4, a * P:(a + 1) * P], self.xn[:, t, k * P:(k + 1) * P],
                                          self.c("ident"))
                    mm.then_inc(turned.sem, 1)
        squares.advance(1)
        mean.advance(1)
        root.advance(1)
        normed.advance(n)
        turned.advance(len(items))
        modulated.advance(len(items))

    def attention(self, l, last):
        nc, io = self.nc, self.io
        landed = self.count("mla_weights_landed", 16)
        names = ("projected", "squares", "mean", "root", "latents", "latents_turned", "latents_t", "heads_made",
                 "heads_copied", "head_mean", "head_root", "heads_normed", "heads_turned", "heads_t")
        s = {n: self.count("mla_" + n) for n in names}
        with ExitStack() as att_scope:
            sb = lambda name, shape: self.sbuf(att_scope, name, shape)
            q_t, k_t = sb("q_t", [QK, HEADS, TOK]), sb("k_t", [QK, HEADS, TOK])
            v = sb("v", [P, NT, HEADS, VD])
            with ExitStack() as scope:
                sb = lambda name, shape: self.sbuf(scope, name, shape)
                w = sb("w_mla", [P, KD, MLA_COLS])
                spare = self.mix_t[:, :, :].rearrange("p k n -> p (k n)")
                wq = spare[:, 0:3 * 768].rearrange("p (k n) -> p k n", k=3)
                wkv = spare[:, 2304:2304 + 2048].rearrange("p (k n) -> p k n", k=2)
                junk, lat = sb("mla_junk", [P, QR]), sb("latents", [P, MLA_COLS])
                lat_t = sb("latents_t", [P, 5, P])
                qk = sb("qk_rows", [P, 2, HEADS, QK])
                sq = sb("qk_squares", [P, 2, HEADS, QK])
                turn = sb("rope_parts", [P, 4, 2 * HEADS, 16])
                st = self.stat
                block = scope.enter_context(nc.Block())
                pa, pt = self.flat[:, 0:MLA_COLS], self.flat[:, 1024:1024 + 640]
                pq, pkv = self.flat[:, 2048:2048 + 768], self.flat[:, 3072:4096].rearrange("p (h d) -> p h d", h=HEADS)
                ph = self.psum[0:QK, 4:8, :].rearrange("p b (a n) -> p (b a) n", n=P)

                @block.sync
                def _(sp):
                    sp.dma_start(w[:, :, :], io["w_in"][l, :, 0:MLA_COLS].rearrange("(k p) n -> p k n", p=P)).then_inc(landed.sem, 16)
                    sp.dma_start(wq, io["mla_w_uq"][l].rearrange("(k p) n -> p k n", p=P)).then_inc(landed.sem, 16)
                    sp.dma_start(wkv, io["mla_w_ukv"][l].rearrange("(k p) n -> p k n", p=P)).then_inc(landed.sem, 16)

                @block.tensor
                def _(pe):
                    def project(t):
                        if t >= 1:
                            pe.wait_ge(s["latents"].sem, s["latents"] + t)
                        for lo, hi in ((0, 512), (512, MLA_COLS)):
                            for k in range(KD):
                                mm = pe.matmul(pa[:, lo:hi], self.u_t[:, k, t * P:(t + 1) * P], w[:, k, lo:hi],
                                               start=(k == 0), stop=(k == KD - 1))
                        mm.then_inc(s["projected"].sem, 1)

                    pe.wait_ge(landed.sem, landed + 3)
                    project(0)
                    for t in range(NT):
                        pe.wait_ge(s["latents"].sem, s["latents"] + (t + 1))
                        for a in range(5):
                            mm = pe.transpose(pt[:, a * P:(a + 1) * P], lat[:, a * P:(a + 1) * P], self.c("ident"))
                        mm.then_inc(s["latents_turned"].sem, 1)
                        if t + 1 < NT:
                            project(t + 1)
                        pe.wait_ge(s["latents_t"].sem, s["latents_t"] + (t + 1))
                        if t >= 1:
                            pe.wait_ge(s["heads_t"].sem, s["heads_t"] + 2 * t)
                        for lo, hi in ((0, 512), (512, 768)):
                            for k in range(3):
                                pe.matmul(pq[:, lo:hi], lat_t[:, k, :], wq[:, k, lo:hi], start=(k == 0), stop=(k == 2))
                        for b in range(2):
                            for k in range(2):
                                mm = pe.matmul(self.psum[:, 6 + b, :], lat_t[:, 3 + k, :], wkv[:, k, b * 512:(b + 1) * 512],
                                               start=(k == 0), stop=(k == 1))
                        mm.then_inc(s["heads_made"].sem, 1)
                        pe.wait_ge(s["heads_normed"].sem, s["heads_normed"] + (t + 1))
                        for a in range(2):
                            for h in range(HEADS):
                                mm = pe.transpose(ph[:, a * HEADS + h, :], qk[:, a, h, :], self.c("ident"))
                            mm.then_inc(s["heads_turned"].sem, 1)

                @block.scalar
                def _(act):
                    link = self.act_chain.on(act)
                    for t in range(NT):
                        act.wait_ge(s["projected"].sem, s["projected"] + (t + 1))
                        link(act.activation(junk[:, 0:QR], pa[:, 0:QR], ACT.Square, accum_out=st[:, 0:1]))
                        link(act.activation(junk[:, 0:KVR], pa[:, QR:QR + KVR], ACT.Square, accum_out=st[:, 1:2]))
                        act.copy(junk[:, 0:1], junk[:, 1:2]).then_inc(s["squares"].sem, 1)
                        act.wait_ge(s["mean"].sem, s["mean"] + (t + 1))
                        act.activation(st[:, 4:6], st[:, 2:4], ACT.Sqrt).then_inc(s["root"].sem, 1)
                        act.wait_ge(s["heads_made"].sem, s["heads_made"] + (t + 1))
                        if t >= 1:
                            act.wait_ge(s["heads_turned"].sem, s["heads_turned"] + 2 * t)
                        act.copy(qk[:, 0, :, :].rearrange("p h d -> p (h d)"), pq)
                        act.copy(qk[:, 1, :, 0:NOPE], pkv[:, :, 0:NOPE])
                        act.copy(v[:, t, :, :], pkv[:, :, NOPE:NOPE + VD]).then_inc(s["heads_copied"].sem, 1)
                        act.wait_ge(s["head_mean"].sem, s["head_mean"] + (t + 1))
                        act.activation(st[:, 32:48], st[:, 16:32], ACT.Sqrt).then_inc(s["head_root"].sem, 1)
                        act.wait_ge(s["heads_turned"].sem, s["heads_turned"] + (2 * t + 1))
                        act.copy(q_t[:, :, t * P:(t + 1) * P], ph[:, 0:HEADS, :]).then_inc(s["heads_t"].sem, 1)

                @block.vector
                def _(dve):
                    link = self.dve_chain.on(dve)
                    for t in range(NT):
                        dve.wait_ge(s["squares"].sem, s["squares"] + (t + 1))
                        link(dve.tensor_scalar(st[:, 2:3], st[:, 0:1], 1.0 / QR, EPS, ALU.mult, ALU.add))
                        dve.tensor_scalar(st[:, 3:4], st[:, 1:2], 1.0 / KVR, EPS, ALU.mult, ALU.add).then_inc(s["mean"].sem, 1)
                        dve.wait_ge(s["root"].sem, s["root"] + (t + 1))
                        link(dve.reciprocal(st[:, 6:8], st[:, 4:6]))
                        link(dve.tensor_scalar(lat[:, 0:QR], pa[:, 0:QR], st[:, 6:7], None, ALU.mult))
                        link(dve.tensor_scalar(lat[:, QR:640], pa[:, QR:640], st[:, 7:8], None, ALU.mult))
                        dve.tensor_copy(lat[:, 640:MLA_COLS], pa[:, 640:MLA_COLS]).then_inc(s["latents"].sem, 1)
                        dve.wait_ge(s["latents_turned"].sem, s["latents_turned"] + (t + 1))
                        dve.tensor_tensor(lat_t[:, :, :], pt.rearrange("p (a n) -> p a n", n=P),
                                          spread(self.col("cn"), 2, P), ALU.mult).then_inc(s["latents_t"].sem, 1)
                        if t >= 1:
                            dve.wait_ge(s["heads_turned"].sem, s["heads_turned"] + 2 * t)
                        dve.wait_ge(s["latents"].sem, s["latents"] + (t + 1))
                        link(dve.tensor_copy(qk[:, 1, :, NOPE:QK], spread(lat[:, 640:MLA_COLS], 1, HEADS)))
                        dve.wait_ge(s["heads_copied"].sem, s["heads_copied"] + (t + 1))
                        rows = qk[:, :, :, :].rearrange("p a h d -> p (a h) d")
                        link(dve.tensor_tensor(sq[:, :, :, :], qk[:, :, :, :], qk[:, :, :, :], ALU.mult))
                        link(dve.tensor_reduce(st[:, 16:32], sq[:, :, :, :].rearrange("p a h d -> p (a h) d"), AX, ALU.add))
                        dve.tensor_scalar(st[:, 16:32], st[:, 16:32], 1.0 / QK, EPS, ALU.mult, ALU.add).then_inc(s["head_mean"].sem, 1)
                        dve.wait_ge(s["head_root"].sem, s["head_root"] + (t + 1))
                        link(dve.reciprocal(st[:, 48:64], st[:, 32:48]))
                        link(dve.tensor_tensor(rows, rows, spread(st[:, 48:64], 2, QK), ALU.mult))
                        gain = spread(self.row("qk_gain").rearrange("p (a d) -> p a d", a=2), 2, HEADS)
                        link(dve.tensor_tensor(qk[:, :, :, :], qk[:, :, :, :], gain, ALU.mult))
                        if t >= CT:
                            at = (t - CT) * 16
                            cos = spread(self.c("axial_cos")[:, at:at + 16], 1, 2 * HEADS)
                            sin = spread(self.c("axial_sin")[:, at:at + 16], 1, 2 * HEADS)
                            x1, x2 = rows[:, :, NOPE:NOPE + 16], rows[:, :, NOPE + 16:QK]
                            link(dve.tensor_tensor(turn[:, 0], x1, cos, ALU.mult))
                            link(dve.tensor_tensor(turn[:, 1], x2, sin, ALU.mult))
                            link(dve.tensor_tensor(turn[:, 2], x1, sin, ALU.mult))
                            link(dve.tensor_tensor(turn[:, 3], x2, cos, ALU.mult))
                            link(dve.tensor_tensor(x1, turn[:, 0], turn[:, 1], ALU.subtract))
                            dve.tensor_tensor(x2, turn[:, 2], turn[:, 3], ALU.add).then_inc(s["heads_normed"].sem, 1)
                        else:
                            dve.tensor_copy(turn[:, 0, 0, 0:1], rows[:, 0, 0:1]).then_inc(s["heads_normed"].sem, 1)
                        dve.wait_ge(s["heads_turned"].sem, s["heads_turned"] + (2 * t + 2))
                        dve.tensor_copy(k_t[:, :, t * P:(t + 1) * P], ph[:, HEADS:2 * HEADS, :]).then_inc(s["heads_t"].sem, 1)
            landed.advance(3)
            for n in names:
                s[n].advance(2 * NT if n in ("heads_turned", "heads_t") else NT)
            self.attend(l, last, q_t, k_t, v)

    def attend(self, l, last, q_t, k_t, v):
        nc = self.nc
        names = ("scores", "max", "exp", "turned", "probs_t", "values", "outs", "out_turned", "out_t")
        s = {n: self.count("att_" + n) for n in names}
        tiles = list(range(CT if last else 0, NT))
        items = [(h, t) for h in range(HEADS) for t in tiles]
        n_items = len(items)
        keys = [CT if t < CT else NT for _, t in items]
        with ExitStack() as scope:
            sb = lambda name, shape: self.sbuf(scope, name, shape)
            probs, probs_t = sb("probs", [P, 2, TOK]), sb("probs_t", [P, 2, NT, P])
            outs = sb("attended", [P, NT, HEADS * VD])
            stat = sb("softmax_stat", [P, 4, 4])
            block = scope.enter_context(nc.Block())
            scale = float(QK) ** -0.5
            score = lambda i: self.flat[:, 1024 * (i % 2):1024 * (i % 2) + TOK]
            turned = self.flat[:, 2048:2048 + TOK].rearrange("p (a n) -> p a n", n=P)

            @block.tensor
            def _(pe):
                def scores(i):
                    h, t = items[i]
                    if i >= 2:
                        pe.wait_ge(s["exp"].sem, s["exp"] + (i - 1))
                    for lo in range(0, keys[i] * P, 512):
                        hi = min(lo + 512, keys[i] * P)
                        mm = pe.matmul(score(i)[:, lo:hi], q_t[:, h, t * P:(t + 1) * P], k_t[:, h, lo:hi],
                                       start=True, stop=True)
                    mm.then_inc(s["scores"].sem, 1)

                def turn(i):
                    pe.wait_ge(s["exp"].sem, s["exp"] + (i + 1))
                    if i >= 1:
                        pe.wait_ge(s["probs_t"].sem, s["probs_t"] + i)
                    for k in range(keys[i]):
                        mm = pe.transpose(turned[:, k, :], probs[:, i % 2, k * P:(k + 1) * P], self.c("ident"))
                    mm.then_inc(s["turned"].sem, 1)

                def values(i):
                    h, t = items[i]
                    pe.wait_ge(s["probs_t"].sem, s["probs_t"] + (i + 1))
                    if i >= 2:
                        pe.wait_ge(s["outs"].sem, s["outs"] + (i - 1))
                    for k in range(keys[i]):
                        mm = pe.matmul(self.psum[:, 6 + i % 2, 0:VD], probs_t[:, i % 2, k, :], v[:, k, h, :],
                                       start=(k == 0), stop=(k == keys[i] - 1))
                    mm.then_inc(s["values"].sem, 1)

                for i in range(n_items + 2):
                    if i < n_items:
                        scores(i)
                    if 1 <= i <= n_items:
                        turn(i - 1)
                    if i >= 2:
                        values(i - 2)
                pe.wait_ge(s["outs"].sem, s["outs"] + n_items)
                for n, t in enumerate(tiles):
                    if n >= 2:
                        pe.wait_ge(s["out_t"].sem, s["out_t"] + (n - 1))
                    for a in range(4):
                        mm = pe.transpose(self.psum[:, n % 2, a * P:(a + 1) * P], outs[:, t, a * P:(a + 1) * P], self.c("ident"))
                    mm.then_inc(s["out_turned"].sem, 1)

            @block.scalar
            def _(act):
                for i in range(n_items):
                    act.wait_ge(s["max"].sem, s["max"] + (i + 1))
                    if i >= 2:
                        act.wait_ge(s["turned"].sem, s["turned"] + (i - 1))
                    n = keys[i] * P
                    act.activation(probs[:, i % 2, 0:n], score(i)[:, 0:n], ACT.Exp, bias=stat[:, i % 4, 1:2],
                                   scale=scale, accum_out=stat[:, i % 4, 2:3]).then_inc(s["exp"].sem, 1)
                for n, t in enumerate(tiles):
                    act.wait_ge(s["out_turned"].sem, s["out_turned"] + (n + 1))
                    act.copy(self.mix_t[:, 0:4, t * P:(t + 1) * P],
                             self.psum[:, n % 2, :].rearrange("p (a n) -> p a n", n=P)).then_inc(s["out_t"].sem, 1)

            @block.vector
            def _(dve):
                link = self.dve_chain.on(dve)
                for i in range(n_items + 2):
                    if i < n_items:
                        dve.wait_ge(s["scores"].sem, s["scores"] + (i + 1))
                        link(dve.tensor_reduce(stat[:, i % 4, 0:1], score(i)[:, 0:keys[i] * P], AX, ALU.max))
                        dve.tensor_scalar(stat[:, i % 4, 1:2], stat[:, i % 4, 0:1], -scale, None, ALU.mult).then_inc(s["max"].sem, 1)
                    if 1 <= i <= n_items:
                        j = i - 1
                        dve.wait_ge(s["turned"].sem, s["turned"] + (j + 1))
                        if j >= 2:
                            dve.wait_ge(s["values"].sem, s["values"] + (j - 1))
                        dve.tensor_copy(probs_t[:, j % 2, 0:keys[j], :], turned[:, 0:keys[j], :]).then_inc(s["probs_t"].sem, 1)
                    if i >= 2:
                        j = i - 2
                        h, t = items[j]
                        dve.wait_ge(s["values"].sem, s["values"] + (j + 1))
                        link(dve.reciprocal(stat[:, j % 4, 3:4], stat[:, j % 4, 2:3]))
                        dve.tensor_scalar(outs[:, t, h * VD:(h + 1) * VD], self.psum[:, 6 + j % 2, 0:VD],
                                          stat[:, j % 4, 3:4], None, ALU.mult).then_inc(s["outs"].sem, 1)
        for n in names:
            s[n].advance(len(tiles) if n.startswith("out_") else n_items)

    def retention(self, l, last):
        nc, io = self.nc, self.io
        landed = self.count("ret_weights_landed", 16)
        tiles = list(range(CT if last else 0, NT))
        names = ("projected", "rotated", "v_copied", "gate", "gated", "turned", "turned_t", "rows_read",
                 "decay_exp", "decay_ln", "log_decay", "powers", "strips",
                 "scores", "weighted", "head_done", "var", "root", "normed", "out_turned", "out_t")
        s = {n: self.count("ret_" + n) for n in names}
        n_scores = HEADS // 2 * NT
        with ExitStack() as scope:
            sb = lambda name, shape: self.sbuf(scope, name, shape)
            cst = sb("ret_const", [P, RETC_N])
            cc = lambda n: cst[:, RETC[n][0]:RETC[n][1]]
            w = sb("w_ret", [P, KD, RET_COLS])
            qk = sb("ret_qk", [P, 2, 8, 64])
            turn = sb("ret_turn", [P, 4, 8, 32])
            v, g = sb("ret_v", [P, NT, 256]), sb("ret_gate", [P, NT, 256])
            qk_t = sb("ret_qk_t", [P, 4, TOK])
            strip_a, strip_b = sb("strip_a", [P, 896]), sb("strip_b", [P, 640])
            part_a, part_b = sb("part_a", [P, 896]), sb("part_b", [P, 640])
            spare = w[:, :, :].rearrange("p k n -> p (k n)")
            att = spare[:, 0:NT * 512].rearrange("p (t n) -> p t n", t=NT)
            att_c = spare[:, 3072:3072 + CT * 256].rearrange("p (t n) -> p t n", t=CT)
            out = spare[:, 4096:4096 + NT * 256].rearrange("p (t n) -> p t n", t=NT)
            dec = sb("ret_decay", [P, 4, 8])
            st = sb("ret_stat", [P, 4, 24])
            block = scope.enter_context(nc.Block())
            proj = lambda t: self.flat[:, 1024 * (t % 2):1024 * (t % 2) + 1024]
            o = self.flat[:, 2048 + 512:2048 + 512 + NT * 256].rearrange("p (t n) -> p t n", t=NT)

            @block.sync
            def _(sp):
                sp.dma_start(cst[:, :], io["retc"]).then_inc(landed.sem, 16)
                sp.dma_start(w[:, :, :], io["w_in"][l, :, MLA_COLS:MLA_COLS + RET_COLS].rearrange("(k p) n -> p k n", p=P)).then_inc(landed.sem, 16)

            @block.tensor
            def _(pe):
                pe.wait_ge(landed.sem, landed + 2)

                def turn_tile(t):
                    pe.wait_ge(s["rotated"].sem, s["rotated"] + (t + 1))
                    if t >= 1:
                        pe.wait_ge(s["turned_t"].sem, s["turned_t"] + t)
                    for a in range(4):
                        mm = pe.transpose(self.psum[:, 4, a * P:(a + 1) * P],
                                          qk[:, t % 2, 2 * a:2 * a + 2, :].rearrange("p a d -> p (a d)"), self.c("ident"))
                    mm.then_inc(s["turned"].sem, 1)

                for t in range(NT):
                    if t >= 2:
                        pe.wait_ge(s["rotated"].sem, s["rotated"] + (t - 1))
                        pe.wait_ge(s["gated"].sem, s["gated"] + (t - 1))
                        pe.wait_ge(s["v_copied"].sem, s["v_copied"] + (t - 1))
                    for b in range(2):
                        for k in range(KD):
                            mm = pe.matmul(proj(t)[:, b * 512:(b + 1) * 512], self.u_t[:, k, t * P:(t + 1) * P],
                                           w[:, k, b * 512:(b + 1) * 512], start=(k == 0), stop=(k == KD - 1))
                    mm.then_inc(s["projected"].sem, 1)
                    if t >= 1:
                        turn_tile(t - 1)
                turn_tile(NT - 1)
                pe.wait_ge(s["turned_t"].sem, s["turned_t"] + NT)
                pe.wait_ge(s["gated"].sem, s["gated"] + NT)
                pe.wait_ge(s["v_copied"].sem, s["v_copied"] + NT)
                n = 0
                for h in range(4):
                    lo, f = 64 * (h % 2), h // 2
                    for j in range(NT):
                        if n >= 2:
                            pe.wait_ge(s["weighted"].sem, s["weighted"] + (n - 1))
                        key = qk_t[lo:lo + 64, 2 + f, j * P:(j + 1) * P]
                        if j < CT and not last:
                            pe.matmul(proj(n)[:, 0:CTX], key, qk_t[lo:lo + 64, f, 0:CTX], start=True, stop=True)
                        pe.matmul(proj(n)[:, 512:1024], key, qk_t[lo:lo + 64, f, CTX:TOK], start=True, stop=True
                                  ).then_inc(s["scores"].sem, 1)
                        n += 1
                    pe.wait_ge(s["weighted"].sem, s["weighted"] + n)
                    for t in tiles:
                        keys = list(range(CT if t < CT else NT))
                        for j in keys:
                            a = att_c[:, j, t * P:(t + 1) * P] if t < CT else att[:, j, (t - CT) * P:(t - CT + 1) * P]
                            mm = pe.matmul(o[:, t, h * 64:(h + 1) * 64], a, v[:, j, h * 64:(h + 1) * 64],
                                           start=(j == keys[0]), stop=(j == keys[-1]))
                    mm.then_inc(s["head_done"].sem, 1)
                pe.wait_ge(s["normed"].sem, s["normed"] + 1)
                for n, t in enumerate(tiles):
                    if n >= 2:
                        pe.wait_ge(s["out_t"].sem, s["out_t"] + (n - 1))
                    for a in range(2):
                        mm = pe.transpose(self.psum[:, n % 2, a * P:(a + 1) * P], out[:, t, a * P:(a + 1) * P], self.c("ident"))
                    mm.then_inc(s["out_turned"].sem, 1)

            @block.scalar
            def _(act):
                link = self.act_chain.on(act)
                for t in range(NT):
                    act.wait_ge(s["projected"].sem, s["projected"] + (t + 1))
                    act.copy(v[:, t, :], proj(t)[:, 512:768]).then_inc(s["v_copied"].sem, 1)
                    act.activation(g[:, t, :], proj(t)[:, 768:1024], ACT.Sigmoid).then_inc(s["gate"].sem, 1)
                act.wait_ge(s["log_decay"].sem, s["log_decay"] + 1)
                act.activation(dec[:, 1, :], dec[:, 0, :], ACT.Exp, scale=-1.0).then_inc(s["decay_exp"].sem, 1)
                act.wait_ge(s["decay_exp"].sem, s["decay_exp"] + 1)
                act.activation(dec[:, 2, :], dec[:, 1, :], ACT.Ln, bias=1.0).then_inc(s["decay_ln"].sem, 1)
                act.wait_ge(s["log_decay"].sem, s["log_decay"] + 2)
                for h in range(4):
                    if h >= 1:
                        act.wait_ge(s["strips"].sem, s["strips"] + h)
                        act.wait_ge(s["weighted"].sem, s["weighted"] + h * NT)
                    f, b = dec[:, 3, h:h + 1], dec[:, 3, 4 + h:5 + h]
                    act.activation(strip_a[:, :], cc("dist"), ACT.Exp, scale=f)
                    act.activation(part_a[:, :], cc("dist"), ACT.Exp, scale=b)
                    act.activation(strip_b[:, :], cc("dist_f"), ACT.Exp, scale=f)
                    act.activation(part_b[:, :], cc("dist_b"), ACT.Exp, scale=b).then_inc(s["powers"].sem, 1)
                act.wait_ge(s["var"].sem, s["var"] + 1)
                act.activation(st[:, 2, :], st[:, 1, :], ACT.Sqrt).then_inc(s["root"].sem, 1)
                for n, t in enumerate(tiles):
                    act.wait_ge(s["out_turned"].sem, s["out_turned"] + (n + 1))
                    act.copy(self.mix_t[:, 4:6, t * P:(t + 1) * P],
                             self.psum[:, n % 2, 0:256].rearrange("p (a n) -> p a n", n=P)).then_inc(s["out_t"].sem, 1)

            @block.vector
            def _(dve):
                link = self.dve_chain.on(dve)
                dve.wait_ge(landed.sem, landed + 2)
                link(dve.tensor_scalar(dec[:, 3, :], self.row("decay"), -1.0, None, ALU.mult))
                dve.tensor_tensor(dec[:, 0, :], dec[:, 3, :], self.row("decay"), ALU.max).then_inc(s["log_decay"].sem, 1)
                for t in range(NT):
                    dve.wait_ge(s["projected"].sem, s["projected"] + (t + 1))
                    rows = proj(t)[:, 0:512].rearrange("p (a d) -> p a d", d=64)
                    x1, x2 = rows[:, :, 0:32], rows[:, :, 32:64]
                    cos = spread(cc("seq_cos")[:, t * 32:(t + 1) * 32], 1, 8)
                    sin = spread(cc("seq_sin")[:, t * 32:(t + 1) * 32], 1, 8)
                    link(dve.tensor_tensor(turn[:, 0], x1, cos, ALU.mult))
                    link(dve.tensor_tensor(turn[:, 1], x2, sin, ALU.mult))
                    link(dve.tensor_tensor(turn[:, 2], x1, sin, ALU.mult))
                    link(dve.tensor_tensor(turn[:, 3], x2, cos, ALU.mult))
                    if t >= 2:
                        dve.wait_ge(s["turned"].sem, s["turned"] + (t - 1))
                    link(dve.tensor_tensor(qk[:, t % 2, :, 0:32], turn[:, 0], turn[:, 1], ALU.subtract))
                    dve.tensor_tensor(qk[:, t % 2, :, 32:64], turn[:, 2], turn[:, 3], ALU.add).then_inc(s["rotated"].sem, 1)
                    dve.wait_ge(s["gate"].sem, s["gate"] + (t + 1))
                    dve.tensor_tensor(g[:, t, :], g[:, t, :], proj(t)[:, 768:1024], ALU.mult).then_inc(s["gated"].sem, 1)
                    dve.wait_ge(s["turned"].sem, s["turned"] + (t + 1))
                    dve.tensor_copy(qk_t[:, :, t * P:(t + 1) * P],
                                    self.psum[:, 4, :].rearrange("p (a n) -> p a n", n=P)).then_inc(s["turned_t"].sem, 1)
                dve.wait_ge(s["decay_ln"].sem, s["decay_ln"] + 1)
                link(dve.tensor_scalar(dec[:, 3, :], self.row("decay"), 0.0, None, ALU.min))
                dve.tensor_tensor(dec[:, 3, :], dec[:, 3, :], dec[:, 2, :], ALU.subtract).then_inc(s["log_decay"].sem, 1)
                n = 0
                for h in range(4):
                    dve.wait_ge(s["powers"].sem, s["powers"] + (h + 1))
                    link(dve.tensor_tensor(strip_a[:, :], strip_a[:, :], cc("after"), ALU.mult))
                    link(dve.tensor_tensor(part_a[:, :], part_a[:, :], cc("before"), ALU.mult))
                    link(dve.tensor_tensor(strip_a[:, :], strip_a[:, :], part_a[:, :], ALU.add))
                    dve.tensor_tensor(strip_b[:, :], strip_b[:, :], part_b[:, :], ALU.add).then_inc(s["strips"].sem, 1)
                    dve.wait_ge(s["strips"].sem, s["strips"] + (h + 1))
                    if h >= 1:
                        dve.wait_ge(s["head_done"].sem, s["head_done"] + h)
                    for j in range(NT):
                        dve.wait_ge(s["scores"].sem, s["scores"] + (n + 1))
                        if j < CT:
                            if not last:
                                dve.scalar_tensor_tensor(att_c[:, j, :], proj(n)[:, 0:CTX], 0.125,
                                                         strip_a[:, 384 - j * P:384 - j * P + CTX], ALU.mult, ALU.mult)
                            strip = strip_b[:, P - j * P:P - j * P + LAT]
                        else:
                            strip = strip_a[:, 384 - (j - CT) * P:384 - (j - CT) * P + LAT]
                        dve.scalar_tensor_tensor(att[:, j, :], proj(n)[:, 512:1024], 0.125, strip,
                                                 ALU.mult, ALU.mult).then_inc(s["weighted"].sem, 1)
                        n += 1
                dve.wait_ge(s["head_done"].sem, s["head_done"] + 4)
                lo = tiles[0]
                rows = lambda a: a.rearrange("p t (h d) -> p (t h) d", d=64)
                src, dst = rows(o[:, lo:NT, :]), rows(out[:, lo:NT, :])
                a, b = lo * 4, NT * 4
                link(dve.memset(st[:, :, :], 1.0))
                link(dve.tensor_reduce(st[:, 0, a:b], src, AX, ALU.add))
                link(dve.tensor_scalar(st[:, 0, a:b], st[:, 0, a:b], 1.0 / 64, None, ALU.mult))
                link(dve.tensor_tensor(dst, src, spread(st[:, 0, a:b], 2, 64), ALU.subtract))
                sq = att[:, 0:3, :].rearrange("p a b -> p (a b)")[:, 0:(b - a) * 64].rearrange("p (r d) -> p r d", d=64)
                link(dve.tensor_tensor(sq, dst, dst, ALU.mult))
                link(dve.tensor_reduce(st[:, 1, a:b], sq, AX, ALU.add))
                dve.tensor_scalar(st[:, 1, a:b], st[:, 1, a:b], 1.0 / 64, 1e-5, ALU.mult, ALU.add).then_inc(s["var"].sem, 1)
                dve.wait_ge(s["root"].sem, s["root"] + 1)
                link(dve.reciprocal(st[:, 3, a:b], st[:, 2, a:b]))
                link(dve.tensor_tensor(dst, dst, spread(st[:, 3, a:b], 2, 64), ALU.mult))
                link(dve.tensor_tensor(out[:, lo:NT, :], out[:, lo:NT, :], spread(self.row("gn_w"), 1, NT - lo), ALU.mult))
                dve.tensor_tensor(out[:, lo:NT, :], out[:, lo:NT, :], g[:, lo:NT, :], ALU.mult).then_inc(s["normed"].sem, 1)
        landed.advance(2)
        once = {"decay_exp": 1, "decay_ln": 1, "log_decay": 2, "powers": 4, "strips": 4, "head_done": 4, "var": 1,
                "root": 1, "normed": 1, "scores": n_scores, "weighted": n_scores,
                "out_turned": len(tiles), "out_t": len(tiles)}
        for n in names:
            s[n].advance(once.get(n, NT))

    def rwkv(self, l, last):
        with ExitStack() as scope:
            sb = lambda name, shape: self.sbuf(scope, name, shape)
            cst = sb("rwkv_const", [P, RWKVC_N])
            self.cc = lambda n: cst[:, RWKVC[n][0]:RWKVC[n][1]]
            g, bonus = sb("rwkv_g", [P, 2, TOK]), sb("rwkv_bonus", [P, 2, TOK])
            v = sb("rwkv_v", [P, 2, TOK])
            queries = self.u_t[:, :, :].rearrange("p k n -> p (k n)").rearrange("p (q c a t) -> p q c a t", q=4, c=NCH, a=2)
            updates = sb("updates", [P, 4, NCH, 2, C])
            half = sb("half_decay", [P, 4, NCH])
            self.rwkv_features(l, cst, g, bonus, v, queries, updates, half)
            self.rwkv_chunks(l, last, g, bonus, v, queries, updates, half)

    def rwkv_features(self, l, cst, g, bonus, v, queries, updates, half):
        nc, io, cc = self.nc, self.io, self.cc
        landed = self.count("rwkv_weights_landed", 16)
        names = ("projected", "tile_read", "shifted", "wide", "wide_act", "wide_read", "table", "root",
                 "decay_exp", "decay_in")
        s = {n: self.count("rwkv_" + n) for n in names}
        order = (7, 8, 6, 0, 1, 2, 3, 4, 5)
        at = [(n * P, P) for n in range(7)] + [(896, 64), (960, P)]
        with ExitStack() as scope:
            sb = lambda name, shape: self.sbuf(scope, name, shape)
            feat = sb("rwkv_feat", [P, 4, TOK])
            low = sb("rwkv_low", [P, 3, TOK])
            raw = sb("rwkv_raw", [P, TOK + 4])
            lw = sb("log_w", [P, 4, TOK])
            a = sb("rwkv_a", [P, 2, TOK])
            small = sb("rwkv_small", [P, 3, 256])
            with ExitStack() as inner:
                w = self.sbuf(inner, "w_rwkv", [P, KD, 2, P])
                s_w = [self.count(f"rwkv_w_landed{i}", 16) for i in range(2)]
                block = inner.enter_context(nc.Block())

                @block.sync
                def _(sp):
                    sp.dma_start(cst[:, :], io["rwkvc"]).then_inc(landed.sem, 16)
                    sp.dma_start(small[:, 0, :], io["rwkv_w2"][l].rearrange("d k n -> (d k) n")).then_inc(landed.sem, 16)
                    sp.dma_start(small[0:64, 1, :], io["rwkv_a2"][l]).then_inc(landed.sem, 16)
                    sp.dma_start(small[:, 2, :], io["rwkv_g2"][l]).then_inc(landed.sem, 16)
                    for n, f in enumerate(order):
                        lo, width = at[f]
                        if n >= 2:
                            sp.wait_ge(s["projected"].sem, s["projected"] + (n - 1))
                        c0 = MLA_COLS + RET_COLS + lo
                        sp.dma_start(w[:, :, n % 2, 0:width], io["w_in"][l, :, c0:c0 + width].rearrange("(k p) n -> p k n", p=P)
                                     ).then_inc(s_w[n % 2].sem, 16)
                    sp.wait_ge(landed.sem, landed + 4)

                @block.tensor
                def _(pe):
                    for n, f in enumerate(order):
                        width = at[f][1]
                        pe.wait_ge(s_w[n % 2].sem, s_w[n % 2] + (n // 2 + 1))
                        if n >= 2:
                            pe.wait_ge(s["tile_read"].sem, s["tile_read"] + (n - 1))
                        for lo, hi in ((0, CTX), (CTX, TOK)):
                            b = 2 * (n % 2) + (lo > 0)
                            for k in range(KD):
                                mm = pe.matmul(self.psum[0:width, b, 0:hi - lo], w[:, k, n % 2, 0:width],
                                               self.u_t[:, k, lo:hi], start=(k == 0), stop=(k == KD - 1))
                        mm.then_inc(s["projected"].sem, 1)

                @block.vector
                def _(dve):
                    link = self.dve_chain.on(dve)
                    link(dve.memset(raw[:, :], 0.0))
                    for n, f in enumerate(order):
                        width = at[f][1]
                        dve.wait_ge(s["projected"].sem, s["projected"] + (n + 1))
                        link(dve.tensor_copy(raw[0:width, 1:1 + CTX], self.psum[0:width, 2 * (n % 2), 0:CTX]))
                        dve.tensor_copy(raw[0:width, 3 + CTX:3 + TOK], self.psum[0:width, 2 * (n % 2) + 1, 0:LAT]
                                        ).then_inc(s["tile_read"].sem, 1)
                        dve.wait_ge(s["tile_read"].sem, s["tile_read"] + (n + 1))
                        dst = {6: low[:, 0], 7: low[:, 1], 8: low[:, 2], 4: v[:, 0], 5: v[:, 1]}.get(f)
                        if dst is None:
                            dst = feat[:, f]
                        for lo, off in ((0, 1), (CTX, 3)):
                            width_t = CTX if lo == 0 else LAT
                            now = raw[0:width, lo + off:lo + off + width_t]
                            before, after = (raw[0:width, lo + off + d:lo + off + d + width_t] for d in (-1, 1))
                            to = dst[0:width, lo:lo + width_t]
                            link(dve.tensor_tensor(to, before, after, ALU.add))
                            link(dve.scalar_tensor_tensor(to, to, 0.5, now, ALU.mult, ALU.subtract))
                            link(dve.scalar_tensor_tensor(to, to, self.col("mu")[0:width, f:f + 1], now, ALU.mult, ALU.add))
            landed.advance(4)
            s["projected"].advance(9)
            s["tile_read"].advance(9)
            s_w[0].advance(5)
            s_w[1].advance(4)

            with ExitStack() as inner:
                sb = lambda name, shape: self.sbuf(inner, name, shape)
                kk, tmp = sb("kk", [P, 2, TOK]), raw[:, 0:TOK]
                inc, exc = sb("decay_x1", [P, TOK]), sb("decay_x2", [P, TOK])
                exps = low
                tot = sb("chunk_total", [P, NCH])
                block = inner.enter_context(nc.Block())
                halves = ((0, CTX), (CTX, TOK))
                wide = lambda n: self.psum[:, 2 * (n % 2):2 * (n % 2) + 2, :]
                jobs = [("w", q) for q in range(4)] + [("a", f) for f in range(2)] + [("g", f) for f in range(2)] + \
                       [("kk", f) for f in range(2)] + [("bonus", f) for f in range(2)]

                def each_half(n):
                    return [(wide(n)[:, b, 0:hi - lo], slice(lo, hi)) for b, (lo, hi) in enumerate(halves)]

                @block.tensor
                def _(pe):
                    pe.wait_ge(s["wide_act"].sem, s["wide_act"] + 1)
                    for n, (job, q) in enumerate(jobs):
                        if n >= 2:
                            pe.wait_ge(s["wide_read"].sem, s["wide_read"] + (n - 1))
                        if job in ("kk", "bonus"):
                            pe.wait_ge(s["table"].sem, s["table"] + (n - 7))
                        for b, (lo, hi) in enumerate(halves):
                            d, f = divmod(q, 2)
                            lhs, rhs = {
                                "w": lambda: (small[64 * d:64 * d + 64, 0, f * P:(f + 1) * P], low[64 * d:64 * d + 64, 0, lo:hi]),
                                "a": lambda: (small[0:64, 1, q * P:(q + 1) * P], low[0:64, 1, lo:hi]),
                                "g": lambda: (small[:, 2, q * P:(q + 1) * P], low[:, 2, lo:hi]),
                                "kk": lambda: (self.c("pair_ones"), tmp[:, lo:hi]),
                                "bonus": lambda: (self.c("pair_ones"), tmp[:, lo:hi])}[job]()
                            mm = pe.matmul(wide(n)[:, b, 0:hi - lo], lhs, rhs, start=True, stop=True)
                        mm.then_inc(s["wide"].sem, 1)

                @block.scalar
                def _(act):
                    act.activation(low[:, 0, :], low[:, 0, :], ACT.Tanh)
                    act.activation(low[:, 2, :], low[:, 2, :], ACT.Sigmoid).then_inc(s["wide_act"].sem, 1)
                    for n, (job, q) in enumerate(jobs[0:8]):
                        act.wait_ge(s["wide"].sem, s["wide"] + (n + 1))
                        for src, cut in each_half(n):
                            if job == "w":
                                ins = act.activation(lw[:, q, cut], src, ACT.Sigmoid, bias=self.col("w0")[:, q:q + 1])
                            elif job == "a":
                                ins = act.activation(a[:, q, cut], src, ACT.Sigmoid, bias=self.col("a0")[:, q:q + 1])
                            else:
                                ins = act.copy(g[:, q, cut], src)
                        ins.then_inc(s["wide_read"].sem, 1)
                    for f in range(2):
                        act.wait_ge(s["root"].sem, s["root"] + (2 * f + 1))
                        act.activation(tmp, tmp, ACT.Sqrt).then_inc(s["root"].sem, 1)
                    for q in range(4):
                        act.wait_ge(s["decay_in"].sem, s["decay_in"] + (q + 1))
                        sign = (1.0, -1.0)[q // 2]
                        by_query, by_update = (exc, inc) if q < 2 else (inc, exc)
                        act.activation(exps[:, 0, :], by_query[:, :], ACT.Exp, scale=sign)
                        act.activation(exps[:, 1, :], by_update[:, :], ACT.Exp, scale=sign)
                        act.activation(exps[:, 2, :], by_update[:, :], ACT.Exp, scale=-sign)
                        act.activation(half[:, q, :], tot[:, :], ACT.Exp, scale=0.5).then_inc(s["decay_exp"].sem, 1)

                @block.vector
                def _(dve):
                    link = self.dve_chain.on(dve)
                    dve.wait_ge(s["wide_read"].sem, s["wide_read"] + 8)
                    for q in range(4):
                        link(dve.tensor_scalar(lw[:, q, :], lw[:, q, :], DECAY, None, ALU.mult))
                    for f in range(2):
                        n = 8 + f
                        link(dve.tensor_scalar(kk[:, f, :], feat[:, 2 + f, :], self.col("k_k")[:, f:f + 1], None, ALU.mult))
                        dve.tensor_tensor(tmp, kk[:, f, :], kk[:, f, :], ALU.mult).then_inc(s["table"].sem, 1)
                        dve.wait_ge(s["wide"].sem, s["wide"] + (n + 1))
                        for src, cut in each_half(n):
                            ins = dve.tensor_scalar(tmp[:, cut], src, 1e-24, None, ALU.max)
                            if cut.start:
                                ins.then_inc(s["wide_read"].sem, 1)
                            else:
                                link(ins)
                        dve.wait_ge(s["wide_read"].sem, s["wide_read"] + (n + 1))
                        dve.tensor_copy(tot[:, 0:1], tmp[:, 0:1]).then_inc(s["root"].sem, 1)
                        dve.wait_ge(s["root"].sem, s["root"] + (2 * f + 2))
                        link(dve.reciprocal(tmp, tmp))
                        link(dve.tensor_tensor(kk[:, f, :], kk[:, f, :], tmp, ALU.mult))
                    for f in range(2):
                        link(dve.tensor_scalar(tmp, a[:, f, :], -1.0, self.col("k_a")[:, f:f + 1], ALU.add, ALU.mult))
                        link(dve.scalar_tensor_tensor(feat[:, 2 + f, :], tmp, 1.0, feat[:, 2 + f, :], ALU.add, ALU.mult))
                        link(dve.tensor_tensor(a[:, f, :], a[:, f, :], kk[:, f, :], ALU.mult))
                    for f in range(2):
                        n = 10 + f
                        dve.scalar_tensor_tensor(tmp, feat[:, f, :], self.col("r_k")[:, f:f + 1], feat[:, 2 + f, :],
                                                 ALU.mult, ALU.mult).then_inc(s["table"].sem, 1)
                        dve.wait_ge(s["wide"].sem, s["wide"] + (n + 1))
                        for src, cut in each_half(n):
                            ins = dve.tensor_tensor(bonus[:, f, cut], src, v[:, f, cut], ALU.mult)
                        ins.then_inc(s["wide_read"].sem, 1)
                    chunks = lambda ap: ap.rearrange("p (c t) -> p c t", t=C)
                    for q in range(4):
                        f = q % 2
                        link(dve.tensor_tensor_scan(inc[:, :], cc("restart"), lw[:, q, :], 0.0, ALU.mult, ALU.add))
                        link(dve.tensor_copy(tot[:, :], chunks(inc[:, :])[:, :, C - 1]))
                        link(dve.scalar_tensor_tensor(chunks(inc[:, :]), spread(tot[:, :], 2, C), -0.5, chunks(inc[:, :]),
                                                      ALU.mult, ALU.add))
                        dve.tensor_tensor(exc[:, :], inc[:, :], lw[:, q, :], ALU.subtract).then_inc(s["decay_in"].sem, 1)
                        dve.wait_ge(s["decay_exp"].sem, s["decay_exp"] + (q + 1))
                        e = lambda i: chunks(exps[:, i, :])
                        dve.tensor_tensor(queries[:, q, :, 0, :], chunks(kk[:, f, :]), e(0), ALU.mult)
                        dve.tensor_tensor(queries[:, q, :, 1, :], chunks(feat[:, f, :]), e(1), ALU.mult)
                        dve.scalar_tensor_tensor(updates[:, q, :, 0, :], chunks(a[:, f, :]), -1.0, e(2), ALU.mult, ALU.mult)
                        link(dve.tensor_tensor(updates[:, q, :, 1, :], chunks(feat[:, 2 + f, :]), e(2), ALU.mult))
            for n, k in (("wide", 12), ("wide_act", 1), ("wide_read", 12), ("table", 4), ("root", 4),
                         ("decay_exp", 4), ("decay_in", 4)):
                s[n].advance(k)

    def rwkv_chunks(self, l, last, g, bonus, v, queries, updates, half):
        nc, cc = self.nc, self.cc
        back = list(range(CCH - 1, -1, -1)) + list(range(NCH - 1, CCH - 1, -1))
        ch = lambda q, i: i if q < 2 else back[i]
        names = ("prep", "masked_b", "masked_k", "blocks", "copied", "inner", "inner_copied", "grown", "added",
                 "rest", "rest_copied", "removed", "removed_copied", "moved", "state", "y_copied",
                 "var", "root", "normed", "turned")
        s = {n: self.count("chunk_" + n) for n in names}
        NL = len(LEVELS)
        chain_at = {(0, 0): ("rest", 0), (0, 1): ("removed", 0), (1, 0): ("move", 0),
                    (2, 0): ("rest", 1), (2, 1): ("removed", 1), (3, 0): ("move", 1)}
        nth = lambda i, n: 2 * NL * (i // 2) + 2 * n + i % 2
        with ExitStack() as scope:
            sb = lambda name, shape: self.sbuf(scope, name, shape)
            m_b, m_k = sb("queries_b", [P, 4, 4, 2, C]), sb("queries_k", [P, 4, 4, 2, C])
            inv = sb("inverse", [P, 4, 2, 4, C])
            steps = sb("level_blocks", [P, 2, NL, 4, C])
            inner = sb("inner", [P, 2, 4, C])
            rows = sb("update_rows", [P, 4, 3, 4, C])
            state, rest, removed = sb("state", [P, 4, C]), sb("rest", [P, 4, C]), sb("removed", [P, 4, C])
            move = sb("state_decay", [P, 4])
            y = [self.mix_t[:, 6:8, :].rearrange("p k n -> p (k n)").rearrange("p (c f t) -> p c f t", c=NCH, f=2),
                 sb("rwkv_y", [P, NCH, 2, C])[:, :, :, :]]
            st = sb("rwkv_stat", [P, 4, 2 * NCH])
            block = scope.enter_context(nc.Block())
            ps = lambda bank, half_: self.psum[:, bank, 256 * half_:256 * half_ + 256].rearrange("p (q t) -> p q t", q=4)
            heads = [(q, slice(64 * e, 64 * e + 64)) for q in range(4) for e in range(2)]

            @block.tensor
            def _(pe):
                def masked_products(i):
                    for bank, what in ((0, "masked_b"), (1, "masked_k")):
                        if i >= 1:
                            pe.wait_ge(s[what].sem, s[what] + i)
                        for q, r in heads:
                            c = ch(q, i)
                            mm = pe.matmul(self.psum[r, bank, q * 128:q * 128 + 128], updates[r, q, c, bank, :],
                                           queries[r, q, c, :, :].rearrange("p a t -> p (a t)"), start=True, stop=True)
                        mm.then_inc(s["prep"].sem, 1)

                def turn_updates(i):
                    b_bank, k_bank = (6, 7) if i % 2 == 0 else (7, 6)
                    if i >= 2:
                        last_pair = nth(i // 2 * 2 - 1, NL - 1) + 1
                        pe.wait_ge(s["inner_copied"].sem, s["inner_copied"] + last_pair)
                        pe.wait_ge(s["added"].sem, s["added"] + last_pair)
                    if i % 2:
                        pe.wait_ge(s["copied"].sem, s["copied"] + 2 * i)
                    for bank, of in ((4 + i % 2, lambda q, c: v[:, q % 2, c * C:(c + 1) * C]),
                                     (b_bank, lambda q, c: updates[:, q, c, 0, :]), (k_bank, lambda q, c: updates[:, q, c, 1, :])):
                        for q in range(4):
                            mm = pe.transpose(self.psum[0:C, bank, q * P:(q + 1) * P], of(q, ch(q, i)), self.c("ident"))
                        mm.then_inc(s["prep"].sem, 1)

                def inner_part(i, n):
                    if n == 0:
                        pe.wait_ge(s["blocks"].sem, s["blocks"] + (i + 1))
                    else:
                        pe.wait_ge(s["added"].sem, s["added"] + (nth(i, n - 1) + 1))
                    for q, r in heads:
                        mm = pe.matmul(ps(4 + i % 2, 0)[r, q, :], steps[r, i % 2, n, q, :], inv[r, i % 4, 1, q, :], start=True, stop=True)
                    mm.then_inc(s["inner"].sem, 1)

                def grow(i, n):
                    if n == 0:
                        pe.wait_ge(s["copied"].sem, s["copied"] + 2 * (i // 2 * 2 + 2))
                    pe.wait_ge(s["inner_copied"].sem, s["inner_copied"] + (nth(i, n) + 1))
                    for q, r in heads:
                        mm = pe.matmul(ps(6 + i % 2, 0)[r, q, :], inner[r, i % 2, q, :], inv[r, i % 4, 0, q, :], start=True, stop=True)
                    mm.then_inc(s["grown"].sem, 1)

                def rest_part(i):
                    pe.wait_ge(s["state"].sem, s["state"] + (i + 1))
                    for q, r in heads:
                        pe.matmul(ps(2, 0)[r, q, :], queries[r, q, ch(q, i), 0, :], state[r, q, :], start=True, stop=False)
                        mm = pe.matmul(ps(2, 0)[r, q, :], m_k[r, i % 4, q, 0, :], rows[r, i % 4, 2, q, :], start=False, stop=True)
                    mm.then_inc(s["rest"].sem, 1)

                def removed_part(i):
                    pe.wait_ge(s["rest_copied"].sem, s["rest_copied"] + (i + 1))
                    pe.wait_ge(s["added"].sem, s["added"] + (nth(i, NL - 1) + 1))
                    for q, r in heads:
                        mm = pe.matmul(ps(2, 1)[r, q, :], inv[r, i % 4, 0, q, :], rest[r, q, :], start=True, stop=True)
                    mm.then_inc(s["removed"].sem, 1)

                def move_part(i):
                    pe.wait_ge(s["removed_copied"].sem, s["removed_copied"] + (i + 1))
                    if i >= 1:
                        pe.wait_ge(s["y_copied"].sem, s["y_copied"] + i)
                    for q, r in heads:
                        pe.matmul(ps(3, 0)[r, q, :], queries[r, q, ch(q, i), 1, :], state[r, q, :], start=True, stop=False)
                        pe.matmul(ps(3, 0)[r, q, :], m_b[r, i % 4, q, 1, :], removed[r, q, :], start=False, stop=False)
                        pe.matmul(ps(3, 0)[r, q, :], m_k[r, i % 4, q, 1, :], rows[r, i % 4, 2, q, :], start=False, stop=True)
                        pe.matmul(ps(3, 1)[r, q, :], rows[r, i % 4, 0, q, :], removed[r, q, :], start=True, stop=False)
                        mm = pe.matmul(ps(3, 1)[r, q, :], rows[r, i % 4, 1, q, :], rows[r, i % 4, 2, q, :], start=False, stop=True)
                    mm.then_inc(s["moved"].sem, 1)

                parts = {"rest": rest_part, "removed": removed_part, "move": move_part}
                for i in range(0, NCH + 2, 2):
                    if i < NCH:
                        for j in (i, i + 1):
                            masked_products(j)
                            turn_updates(j)
                    for n in range(NL):
                        for a in range(2):
                            if i < NCH:
                                inner_part(i + a, n)
                            if i >= 2 and (n, a) in chain_at:
                                part, b = chain_at[n, a]
                                parts[part](i - 2 + b)
                        if i < NCH:
                            grow(i, n)
                            grow(i + 1, n)
                pe.wait_ge(s["normed"].sem, s["normed"] + 1)
                for f in range(2):
                    for c in range(NCH):
                        for r in (slice(0, 64), slice(64, 128)):
                            mm = pe.matmul(self.flat[r, 1024 * f + c * C:1024 * f + (c + 1) * C], y[0][r, c, f, :],
                                           self.c("ident64")[r, :], start=True, stop=True)
                mm.then_inc(s["turned"].sem, 1)

            @block.scalar
            def _(act):
                def copy_rows(i):
                    if i >= 4:
                        act.wait_ge(s["moved"].sem, s["moved"] + (i - 3))
                    for a, bank in enumerate((6, 7) if i % 2 == 0 else (7, 6)):
                        act.wait_ge(s["prep"].sem, s["prep"] + (5 * i + 4 + a))
                        for e in range(2):
                            turned = self.psum[0:C, bank, :].rearrange("p (q e d) -> p q e d", q=4, e=2)[:, :, e, :]
                            ins = act.copy(rows[64 * e:64 * e + 64, i % 4, a], turned)
                        ins.then_inc(s["copied"].sem, 1)

                for i in range(0, NCH + 2, 2):
                    if i < NCH:
                        copy_rows(i)
                        copy_rows(i + 1)
                    for n in range(NL):
                        for a in range(2):
                            if i < NCH:
                                act.wait_ge(s["inner"].sem, s["inner"] + (nth(i + a, n) + 1))
                                if n >= 1:
                                    act.wait_ge(s["grown"].sem, s["grown"] + (nth(i + a, n - 1) + 1))
                                act.copy(inner[:, a, :, :], ps(4 + a, 0)).then_inc(s["inner_copied"].sem, 1)
                            part, b = chain_at.get((n, a), ("", 0))
                            if i >= 2 and part == "rest":
                                act.wait_ge(s["rest"].sem, s["rest"] + (i - 2 + b + 1))
                                act.copy(rest[:, :, :], ps(2, 0)).then_inc(s["rest_copied"].sem, 1)
                            if i >= 2 and part == "removed":
                                act.wait_ge(s["removed"].sem, s["removed"] + (i - 2 + b + 1))
                                act.copy(removed[:, :, :], ps(2, 1)).then_inc(s["removed_copied"].sem, 1)
                act.wait_ge(s["var"].sem, s["var"] + 1)
                act.activation(st[:, 2, :], st[:, 1, :], ACT.Sqrt).then_inc(s["root"].sem, 1)

            @block.vector
            def _(dve):
                link = self.dve_chain.on(dve)

                def plain(a):
                    flat = lambda x: inv[:, a, x].rearrange("p q t -> p (q t)")
                    return dve.transpose(flat(1), flat(0))

                def mask(i):
                    full = lambda b: self.psum[:, b, :].rearrange("p (q a t) -> p q a t", q=4, a=2)
                    m = cc("mask").rearrange("p (q a t) -> p q a t", q=4, a=2)
                    quarter = lambda ap: ap.rearrange("p (q t) -> p q t", q=4)
                    a = i % 4
                    dve.wait_ge(s["prep"].sem, s["prep"] + (5 * i + 1))
                    if i >= 4:
                        dve.wait_ge(s["moved"].sem, s["moved"] + (i - 3))
                    dve.tensor_tensor(m_b[:, a], full(0), m, ALU.mult).then_inc(s["masked_b"].sem, 1)
                    dve.wait_ge(s["prep"].sem, s["prep"] + (5 * i + 2))
                    dve.tensor_tensor(m_k[:, a], full(1), m, ALU.mult).then_inc(s["masked_k"].sem, 1)
                    dve.wait_ge(s["masked_b"].sem, s["masked_b"] + (i + 1))
                    if i >= 2:
                        dve.wait_ge(s["grown"].sem, s["grown"] + (nth(i - 2, NL - 1) + 1))
                    dve.tensor_tensor(steps[:, i % 2, :, :, :], spread(m_b[:, a, :, 0, :], 1, NL),
                                      cc("level").rearrange("p (n q t) -> p n q t", n=NL, q=4), ALU.mult)
                    link(dve.tensor_tensor(inv[:, a, 0], m_b[:, a, :, 0, :], quarter(cc("first_t")), ALU.mult))
                    link(dve.tensor_tensor(inv[:, a, 0], inv[:, a, 0], spread(self.c("ident64"), 1, 4), ALU.add))
                    dve.wait_ge(s["prep"].sem, s["prep"] + (5 * i + 3))
                    for e in range(2):
                        turned = self.psum[0:C, 4 + i % 2, :].rearrange("p (q e d) -> p q e d", q=4, e=2)[:, :, e, :]
                        dve.tensor_copy(rows[64 * e:64 * e + 64, a, 2], turned)
                    plain(a).then_inc(s["blocks"].sem, 1)

                def move_state(j):
                    for d in range(2):
                        now, then = ch(2 * d, j), ch(2 * d, min(j + 1, NCH - 1))
                        link(dve.tensor_tensor(move[:, 2 * d:2 * d + 2], half[:, 2 * d:2 * d + 2, now],
                                               half[:, 2 * d:2 * d + 2, then], ALU.mult))
                    dve.wait_ge(s["moved"].sem, s["moved"] + (j + 1))
                    link(dve.tensor_tensor(state[:, :, :], state[:, :, :], ps(3, 1), ALU.add))
                    dve.tensor_tensor(state[:, :, :], state[:, :, :], spread(move[:, :], 2, C), ALU.mult).then_inc(s["state"].sem, 1)
                    dve.tensor_copy(y[0][:, ch(0, j), :, :], ps(3, 0)[:, 0:2, :])
                    dve.tensor_copy(y[1][:, ch(2, j), :, :], ps(3, 0)[:, 2:4, :]).then_inc(s["y_copied"].sem, 1)
                    dve.wait_ge(s["state"].sem, s["state"] + (j + 2))

                dve.memset(state[:, :, :], 0.0).then_inc(s["state"].sem, 1)
                for i in range(0, NCH + 2, 2):
                    if i < NCH:
                        mask(i)
                        mask(i + 1)
                    for n in range(NL):
                        part, b = chain_at.get((n, 0), ("", 0))
                        if i >= 2 and part == "move":
                            move_state(i - 2 + b)
                        if i < NCH:
                            for j in (i, i + 1):
                                dve.wait_ge(s["grown"].sem, s["grown"] + (nth(j, n) + 1))
                                if n == 0:
                                    dve.wait_ge(s["blocks"].sem, s["blocks"] + (j + 1))
                                else:
                                    dve.wait_ge(s["added"].sem, s["added"] + (nth(j, n - 1) + 1))
                                ins = dve.tensor_tensor(inv[:, j % 4, 0], inv[:, j % 4, 0], ps(6 + j % 2, 0), ALU.add)
                                if n < NL - 1:
                                    link(ins)
                                    ins = plain(j % 4)
                                ins.then_inc(s["added"].sem, 1)
                dve.wait_ge(s["y_copied"].sem, s["y_copied"] + NCH)
                sq = m_b[:, 0:3].rearrange("p a q b t -> p (a q b) t")
                y0, y1 = (a.rearrange("p c f t -> p (c f) t") for a in y)
                link(dve.tensor_tensor(y0, y0, y1, ALU.add))
                link(dve.tensor_reduce(st[:, 0, :], y0, AX, ALU.add))
                link(dve.tensor_scalar(st[:, 0, :], st[:, 0, :], 1.0 / 64, None, ALU.mult))
                link(dve.tensor_tensor(y0, y0, spread(st[:, 0, :], 2, C), ALU.subtract))
                link(dve.tensor_tensor(sq, y0, y0, ALU.mult))
                link(dve.tensor_reduce(st[:, 1, :], sq, AX, ALU.add))
                dve.tensor_scalar(st[:, 1, :], st[:, 1, :], 1.0 / 64, 64e-5, ALU.mult, ALU.add).then_inc(s["var"].sem, 1)
                dve.wait_ge(s["root"].sem, s["root"] + 1)
                link(dve.reciprocal(st[:, 3, :], st[:, 2, :]))
                link(dve.tensor_tensor(y0, y0, spread(st[:, 3, :], 2, C), ALU.mult))
                lnw = spread(self.row("ln_w").rearrange("p (f t) -> p f t", f=2), 1, NCH)
                dve.tensor_tensor(y[0], y[0], lnw, ALU.mult).then_inc(s["normed"].sem, 1)
                dve.wait_ge(s["turned"].sem, s["turned"] + 1)
                for f in range(2):
                    to = self.mix_t[:, 6 + f, :]
                    link(dve.tensor_tensor(to, self.flat[:, 1024 * f:1024 * f + TOK], bonus[:, f, :], ALU.add))
                    link(dve.tensor_tensor(to, to, g[:, f, :], ALU.mult))
        per = {"state": NCH + 1, "prep": 5 * NCH, "copied": 2 * NCH, **{n: NL * NCH for n in ("inner", "inner_copied", "grown", "added")},
               **{n: 1 for n in ("var", "root", "normed", "turned")}}
        for n in names:
            s[n].advance(per.get(n, NCH))

    def project_out(self, l, last, tiles):
        nc, io = self.nc, self.io
        landed, made, added = self.count("w_out_landed", 16), self.count("out_made"), self.count("out_added")
        with ExitStack() as scope:
            w = self.sbuf(scope, "w_out", [P, KD, D])
            tmp = self.sbuf(scope, "gated", [P, D])
            block = scope.enter_context(nc.Block())

            @block.sync
            def _(sp):
                sp.dma_start(w[:, :, :], io["w_out"][l].rearrange("(k p) n -> p k n", p=P)).then_inc(landed.sem, 16)

            @block.tensor
            def _(pe):
                pe.wait_ge(landed.sem, landed + 1)
                for n, t in enumerate(tiles):
                    if n >= 2:
                        pe.wait_ge(added.sem, added + (n - 1))
                    for b in range(2):
                        for k in range(KD):
                            mm = pe.matmul(self.psum[:, 2 * (n % 2) + b, :], self.mix_t[:, k, t * P:(t + 1) * P],
                                           w[:, k, b * 512:(b + 1) * 512], start=(k == 0), stop=(k == KD - 1))
                    mm.then_inc(made.sem, 1)

            @block.vector
            def _(dve):
                self.add_gated(dve, tmp, 0, tiles, made, added)
        landed.advance(1)
        made.advance(len(tiles))
        added.advance(len(tiles))

    def add_gated(self, dve, tmp, which, tiles, made, added):
        link = self.dve_chain.on(dve)
        for n, t in enumerate(tiles):
            dve.wait_ge(made.sem, made + (n + 1))
            product = self.flat[:, 1024 * (n % 2):1024 * (n % 2) + D]
            if n >= 1:
                dve.wait_ge(added.sem, added + n)
            link(dve.tensor_tensor(tmp[:, :], product, self.gates[:, which, int(t < CT), :], ALU.mult))
            dve.tensor_tensor(self.x[:, t, :], self.x[:, t, :], tmp[:, :], ALU.add).then_inc(added.sem, 1)

    def route(self, l, last, tiles):
        nc, io = self.nc, self.io
        landed = self.count("router_landed", 16)
        names = ("logits", "shifted", "exp", "affinity", "turned", "placed", "back")
        s = {n: self.count("route_" + n) for n in names}
        lo = tiles[0]
        groups = [(CT, NT, CAP_L)] + ([] if last else [(0, CT, CAP_C)])
        with ExitStack() as scope:
            sb = lambda name, shape: self.sbuf(scope, name, shape)
            w = sb("router_w", [P, KD, E_N])
            st = sb("router_stat", [P, 3, NT])
            work, chosen = sb("affinity_left", [E_N, TOK]), sb("chosen", [E_N, TOK])
            place, ones = sb("place", [E_N, TOK]), sb("scan_ones", [E_N, LAT])
            best = sb("best", [E_N, 8])
            block = scope.enter_context(nc.Block())
            logits = self.psum[:, 0, 0:NT * E_N].rearrange("p (t e) -> p t e", e=E_N)
            back = self.psum[:, 3, 0:NT * E_N].rearrange("p (t e) -> p t e", e=E_N)
            turned = lambda a, b: self.psum[0:E_N, 1 if a < CT else 2, 0:(b - a) * P]

            @block.sync
            def _(sp):
                sp.dma_start(w[:, :, :], io["router_w"][l].rearrange("(k p) n -> p k n", p=P)).then_inc(landed.sem, 16)
                for m in range(W_AHEAD):
                    self.load_expert_part(sp, l, 0, m)

            @block.tensor
            def _(pe):
                pe.wait_ge(landed.sem, landed + 1)
                for t in tiles:
                    for k in range(KD):
                        mm = pe.matmul(logits[:, t, :], self.u_t[:, k, t * P:(t + 1) * P], w[:, k, :],
                                       start=(k == 0), stop=(k == KD - 1))
                mm.then_inc(s["logits"].sem, 1)
                pe.wait_ge(s["affinity"].sem, s["affinity"] + 1)
                for a, b, _ in groups:
                    for t in range(a, b):
                        mm = pe.transpose(turned(a, b)[:, (t - a) * P:(t - a + 1) * P], self.aff[:, t, :], self.c("ident"))
                mm.then_inc(s["turned"].sem, 1)
                pe.wait_ge(s["placed"].sem, s["placed"] + 1)
                for t in tiles:
                    mm = pe.transpose(back[:, t, :], place[:, t * P:(t + 1) * P], self.c("ident")[0:E_N, 0:E_N])
                mm.then_inc(s["back"].sem, 1)

            @block.scalar
            def _(act):
                act.wait_ge(s["shifted"].sem, s["shifted"] + 1)
                act.activation(self.aff[:, lo:NT, :], self.aff[:, lo:NT, :], ACT.Exp).then_inc(s["exp"].sem, 1)

            @block.vector
            def _(dve):
                link = self.dve_chain.on(dve)
                link(dve.memset(ones[:, :], 1.0))
                dve.wait_ge(s["logits"].sem, s["logits"] + 1)
                aff = self.aff[:, lo:NT, :]
                link(dve.tensor_reduce(st[:, 0, lo:NT], logits[:, lo:NT, :], AX, ALU.max))
                dve.tensor_tensor(aff, logits[:, lo:NT, :], spread(st[:, 0, lo:NT], 2, E_N), ALU.subtract).then_inc(s["shifted"].sem, 1)
                dve.wait_ge(s["exp"].sem, s["exp"] + 1)
                link(dve.tensor_reduce(st[:, 1, lo:NT], aff, AX, ALU.add))
                link(dve.reciprocal(st[:, 2, lo:NT], st[:, 1, lo:NT]))
                dve.tensor_tensor(aff, aff, spread(st[:, 2, lo:NT], 2, E_N), ALU.mult).then_inc(s["affinity"].sem, 1)
                dve.wait_ge(s["turned"].sem, s["turned"] + 1)
                for n, (a, b, cap) in enumerate(groups):
                    cut = slice(a * P, b * P)
                    link(dve.tensor_copy(work[:, cut], turned(a, b)))
                    for _ in range(cap // 8):
                        link(dve.max(best[:, :], work[:, cut]))
                        link(dve.match_replace(work[:, cut], best[:, :], work[:, cut], -1.0))
                    link(dve.tensor_scalar(chosen[:, cut], work[:, cut], -1.0, None, ALU.is_equal))
                    link(dve.tensor_tensor_scan(place[:, cut], ones[:, 0:(b - a) * P], chosen[:, cut], 0.0, ALU.mult, ALU.add))
                    link(dve.tensor_tensor(place[:, cut], place[:, cut], chosen[:, cut], ALU.mult))
                    ins = dve.tensor_scalar(place[:, cut], place[:, cut], 1.0, None, ALU.subtract)
                    if n == len(groups) - 1:
                        ins.then_inc(s["placed"].sem, 1)
                    else:
                        link(ins)
                dve.wait_ge(s["back"].sem, s["back"] + 1)
                link(dve.tensor_copy(self.slot[:, lo:NT, :], back[:, lo:NT, :]))
        landed.advance(1)
        for n in names:
            s[n].advance(1)

    def gather(self, l, last):
        nc = self.nc
        onehot, gathered = self.count("gather_onehot"), self.count("gathered")
        kept = [self.count("gather_kept_dve"), self.count("gather_kept_act")]
        halves = 2
        items = [(CT, NT, CAP_L, 0, g * E_N // halves, (g + 1) * E_N // halves, k) for k in range(KD) for g in range(halves)] + \
                ([] if last else [(0, CT, CAP_C, 1, 0, E_N, k) for k in range(KD)])
        with ExitStack() as scope:
            hot_l = self.sbuf(scope, "onehot_lat", [P, NT - CT, E_N, CAP_L])
            hot_c = self.sbuf(scope, "onehot_ctx", [P, CT, E_N, CAP_C])
            block = scope.enter_context(nc.Block())

            def result(i):
                a, b, cap, v, e0, e1, k = items[i]
                at = 0 if cap == CAP_L else CAP_L
                return (self.chosen[:, e0:e1, k, at:at + cap],
                        self.psum[:, i % 4, 0:(e1 - e0) * cap].rearrange("p (e c) -> p e c", c=cap),
                        self.scale2[:, k, v:v + 1], self.mod[:, 24 + k, v:v + 1])

            @block.tensor
            def _(pe):
                pe.wait_ge(onehot.sem, onehot + 1)
                for i, (a, b, cap, v, e0, e1, k) in enumerate(items):
                    if i >= 4:
                        pe.wait_ge(kept[i % 2].sem, kept[i % 2] + ((i - 4) // 2 + 1))
                    hot = hot_l if cap == CAP_L else hot_c
                    for t in range(a, b):
                        mm = pe.matmul(self.psum[:, i % 4, 0:(e1 - e0) * cap], self.xn[:, t, k * P:(k + 1) * P],
                                       hot[:, t - a, e0:e1, :].rearrange("p e c -> p (e c)"), start=(t == a), stop=(t == b - 1))
                    mm.then_inc(gathered.sem, 1)

            @block.scalar
            def _(act):
                for i in range(1, len(items), 2):
                    to, got, scale, shift = result(i)
                    act.wait_ge(gathered.sem, gathered + (i + 1))
                    act.activation(to, got, ACT.Identity, bias=shift, scale=scale).then_inc(kept[1].sem, 1)

            @block.vector
            def _(dve):
                cuts = [(t, hot_l[:, t - CT], CAP_L) for t in range(CT, NT)] + ([] if last else [(t, hot_c[:, t], CAP_C) for t in range(CT)])
                for t, hot, cap in cuts:
                    ins = dve.tensor_tensor(hot, spread(self.c("iota")[:, 0:cap], 1, E_N), spread(self.slot[:, t, :], 2, cap), ALU.is_equal)
                ins.then_inc(onehot.sem, 1)
                for i in range(0, len(items), 2):
                    to, got, scale, shift = result(i)
                    dve.wait_ge(gathered.sem, gathered + (i + 1))
                    dve.tensor_scalar(to, got, scale, shift, ALU.mult, ALU.add).then_inc(kept[0].sem, 1)
        onehot.advance(1)
        gathered.advance(len(items))
        for side in kept:
            side.advance(len(items) // 2)

    def load_expert_part(self, sp, l, expert, m):
        name, h = W_PARTS[m % len(W_PARTS)]
        src = self.io[name][l].rearrange("e (k p) n -> p e k n", p=P)
        src = src[:, expert, :, h * 512:(h + 1) * 512] if isinstance(expert, int) else \
            src[:, bass.ds(expert, 1), :, h * 512:(h + 1) * 512].rearrange("p e k n -> p (e k) n")
        landed = self.count(f"expert_w_landed{m % W_SLOTS}", 16)
        sp.dma_start(self.expert_w[:, m % W_SLOTS, :, :], src).then_inc(landed.sem, 16)

    def experts(self, l, last, scope):
        nc = self.nc
        UNROLL = 4
        landed = [self.count(f"expert_w_landed{i}", 16) for i in range(W_SLOTS)]
        multiplied = [self.count(f"expert_w_multiplied{i}") for i in range(W_SLOTS)]
        names = ("sigmoid", "gated", "hidden", "stored")
        s = {n: self.count("expert_" + n) for n in names}
        M = CAP_L + (0 if last else CAP_C)
        per_body = UNROLL * len(W_PARTS)
        rounds = per_body // W_SLOTS
        nth = lambda i, m: i * rounds + (m // W_SLOTS + 1)
        for first in (*multiplied, s["hidden"], s["stored"]):
            first.advance(1)
        sb = lambda name, shape: self.sbuf(scope, name, shape)
        w = self.expert_w
        sig, hid = sb("expert_sigmoid", [P, 2, 4 * M]), sb("expert_hidden", [P, 2, 4 * M])
        hidden = hid[:, :, :].rearrange("p h (f m) -> p (h f) m", f=4)
        with nc.Block() as block:
            @block.sync
            def _(sp):
                def load(i, m):
                    slot = m % W_SLOTS
                    sp.wait_ge(multiplied[slot].sem, multiplied[slot] + (nth(i, m) - 1))
                    self.load_expert_part(sp, l, (i + m // per_body) * UNROLL + m % per_body // len(W_PARTS), m)

                with sp.Fori(0, E_N // UNROLL - 1) as i:
                    for m in range(W_AHEAD, per_body + W_AHEAD):
                        load(i, m)
                for m in range(W_AHEAD, per_body):
                    load(E_N // UNROLL - 1, m)

            @block.tensor
            def _(pe):
                def to_features(i, m, bank, tokens):
                    for h in range(2):
                        slot = (m + h) % W_SLOTS
                        pe.wait_ge(landed[slot].sem, landed[slot] + nth(i, m + h))
                        for f in range(4):
                            for k in range(KD):
                                mm = pe.matmul(self.psum[:, bank + h, f * M:(f + 1) * M], w[:, slot, k, f * P:(f + 1) * P],
                                               tokens(k), start=(k == 0), stop=(k == KD - 1))
                        mm.then_inc(multiplied[slot].sem, 1)

                def to_tokens(i, n, m, bank):
                    for h in range(2):
                        slot = (m + h) % W_SLOTS
                        pe.wait_ge(landed[slot].sem, landed[slot] + nth(i, m + h))
                        for k in range(KD):
                            if h == 0 and k % 4 == 0:
                                pe.wait_ge(s["hidden"].sem, s["hidden"] + (n * 2 + (k // 4 + 1)))
                            mm = pe.matmul(self.psum[0:M, bank + h, :], hidden[:, k, :], w[:, slot, k, :],
                                           start=(k == 0), stop=(k == KD - 1))
                        mm.then_inc(multiplied[slot].sem, 1)

                for slot in range(W_SLOTS):
                    pe.matmul(self.psum[0:1, 2, 511:512], self.c("ident")[:, 0:1], self.c("ident")[:, 0:1],
                              start=True, stop=True).then_inc(multiplied[slot].sem, 1)
                with pe.Fori(0, E_N // UNROLL) as i:
                    for j in range(UNROLL):
                        n, m = i * UNROLL + j, j * len(W_PARTS)
                        tokens = lambda k: self.chosen[:, bass.ds(n, 1), k, :].rearrange("p e m -> p (e m)")
                        to_features(i, m, 2, tokens)
                        to_features(i, m + 2, 4, tokens)
                        pe.wait_ge(s["stored"].sem, s["stored"] + n)
                        to_tokens(i, n, m + 4, 6)

            @block.scalar
            def _(act):
                act.copy(self.stat[0:1, 0:1], self.c("iota")[0:1, 0:1]).then_inc(s["stored"].sem, 1)
                with act.Fori(0, E_N // UNROLL) as i:
                    for j in range(UNROLL):
                        n, m = i * UNROLL + j, j * len(W_PARTS)
                        act.wait_ge(s["hidden"].sem, s["hidden"] + n * 2)
                        for h in range(2):
                            gate = multiplied[(m + h) % W_SLOTS]
                            act.wait_ge(gate.sem, gate + nth(i, m + h))
                            act.activation(sig[:, h, :], self.psum[:, 2 + h, 0:4 * M], ACT.Sigmoid).then_inc(s["sigmoid"].sem, 1)
                        down = multiplied[(m + 5) % W_SLOTS]
                        act.wait_ge(down.sem, down + nth(i, m + 5))
                        y, e = self.flat[:, 3072:4096], j % 2
                        ins = act.copy(self.y_lat[64 * e:64 * e + 64, bass.ds(i * 2 + j // 2, 1), :].rearrange("p a n -> p (a n)"),
                                       y[0:CAP_L, :])
                        if not last:
                            ins = act.copy(self.y_ctx[32 * j:32 * j + 32, bass.ds(i, 1), :].rearrange("p a n -> p (a n)"),
                                           y[CAP_L:M, :])
                        ins.then_inc(s["stored"].sem, 1)

            @block.vector
            def _(dve):
                dve.memset(self.stat[0:1, 1:2], 0.0).then_inc(s["hidden"].sem, 1)
                with dve.Fori(0, E_N // UNROLL) as i:
                    for j in range(UNROLL):
                        n, m = i * UNROLL + j, j * len(W_PARTS)
                        for h in range(2):
                            dve.wait_ge(s["sigmoid"].sem, s["sigmoid"] + (n * 2 + (h + 1)))
                            dve.tensor_tensor(sig[:, h, :], sig[:, h, :], self.psum[:, 2 + h, 0:4 * M], ALU.mult).then_inc(s["gated"].sem, 1)
                        for h in range(2):
                            dve.wait_ge(s["gated"].sem, s["gated"] + (n * 2 + (h + 1)))
                            up = multiplied[(m + 2 + h) % W_SLOTS]
                            dve.wait_ge(up.sem, up + nth(i, m + 2 + h))
                            dve.tensor_tensor(hid[:, h, :], sig[:, h, :], self.psum[:, 4 + h, 0:4 * M], ALU.mult).then_inc(s["hidden"].sem, 1)
        for slot in range(W_SLOTS):
            landed[slot].advance(rounds * E_N // UNROLL)
            multiplied[slot].advance(rounds * E_N // UNROLL)
        for n in names:
            s[n].advance(E_N * (1 if n == "stored" else 2))

    def combine(self, l, last, tiles):
        nc = self.nc
        names = ("weights", "turned", "copied", "made", "added")
        s = {n: self.count("combine_" + n) for n in names}
        groups = [(CT, NT, g, 2, CAP_L) for g in range(E_N // 2)] + \
                 ([] if last else [(0, CT, g, 4, CAP_C) for g in range(E_N // 4)])
        with ExitStack() as scope:
            sb = lambda name, shape: self.sbuf(scope, name, shape)
            hot = sb("weighted_onehot", [P, 2, LAT])
            spare = self.expert_w[:, :, :, :].rearrange("p s k n -> p (s k n)")
            back_l = spare[:, 0:E_N // 2 * LAT].rearrange("p (g t) -> p g t", t=LAT)
            back_c = spare[:, 4096:4096 + E_N // 4 * CTX].rearrange("p (g t) -> p g t", t=CTX)
            tmp = sb("gated_experts", [P, D])
            block = scope.enter_context(nc.Block())

            @block.tensor
            def _(pe):
                for n, (a, b, g, per, cap) in enumerate(groups):
                    pe.wait_ge(s["weights"].sem, s["weights"] + (n + 1))
                    if n >= 2:
                        pe.wait_ge(s["copied"].sem, s["copied"] + (n - 1))
                    for t in range(b - a):
                        mm = pe.transpose(self.psum[:, 4 + n % 2, t * P:(t + 1) * P], hot[:, n % 2, t * P:(t + 1) * P], self.c("ident"))
                    mm.then_inc(s["turned"].sem, 1)
                pe.wait_ge(s["copied"].sem, s["copied"] + len(groups))
                for n, t in enumerate(tiles):
                    if n >= 2:
                        pe.wait_ge(s["added"].sem, s["added"] + (n - 1))
                    back, y, k, t0 = (back_c, self.y_ctx, E_N // 4, t) if t < CT else (back_l, self.y_lat, E_N // 2, t - CT)
                    for b in range(2):
                        for g in range(k):
                            mm = pe.matmul(self.psum[:, 2 * (n % 2) + b, :], back[:, g, t0 * P:(t0 + 1) * P],
                                           y[:, g, b * 512:(b + 1) * 512], start=(g == 0), stop=(g == k - 1))
                    mm.then_inc(s["made"].sem, 1)

            @block.scalar
            def _(act):
                for n, (a, b, g, per, cap) in enumerate(groups):
                    act.wait_ge(s["turned"].sem, s["turned"] + (n + 1))
                    to = (back_c if a < CT else back_l)[:, g, :]
                    act.copy(to, self.psum[:, 4 + n % 2, 0:(b - a) * P]).then_inc(s["copied"].sem, 1)

            @block.vector
            def _(dve):
                link = self.dve_chain.on(dve)
                for n, (a, b, g, per, cap) in enumerate(groups):
                    if n >= 2:
                        dve.wait_ge(s["turned"].sem, s["turned"] + (n - 1))
                    to = hot[:, n % 2, 0:(b - a) * P].rearrange("p (t e c) -> p t e c", e=per, c=cap)
                    of = lambda x: spread(x[:, a:b, g * per:(g + 1) * per], 3, cap)
                    iota = spread(spread(self.c("iota")[:, 0:cap], 1, per), 1, b - a)
                    link(dve.tensor_tensor(to, iota, of(self.slot), ALU.is_equal))
                    dve.tensor_tensor(to, to, of(self.aff), ALU.mult).then_inc(s["weights"].sem, 1)
                self.add_gated(dve, tmp, 1, tiles, s["made"], s["added"])
        for n in names:
            s[n].advance(len(tiles) if n in ("made", "added") else len(groups))

    def store(self):
        nc, io = self.nc, self.io
        stored = self.count("output_stored", 16)
        with nc.Block() as block:
            @block.sync
            def _(sp):
                sp.dma_start(io["out"].rearrange("(t p) d -> p t d", p=P), self.x[:, CT:NT, :]).then_inc(stored.sem, 16)
                sp.wait_ge(stored.sem, stored + 1)


_WHOLE = ["mod_w", "w_in", "mla_w_uq", "mla_w_ukv", "rwkv_w2", "rwkv_a2", "rwkv_g2", "w_out", "router_w",
          "exp_w_gate", "exp_w_up", "exp_w_down"]


def _by_feature(a):
    return np.asarray(a).reshape(-1, P).T


def kernel(**inputs):
    import concourse.bacc as bacc
    from concourse.bass_utils import run_bass_kernel_spmd

    a = {k: np.asarray(v) for k, v in inputs.items()}
    cols, rows = [], []
    for l in range(DEPTH):
        mu = np.zeros(9 * P, np.float32)
        mu[0:896], mu[896:960], mu[1024:1152] = a["rwkv_mu"][l, 0:896], a["rwkv_mu"][l, 896:960], a["rwkv_mu"][l, 960:1088]
        cols.append(np.concatenate([_by_feature(x) for x in (
            a["mod_b"][l], a["norm1_w"][l], a["norm2_w"][l],
            np.concatenate([a["mla_q_norm_w"][l], a["mla_kv_norm_w"][l]]), mu, a["rwkv_w0"][l], a["rwkv_a0"][l],
            a["rwkv_k_k"][l], a["rwkv_k_a"][l], a["rwkv_r_k"][l])], 1))
        ln = a["rwkv_ln_w"][l].reshape(2, 2, 64)
        row = [a["mla_q_gain"][l], a["mla_k_gain"][l], a["ret_decay"][l].reshape(-1), a["ret_gn_w"][l]]
        rows.append(np.concatenate(
            [np.broadcast_to(np.concatenate(row), (P, ROWS_N - 128)),
             np.concatenate([np.broadcast_to(ln[:, e].reshape(-1), (64, 128)) for e in range(2)], 0)], 1))
    base, retc, rwkvc = constants()
    arrays = {"x": a["x"][0], "ctx": a["ctx"][0],
              "cvec": np.stack([_by_feature(a["c"][0]), _by_feature(a["c_ctx"])], 2),
              "cols": np.stack(cols), "rows": np.stack(rows), "base": base, "retc": retc, "rwkvc": rwkvc}
    for name in _WHOLE:
        arrays[name] = a[name]
    nc = bacc.Bacc("TRN2", target_bir_lowering=False, num_devices=1)
    io, fed = {}, {}
    for name, x in arrays.items():
        x = np.ascontiguousarray(x)
        fed[f"in_{name}"] = x
        io[name] = nc.dram_tensor(f"in_{name}", x.shape, mybir.dt.from_np(x.dtype), kind="ExternalInput").ap()
    io["out"] = nc.dram_tensor("out_0", (LAT, D), F32, kind="ExternalOutput").ap()
    build(nc, io)
    r = run_bass_kernel_spmd(nc, [fed], core_ids=[0])
    return r.results[0]["out_0"].reshape(1, LAT, D)
```

```python
from contextlib import ExitStack

import numpy as np

import concourse.bass as bass
from concourse import mybir

P = 128
D = 1024
KD = D // P
LAT, CTX = 512, 256
TOK = LAT + CTX
CT, NT = CTX // P, TOK // P
DEPTH = 2
EPS = 1e-6

HEADS, NOPE, ROPE, QK, VD = 8, 64, 32, 96, 64
QR, KVR = 384, 256
MLA_COLS = QR + KVR + ROPE
RET_COLS = 1024
RWKV_COLS = 1088
IN_COLS = MLA_COLS + RET_COLS + RWKV_COLS
C = 64
NCH = TOK // C
CCH = CTX // C
DECAY = -0.606531
E_N, CAP_L, CAP_C = 16, 64, 32
LEVELS = (2, 4, 8, 16, 32)
W_SLOTS, W_AHEAD = 3, 2
W_PARTS = tuple((name, half) for name in ("exp_w_gate", "exp_w_up", "exp_w_down") for half in range(2))

F32 = mybir.dt.float32
ALU = mybir.AluOpType
ACT = mybir.ActivationFunctionType
AX = mybir.AxisListType.X


def packed(widths):
    at, out = 0, {}
    for name, n in widths:
        out[name] = (at, at + n)
        at += n
    return out, at


BASE, BASE_N = packed([
    ("ident", 128), ("ones", 128), ("pair_ones", 128), ("ident64", 64), ("iota", 64),
    ("axial_cos", 4 * 16), ("axial_sin", 4 * 16)])
RETC, RETC_N = packed([
    ("seq_cos", 6 * 32), ("seq_sin", 6 * 32),
    ("dist", 896), ("after", 896), ("before", 896), ("dist_f", 640), ("dist_b", 640)])
RWKVC, RWKVC_N = packed([
    ("mask", 4 * 2 * 64), ("first_t", 4 * 64), ("level", len(LEVELS) * 4 * 64),
    ("restart", TOK)])
COLS, COLS_N = packed([
    ("mod_b", 48), ("norm1", 8), ("norm2", 8), ("cn", 5), ("mu", 9), ("w0", 4), ("a0", 2),
    ("k_k", 2), ("k_a", 2), ("r_k", 2)])
ROWS, ROWS_N = packed([("qk_gain", 2 * 96), ("decay", 8), ("gn_w", 256), ("ln_w", 128)])


def constants():
    p = np.arange(P)[:, None]
    packs = [(names, np.zeros((P, n), np.float32)) for names, n in
             ((BASE, BASE_N), (RETC, RETC_N), (RWKVC, RWKVC_N))]

    def put(name, a):
        for names, out in packs:
            if name in names:
                lo, hi = names[name]
                out[:, lo:hi] = np.broadcast_to(np.asarray(a, np.float32).reshape(a.shape[0], -1), (P, hi - lo))

    put("ident", np.eye(P))
    put("ones", np.ones((P, P)))
    put("pair_ones", (p // 64 == np.arange(P) // 64))
    put("ident64", (p % 64 == np.arange(64)))
    put("iota", np.arange(64)[None])
    row = np.repeat(np.arange(LAT // 64, dtype=np.float32), 64)
    col = np.tile(np.arange(64, dtype=np.float32), LAT // 64)
    inv = (np.float32(10000.0) ** (-np.arange(8, dtype=np.float32) / 8)).astype(np.float32)
    ang = np.concatenate([row[:, None] * inv, col[:, None] * inv], -1)
    by_tile = lambda a: a.reshape(-1, P, a.shape[-1]).transpose(1, 0, 2)
    put("axial_cos", by_tile(np.cos(ang)))
    put("axial_sin", by_tile(np.sin(ang)))
    inv = (np.float32(10000.0) ** (-np.linspace(0.0, 1.0, 32, dtype=np.float32))).astype(np.float32)
    ang = np.arange(TOK, dtype=np.float32)[:, None] * inv
    put("seq_cos", by_tile(np.cos(ang)))
    put("seq_sin", by_tile(np.sin(ang)))
    d = np.arange(896)[None] - 384 - p
    put("dist", np.abs(d))
    put("after", d >= 0)
    put("before", d <= 0)
    d = np.arange(640)[None] - 128 - p
    put("dist_f", CTX + d)
    put("dist_b", LAT - d)
    s, t = (p % 64)[:, :, None], np.arange(64)[None, None]
    sign = np.array([1, 1, -1, -1])[None, :, None]
    gap = (t - s) * sign
    put("mask", np.stack([gap > 0, gap >= 0], 2))
    pairs = (s // 2 == t // 2) & (gap > 0)
    put("first_t", pairs)
    put("level", np.stack([(s // (2 * m) == t // (2 * m)) & (s // m != t // m) & (gap > 0)
                           for m in LEVELS], 1))
    put("restart", (np.arange(TOK) % C != 0)[None])
    return [out for _, out in packs]


def build(nc, io):
    with ExitStack() as kernel_scope:
        Program(nc, io, kernel_scope).run()


class Count:

    def __init__(self, sem, step=1):
        self.sem, self.step, self.base = sem, step, 0

    def __add__(self, k):
        return self.base + self.step * k

    def advance(self, k):
        self.base += self.step * k


class Chain:

    def __init__(self, sem):
        self.sem, self.n = sem, 0

    def on(self, eng):
        def link(ins):
            self.n += 1
            ins.then_inc(self.sem, 1)
            eng.wait_ge(self.sem, self.n)
        return link


def spread(ap, axis, n):
    a = ap.unsqueeze(axis)
    shape = list(a.shape)
    shape[axis] = n
    return a.broadcast_to(shape)


class Program:
    def __init__(self, nc, io, scope):
        self.nc, self.io, self.scope = nc, io, scope
        self.counts, self.n_tensors = {}, 0
        self.dve_chain = Chain(scope.enter_context(nc.semaphore("dve_chain")))
        self.act_chain = Chain(scope.enter_context(nc.semaphore("act_chain")))
        sb = lambda name, shape: self.sbuf(scope, name, shape)
        self.base = sb("base", [P, BASE_N])
        self.cols = sb("cols", [P, COLS_N])
        self.rows = sb("rows", [P, ROWS_N])
        self.x = sb("x_tokens", [P, NT, D])
        self.cvec = sb("cvec", [P, KD, 2])
        self.silu_c = sb("silu_c", [P, KD, 2])
        self.mod = sb("mod", [P, 48, 2])
        self.scale1 = sb("scale1", [P, KD, 2])
        self.scale2 = sb("scale2", [P, KD, 2])
        self.gates = sb("gates", [P, 2, 2, D])
        self.stat = sb("stat", [P, 64])
        self.psum = scope.enter_context(nc.psum_tensor("psum", [P, 8, 512], F32))
        self.flat = self.psum[:, :, :].rearrange("p b n -> p (b n)")

    def sbuf(self, scope, name, shape):
        self.n_tensors += 1
        return scope.enter_context(self.nc.sbuf_tensor(f"{name}_{self.n_tensors}", shape, F32))

    def count(self, name, step=1):
        if name not in self.counts:
            self.counts[name] = Count(self.scope.enter_context(self.nc.semaphore(name)), step)
        return self.counts[name]

    def c(self, name):
        lo, hi = BASE[name]
        return self.base[:, lo:hi]

    def col(self, name):
        lo, hi = COLS[name]
        return self.cols[:, lo:hi]

    def row(self, name):
        lo, hi = ROWS[name]
        return self.rows[:, lo:hi]

    def run(self):
        self.load_inputs()
        for layer in range(DEPTH):
            last = layer == DEPTH - 1
            self.modulation(layer)
            tiles = list(range(CT if last else 0, NT))
            with ExitStack() as mixer_scope:
                self.mix_t = self.sbuf(mixer_scope, "mix_t", [P, KD, TOK])
                with ExitStack() as scope:
                    self.u_t = self.sbuf(scope, "u_t", [P, KD, TOK])
                    with ExitStack() as weight_scope:
                        self.w_in = self.sbuf(weight_scope, "w_in", [P, KD, RET_COLS])
                        with ExitStack() as inner:
                            self.xn = self.sbuf(inner, "xn", [P, NT, D])
                            self.normalise(layer, "norm1", self.scale1, 0, list(range(NT)),
                                           lambda sp: self.load_attention_weights(sp, layer))
                        self.attention(layer, last)
                        self.retention(layer, last)
                    self.rwkv(layer, last)
                self.project_out(layer, last, tiles)
            with ExitStack() as scope:
                per_expert = CAP_L + (0 if last else CAP_C)
                self.slot = self.sbuf(scope, "slot", [P, NT, E_N])
                self.aff = self.sbuf(scope, "aff", [P, NT, E_N])
                self.chosen = self.sbuf(scope, "chosen_tokens", [P, E_N, KD, per_expert])
                with ExitStack() as loop_scope:
                    self.expert_w = self.sbuf(loop_scope, "expert_w", [P, W_SLOTS, KD, 512])
                    with ExitStack() as inner:
                        self.xn = self.sbuf(inner, "xn", [P, NT, D])
                        with ExitStack() as innermost:
                            self.u_t = self.sbuf(innermost, "h_t", [P, KD, TOK])
                            self.normalise(layer, "norm2", self.scale2, 24, tiles)
                            self.route(layer, last, tiles)
                        self.gather(layer, last)
                    self.y_lat = self.sbuf(loop_scope, "y_lat", [P, E_N // 2, D])
                    self.y_ctx = None if last else self.sbuf(loop_scope, "y_ctx", [P, E_N // 4, D])
                    with ExitStack() as inner:
                        self.experts(layer, last, inner)
                    self.combine(layer, last, tiles)
        self.store()

    def load_inputs(self):
        nc, io = self.nc, self.io
        landed, sig, done = self.count("inputs_landed", 16), self.count("silu_sigmoid"), self.count("silu_done")
        with nc.Block() as block:
            @block.sync
            def _(sp):
                sp.dma_start(self.cvec[:, :, :], io["cvec"]).then_inc(landed.sem, 16)
                sp.dma_start(self.base[:, :], io["base"]).then_inc(landed.sem, 16)
                sp.dma_start(self.x[:, 0:CT, :], io["ctx"].rearrange("(t p) d -> p t d", p=P)).then_inc(landed.sem, 16)
                sp.dma_start(self.x[:, CT:NT, :], io["x"].rearrange("(t p) d -> p t d", p=P)).then_inc(landed.sem, 16)
                sp.wait_ge(landed.sem, landed + 4)

            @block.scalar
            def _(act):
                act.wait_ge(landed.sem, landed + 4)
                act.activation(self.silu_c[:, :, :], self.cvec[:, :, :], ACT.Sigmoid).then_inc(sig.sem, 1)

            @block.vector
            def _(dve):
                dve.wait_ge(sig.sem, sig + 1)
                dve.tensor_tensor(self.silu_c[:, :, :], self.silu_c[:, :, :], self.cvec[:, :, :],
                                  ALU.mult).then_inc(done.sem, 1)

    def modulation(self, l):
        nc, io = self.nc, self.io
        small = self.count("layer_vectors_landed", 16)
        SLOTS, PARTS = 4, 12
        landed = [self.count(f"mod_w_landed{i}", 16) for i in range(SLOTS)]
        made, copied, turned, summed = (self.count("mod_" + n) for n in ("made", "copied", "turned", "summed"))
        vector_parts = list(range(1, PARTS, 3))
        order = [part for j in vector_parts for part in (j - 1, j + 1, j)]
        done_at = {j: n for n, j in enumerate(order)}
        diag_ready, spread_done, gate_copied = (self.count(n) for n in ("gate_diag", "gate_spread", "gate_copied"))
        with ExitStack() as scope:
            w = self.sbuf(scope, "mod_w", [P, SLOTS, KD, 512])
            rows = self.sbuf(scope, "mod_rows", [2, PARTS, 512])
            diag = self.sbuf(scope, "gate_diagonals", [P, 2, 4, P])
            junk = self.sbuf(scope, "squares", [P, D])
            sums = self.sbuf(scope, "mod_sums", [P, 2, 2, 512])
            pick = self.sbuf(scope, "vector_columns", [P, 2, 2])
            block = scope.enter_context(nc.Block())

            @block.sync
            def _(sp):
                for j in range(PARTS):
                    if j >= SLOTS:
                        held = j - SLOTS
                        if held in vector_parts:
                            sp.wait_ge(summed.sem, summed + (held // 3 + 1))
                        else:
                            sp.wait_ge(made.sem, made + (done_at[held] + 1))
                    sp.dma_start(w[:, j % SLOTS, :, :], io["mod_w"][l, :, j * 512:(j + 1) * 512].rearrange("(k p) n -> p k n", p=P)
                                 ).then_inc(landed[j % SLOTS].sem, 16)
                    if j == SLOTS - 1:
                        sp.dma_start(self.cols[:, :], io["cols"][l]).then_inc(small.sem, 16)
                        sp.dma_start(self.rows[:, :], io["rows"][l]).then_inc(small.sem, 16)
                sp.wait_ge(small.sem, small + 2)

            @block.tensor
            def _(pe):
                for n, j in enumerate(order):
                    if n >= 2:
                        pe.wait_ge(copied.sem, copied + (n - 1))
                    if j in vector_parts:
                        pe.wait_ge(summed.sem, summed + (j // 3 + 1))
                        for s in range(2):
                            mm = pe.matmul(self.psum[0:2, 3 + n % 2, :], pick[:, s, :], sums[:, j // 3 % 2, s, :],
                                           start=(s == 0), stop=(s == 1))
                    else:
                        pe.wait_ge(landed[j % SLOTS].sem, landed[j % SLOTS] + (j // SLOTS + 1))
                        for k in range(KD):
                            mm = pe.matmul(self.psum[0:2, 3 + n % 2, :], self.silu_c[:, k, :], w[:, j % SLOTS, k, :],
                                           start=(k == 0), stop=(k == KD - 1))
                    mm.then_inc(made.sem, 1)
                pe.wait_ge(copied.sem, copied + PARTS)
                for j in range(48):
                    mm = pe.transpose(self.flat[:, 2 * j:2 * j + 2], rows[:, j // 4, (j % 4) * P:(j % 4 + 1) * P],
                                      self.c("ident")[0:2, 0:2])
                mm.then_inc(turned.sem, 1)
                for n in range(8):
                    pe.wait_ge(diag_ready.sem, diag_ready + (n + 1))
                    if n >= 2:
                        pe.wait_ge(gate_copied.sem, gate_copied + (n - 1))
                    pe.matmul(self.psum[:, 1 + n % 2, :], self.c("ones"),
                              diag[:, n % 2, :, :].rearrange("p a b -> p (a b)"), start=True, stop=True
                              ).then_inc(spread_done.sem, 1)

            @block.scalar
            def _(act):
                if l == 0:
                    self.sum_squares(act, junk[:, :], list(range(NT)))
                for n, j in enumerate(order):
                    act.wait_ge(made.sem, made + (n + 1))
                    act.copy(rows[:, j, :], self.psum[0:2, 3 + n % 2, :]).then_inc(copied.sem, 1)
                for n in range(8):
                    g, s, half = n // 4, n // 2 % 2, n % 2
                    act.wait_ge(spread_done.sem, spread_done + (n + 1))
                    act.copy(self.gates[:, g, s, half * 512:(half + 1) * 512],
                             self.psum[:, 1 + n % 2, :]).then_inc(gate_copied.sem, 1)

            @block.vector
            def _(dve):
                link = self.dve_chain.on(dve)
                link(dve.memset(pick[:, :, :], 0.0))
                for s in range(2):
                    dve.memset(pick[:, s, s:s + 1], 1.0)
                for j in vector_parts:
                    dve.wait_ge(landed[j % SLOTS].sem, landed[j % SLOTS] + (j // SLOTS + 1))
                    if j >= vector_parts[2]:
                        dve.wait_ge(made.sem, made + (done_at[j - 6] + 1))
                    for k in range(KD):
                        for s in range(2):
                            to, part, c = sums[:, j // 3 % 2, s, :], w[:, j % SLOTS, k, :], self.silu_c[:, k, s:s + 1]
                            if k == 0:
                                ins = dve.tensor_scalar(to, part, c, None, ALU.mult)
                            else:
                                ins = dve.scalar_tensor_tensor(to, part, c, to, ALU.mult, ALU.add)
                        if k < KD - 1:
                            link(ins)
                    ins.then_inc(summed.sem, 1)
                dve.wait_ge(small.sem, small + 2)
                dve.wait_ge(turned.sem, turned + 1)
                link(dve.tensor_tensor(self.mod[:, :, :], self.flat[:, 0:96].rearrange("p (j s) -> p j s", s=2),
                                       spread(self.col("mod_b"), 2, 2), ALU.add))
                for n in range(8):
                    g, s, half = n // 4, n // 2 % 2, n % 2
                    j = (16, 40)[g] + 4 * half
                    if n >= 2:
                        dve.wait_ge(spread_done.sem, spread_done + (n - 1))
                    dve.tensor_tensor(diag[:, n % 2, :, :], spread(self.c("ident"), 1, 4),
                                      spread(self.mod[:, j:j + 4, s], 2, P), ALU.mult).then_inc(diag_ready.sem, 1)
                for scale, j, name in ((self.scale1, 8, "norm1"), (self.scale2, 32, "norm2")):
                    link(dve.tensor_scalar(scale[:, :, :], self.mod[:, j:j + 8, :], 1.0, None, ALU.add))
                    link(dve.tensor_tensor(scale[:, :, :], scale[:, :, :], spread(self.col(name), 2, 2), ALU.mult))
        small.advance(2)
        made.advance(PARTS)
        copied.advance(PARTS)
        summed.advance(len(vector_parts))
        turned.advance(1)
        for slot in landed:
            slot.advance(PARTS // SLOTS)
        for s in (diag_ready, spread_done, gate_copied):
            s.advance(8)

    def normalise(self, l, name, scale, shift, tiles, load_ahead=None):
        nc = self.nc
        mean, root, inverse = (self.count(f"norm_{n}") for n in ("mean", "root", "inverse"))
        normed = [self.count("norm_rows_" + e) for e in ("dve", "act")]
        modulated = [self.count("norm_modulated_" + e) for e in ("dve", "act")]
        turned = self.count("norm_turned")
        n, BANKS = len(tiles), 8
        ss, rs = self.stat[:, 0:NT], self.stat[:, 8:8 + NT]
        groups = [(1, [t for t in tiles if t < CT]), (0, [t for t in tiles if t >= CT])]
        items = [(k, s, ts) for k in range(KD) for s, ts in groups if ts]
        with ExitStack() as scope:
            block = scope.enter_context(nc.Block())

            if load_ahead:
                @block.sync
                def _(sp):
                    load_ahead(sp)

            @block.scalar
            def _(act):
                act.wait_ge(mean.sem, mean + 1)
                act.activation(rs[:, tiles[0]:NT], ss[:, tiles[0]:NT], ACT.Sqrt).then_inc(root.sem, 1)
                act.wait_ge(inverse.sem, inverse + 1)
                for t in tiles[1::2]:
                    act.activation(self.xn[:, t, :], self.x[:, t, :], ACT.Identity, scale=rs[:, t:t + 1]
                                   ).then_inc(normed[1].sem, 1)
                for i, (k, s, ts) in list(enumerate(items))[1::2]:
                    act.wait_ge(turned.sem, turned + (i + 1))
                    act.activation(self.u_t[:, k, ts[0] * P:(ts[-1] + 1) * P], self.psum[:, i % BANKS, 0:len(ts) * P],
                                   ACT.Identity, bias=self.mod[:, shift + k, s:s + 1],
                                   scale=scale[:, k, s:s + 1]).then_inc(modulated[1].sem, 1)

            @block.vector
            def _(dve):
                dve.tensor_scalar(ss[:, tiles[0]:NT], ss[:, tiles[0]:NT], 1.0 / D, EPS, ALU.mult, ALU.add
                                  ).then_inc(mean.sem, 1)
                dve.wait_ge(root.sem, root + 1)
                dve.reciprocal(rs[:, tiles[0]:NT], rs[:, tiles[0]:NT]).then_inc(inverse.sem, 1)
                dve.wait_ge(inverse.sem, inverse + 1)
                for t in tiles[0::2]:
                    dve.tensor_scalar(self.xn[:, t, :], self.x[:, t, :], rs[:, t:t + 1], None,
                                      ALU.mult).then_inc(normed[0].sem, 1)
                for i, (k, s, ts) in list(enumerate(items))[0::2]:
                    dve.wait_ge(turned.sem, turned + (i + 1))
                    dve.tensor_scalar(self.u_t[:, k, ts[0] * P:(ts[-1] + 1) * P], self.psum[:, i % BANKS, 0:len(ts) * P],
                                      scale[:, k, s:s + 1], self.mod[:, shift + k, s:s + 1],
                                      ALU.mult, ALU.add).then_inc(modulated[0].sem, 1)

            @block.tensor
            def _(pe):
                for side in normed:
                    pe.wait_ge(side.sem, side + n // 2)
                for i, (k, s, ts) in enumerate(items):
                    if i >= BANKS:
                        pe.wait_ge(modulated[i % 2].sem, modulated[i % 2] + ((i - BANKS) // 2 + 1))
                    for a, t in enumerate(ts):
                        mm = pe.transpose(self.psum[:, i % BANKS, a * P:(a + 1) * P], self.xn[:, t, k * P:(k + 1) * P],
                                          self.c("ident"))
                    mm.then_inc(turned.sem, 1)
        for once in (mean, root, inverse):
            once.advance(1)
        for side in normed:
            side.advance(n // 2)
        for side in modulated:
            side.advance(len(items) // 2)
        turned.advance(len(items))

    def sum_squares(self, act, junk, tiles, added=None):
        link = self.act_chain.on(act)
        for n, t in enumerate(tiles):
            if added:
                act.wait_ge(added.sem, added + (n + 1))
            link(act.activation(junk, self.x[:, t, :], ACT.Square, accum_out=self.stat[:, t:t + 1]))

    def attention_weights(self):
        flat = self.w_in[:, :, :].rearrange("p k n -> p (k n)")
        spare = self.mix_t[:, :, :].rearrange("p k n -> p (k n)")
        n_q, n_kv = HEADS * QK, HEADS * (NOPE + VD)
        return (flat[:, 0:KD * MLA_COLS].rearrange("p (k n) -> p k n", k=KD),
                spare[:, 0:3 * n_q].rearrange("p (k n) -> p k n", k=3),
                spare[:, 3 * n_q:3 * n_q + 2 * n_kv].rearrange("p (k n) -> p k n", k=2))

    def load_attention_weights(self, sp, l):
        io, landed = self.io, self.count("mla_weights_landed", 16)
        w, wq, wkv = self.attention_weights()
        sp.dma_start(w, io["w_in"][l, :, 0:MLA_COLS].rearrange("(k p) n -> p k n", p=P)).then_inc(landed.sem, 16)
        sp.dma_start(wq, io["mla_w_uq"][l].rearrange("(k p) n -> p k n", p=P)).then_inc(landed.sem, 16)
        sp.dma_start(wkv, io["mla_w_ukv"][l].rearrange("(k p) n -> p k n", p=P)).then_inc(landed.sem, 16)

    def attention(self, l, last):
        nc = self.nc
        landed = self.count("mla_weights_landed", 16)
        names = ("projected", "squares", "mean", "root", "latents", "latents_turned", "latents_t", "q_made",
                 "kv_made", "q_copied", "kv_copied", "rope_copied", "head_mean", "head_root", "heads_normed",
                 "q_turned", "k_turned", "q_t", "k_t")
        s = {n: self.count("mla_" + n) for n in names}
        with ExitStack() as att_scope:
            sb = lambda name, shape: self.sbuf(att_scope, name, shape)
            q_t, k_t = sb("q_t", [QK, HEADS, TOK]), sb("k_t", [QK, HEADS, TOK])
            v = sb("v", [P, NT, HEADS, VD])
            with ExitStack() as scope:
                sb = lambda name, shape: self.sbuf(scope, name, shape)
                w, wq, wkv = self.attention_weights()
                spare = self.w_in[:, :, :].rearrange("p k n -> p (k n)")[:, KD * MLA_COLS:]
                n_sq = 2 * HEADS * QK
                sq = spare[:, 0:n_sq].rearrange("p (a h d) -> p a h d", a=2, h=HEADS)
                lat = spare[:, n_sq:n_sq + MLA_COLS]
                junk = spare[:, n_sq + MLA_COLS:n_sq + MLA_COLS + QR]
                lat_t = sb("latents_t", [P, 5, P])
                qk = sb("qk_rows", [P, 2, 2, HEADS, QK])
                turn = sb("rope_parts", [P, 4, 2 * HEADS, 16])
                st = self.stat
                block = scope.enter_context(nc.Block())
                pa, pt = self.flat[:, 0:MLA_COLS], self.flat[:, 1024:1024 + 640].rearrange("p (a n) -> p a n", n=P)
                pq, pkv = self.flat[:, 2048:2048 + 768], self.flat[:, 3072:4096].rearrange("p (h d) -> p h d", h=HEADS)
                ph = self.psum[0:QK, 2:4, :].rearrange("p b (a n) -> p (b a) n", n=P)

                @block.tensor
                def _(pe):
                    def project(t, lo, hi):
                        for k in range(KD):
                            mm = pe.matmul(pa[:, lo:hi], self.u_t[:, k, t * P:(t + 1) * P], w[:, k, lo:hi],
                                           start=(k == 0), stop=(k == KD - 1))
                        return mm

                    def make_q(t):
                        pe.wait_ge(s["latents_t"].sem, s["latents_t"] + (t + 1))
                        if t >= 1:
                            pe.wait_ge(s["q_copied"].sem, s["q_copied"] + t)
                        for lo, hi in ((0, 512), (512, 768)):
                            for k in range(3):
                                mm = pe.matmul(pq[:, lo:hi], lat_t[:, k, :], wq[:, k, lo:hi], start=(k == 0), stop=(k == 2))
                        mm.then_inc(s["q_made"].sem, 1)

                    def make_kv(t):
                        if t >= 1:
                            pe.wait_ge(s["kv_copied"].sem, s["kv_copied"] + t)
                        for b in range(2):
                            for k in range(2):
                                mm = pe.matmul(self.psum[:, 6 + b, :], lat_t[:, 3 + k, :], wkv[:, k, b * 512:(b + 1) * 512],
                                               start=(k == 0), stop=(k == 1))
                        mm.then_inc(s["kv_made"].sem, 1)

                    def turn_heads(t, a):
                        for h in range(HEADS):
                            mm = pe.transpose(ph[:, h, :], qk[:, t % 2, a, h, :], self.c("ident"))
                        mm.then_inc(s[("q_turned", "k_turned")[a]].sem, 1)

                    pe.wait_ge(landed.sem, landed + 3)
                    for t in range(NT):
                        if t == 0:
                            project(t, 0, 512)
                            project(t, 512, MLA_COLS).then_inc(s["projected"].sem, 1)
                        pe.wait_ge(s["latents"].sem, s["latents"] + (t + 1))
                        if t + 1 < NT:
                            project(t + 1, 0, 512)
                        if t >= 2:
                            pe.wait_ge(s["k_t"].sem, s["k_t"] + (t - 1))
                        for a in range(5):
                            mm = pe.transpose(pt[:, a, :], lat[:, a * P:(a + 1) * P], self.c("ident"))
                        mm.then_inc(s["latents_turned"].sem, 1)
                        if t + 1 < NT:
                            project(t + 1, 512, MLA_COLS).then_inc(s["projected"].sem, 1)
                        make_q(t)
                        if t >= 1:
                            pe.wait_ge(s["heads_normed"].sem, s["heads_normed"] + t)
                            turn_heads(t - 1, 0)
                        make_kv(t)
                        if t >= 1:
                            pe.wait_ge(s["q_t"].sem, s["q_t"] + t)
                            turn_heads(t - 1, 1)
                    pe.wait_ge(s["heads_normed"].sem, s["heads_normed"] + NT)
                    pe.wait_ge(s["k_t"].sem, s["k_t"] + (NT - 1))
                    turn_heads(NT - 1, 0)
                    pe.wait_ge(s["q_t"].sem, s["q_t"] + NT)
                    turn_heads(NT - 1, 1)

                @block.scalar
                def _(act):
                    link = self.act_chain.on(act)

                    def norm_latents(t):
                        act.wait_ge(s["projected"].sem, s["projected"] + (t + 1))
                        link(act.activation(junk[:, 0:QR], pa[:, 0:QR], ACT.Square, accum_out=st[:, 0:1]))
                        link(act.activation(junk[:, 0:KVR], pa[:, QR:QR + KVR], ACT.Square, accum_out=st[:, 1:2]))
                        act.copy(junk[:, 0:1], junk[:, 1:2]).then_inc(s["squares"].sem, 1)
                        act.wait_ge(s["mean"].sem, s["mean"] + (t + 1))
                        act.activation(st[:, 4:6], st[:, 2:4], ACT.Sqrt).then_inc(s["root"].sem, 1)

                    def copy_q(t):
                        act.wait_ge(s["q_turned"].sem, s["q_turned"] + (t + 1))
                        act.activation(q_t[:, :, t * P:(t + 1) * P], ph, ACT.Identity, scale=float(QK) ** -0.5
                                       ).then_inc(s["q_t"].sem, 1)

                    norm_latents(0)
                    for t in range(NT):
                        act.wait_ge(s["latents_turned"].sem, s["latents_turned"] + (t + 1))
                        if t >= 1:
                            act.wait_ge(s["kv_made"].sem, s["kv_made"] + t)
                        for a in range(5):
                            ins = act.activation(lat_t[:, a, :], pt[:, a, :], ACT.Identity, scale=self.col("cn")[:, a:a + 1])
                        ins.then_inc(s["latents_t"].sem, 1)
                        if t + 1 < NT:
                            norm_latents(t + 1)
                        act.wait_ge(s["q_made"].sem, s["q_made"] + (t + 1))
                        if t >= 2:
                            act.wait_ge(s["k_turned"].sem, s["k_turned"] + (t - 1))
                        act.copy(qk[:, t % 2, 0, :, :].rearrange("p h d -> p (h d)"), pq)
                        if t >= 1:
                            act.wait_ge(s["head_mean"].sem, s["head_mean"] + t)
                        act.activation(sq[:, 0, :, :].rearrange("p h d -> p (h d)"), pq, ACT.Square).then_inc(s["q_copied"].sem, 1)
                        if t >= 1:
                            copy_q(t - 1)
                        act.wait_ge(s["kv_made"].sem, s["kv_made"] + (t + 1))
                        act.copy(qk[:, t % 2, 1, :, 0:NOPE], pkv[:, :, 0:NOPE])
                        act.copy(v[:, t, :, :], pkv[:, :, NOPE:NOPE + VD]).then_inc(s["kv_copied"].sem, 1)
                        act.wait_ge(s["head_mean"].sem, s["head_mean"] + (t + 1))
                        act.activation(st[:, 32:48], st[:, 16:32], ACT.Sqrt).then_inc(s["head_root"].sem, 1)
                    copy_q(NT - 1)

                @block.vector
                def _(dve):
                    link = self.dve_chain.on(dve)

                    def make_latents(t):
                        dve.wait_ge(s["squares"].sem, s["squares"] + (t + 1))
                        link(dve.tensor_scalar(st[:, 2:3], st[:, 0:1], 1.0 / QR, EPS, ALU.mult, ALU.add))
                        dve.tensor_scalar(st[:, 3:4], st[:, 1:2], 1.0 / KVR, EPS, ALU.mult, ALU.add).then_inc(s["mean"].sem, 1)
                        dve.wait_ge(s["root"].sem, s["root"] + (t + 1))
                        link(dve.reciprocal(st[:, 6:8], st[:, 4:6]))
                        if t >= 1:
                            dve.wait_ge(s["latents_turned"].sem, s["latents_turned"] + t)
                            dve.wait_ge(s["rope_copied"].sem, s["rope_copied"] + t)
                        dve.tensor_scalar(lat[:, 0:QR], pa[:, 0:QR], st[:, 6:7], None, ALU.mult)
                        dve.tensor_scalar(lat[:, QR:640], pa[:, QR:640], st[:, 7:8], None, ALU.mult)
                        dve.tensor_copy(lat[:, 640:MLA_COLS], pa[:, 640:MLA_COLS]).then_inc(s["latents"].sem, 1)

                    def copy_k(t):
                        dve.wait_ge(s["k_turned"].sem, s["k_turned"] + (t + 1))
                        dve.tensor_copy(k_t[:, :, t * P:(t + 1) * P], ph).then_inc(s["k_t"].sem, 1)

                    dve.wait_ge(landed.sem, landed + 3)
                    make_latents(0)
                    for t in range(NT):
                        if t >= 2:
                            dve.wait_ge(s["k_turned"].sem, s["k_turned"] + (t - 1))
                        dve.wait_ge(s["latents"].sem, s["latents"] + (t + 1))
                        dve.tensor_copy(qk[:, t % 2, 1, :, NOPE:QK], spread(lat[:, 640:MLA_COLS], 1, HEADS)
                                        ).then_inc(s["rope_copied"].sem, 1)
                        if t + 1 < NT:
                            make_latents(t + 1)
                        if t >= 1:
                            copy_k(t - 1)
                        dve.wait_ge(s["q_copied"].sem, s["q_copied"] + (t + 1))
                        dve.wait_ge(s["kv_copied"].sem, s["kv_copied"] + (t + 1))
                        dve.wait_ge(s["rope_copied"].sem, s["rope_copied"] + (t + 1))
                        both = qk[:, t % 2, :, :, :]
                        rows = both.rearrange("p a h d -> p (a h) d")
                        link(dve.tensor_tensor(sq[:, 1, :, :], both[:, 1], both[:, 1], ALU.mult))
                        link(dve.tensor_reduce(st[:, 16:32], sq.rearrange("p a h d -> p (a h) d"), AX, ALU.add))
                        dve.tensor_scalar(st[:, 16:32], st[:, 16:32], 1.0 / QK, EPS, ALU.mult, ALU.add).then_inc(s["head_mean"].sem, 1)
                        dve.wait_ge(s["head_root"].sem, s["head_root"] + (t + 1))
                        link(dve.reciprocal(st[:, 48:64], st[:, 32:48]))
                        link(dve.tensor_tensor(rows, rows, spread(st[:, 48:64], 2, QK), ALU.mult))
                        gain = spread(self.row("qk_gain").rearrange("p (a d) -> p a d", a=2), 2, HEADS)
                        if t < CT:
                            dve.tensor_tensor(both, both, gain, ALU.mult).then_inc(s["heads_normed"].sem, 1)
                        else:
                            link(dve.tensor_tensor(both, both, gain, ALU.mult))
                            at = (t - CT) * 16
                            cos = spread(self.c("axial_cos")[:, at:at + 16], 1, 2 * HEADS)
                            sin = spread(self.c("axial_sin")[:, at:at + 16], 1, 2 * HEADS)
                            x1, x2 = rows[:, :, NOPE:NOPE + 16], rows[:, :, NOPE + 16:QK]
                            dve.tensor_tensor(turn[:, 0], x1, cos, ALU.mult)
                            dve.tensor_tensor(turn[:, 1], x2, sin, ALU.mult)
                            dve.tensor_tensor(turn[:, 2], x1, sin, ALU.mult)
                            link(dve.tensor_tensor(turn[:, 3], x2, cos, ALU.mult))
                            dve.tensor_tensor(x1, turn[:, 0], turn[:, 1], ALU.subtract)
                            dve.tensor_tensor(x2, turn[:, 2], turn[:, 3], ALU.add).then_inc(s["heads_normed"].sem, 1)
                    copy_k(NT - 1)
            landed.advance(3)
            for n in names:
                s[n].advance(NT)
            self.attend(l, last, q_t, k_t, v)

    def attend(self, l, last, q_t, k_t, v):
        nc = self.nc
        names = ("scores", "max", "exp", "turned", "probs_t", "values", "outs", "out_turned", "out_t")
        s = {n: self.count("att_" + n) for n in names}
        tiles = list(range(CT if last else 0, NT))
        items = [(h, t) for h in range(HEADS) for t in tiles]
        n_items = len(items)
        keys = [CT if t < CT else NT for _, t in items]
        with ExitStack() as scope:
            sb = lambda name, shape: self.sbuf(scope, name, shape)
            probs, probs_t = sb("probs", [P, 2, TOK]), sb("probs_t", [P, 2, NT, P])
            outs = self.mix_t[:, 4:8, :].rearrange("p k n -> p (k n)").rearrange("p (t n) -> p t n", t=NT)
            stat = sb("softmax_stat", [P, 4, 4])
            block = scope.enter_context(nc.Block())
            score = lambda i: self.flat[:, 1024 * (i % 2):1024 * (i % 2) + TOK]
            turned = self.flat[:, 2048:2048 + TOK].rearrange("p (a n) -> p a n", n=P)

            @block.sync
            def _(sp):
                sp.dma_start(self.w_in[:, :, :], self.io["w_in"][l, :, MLA_COLS:MLA_COLS + RET_COLS].rearrange(
                    "(k p) n -> p k n", p=P)).then_inc(self.count("ret_weights_landed", 16).sem, 16)

            @block.tensor
            def _(pe):
                def scores(i):
                    h, t = items[i]
                    if i >= 2:
                        pe.wait_ge(s["exp"].sem, s["exp"] + (i - 1))
                    for lo in range(0, keys[i] * P, 512):
                        hi = min(lo + 512, keys[i] * P)
                        mm = pe.matmul(score(i)[:, lo:hi], q_t[:, h, t * P:(t + 1) * P], k_t[:, h, lo:hi],
                                       start=True, stop=True)
                    mm.then_inc(s["scores"].sem, 1)

                def turn(i):
                    pe.wait_ge(s["exp"].sem, s["exp"] + (i + 1))
                    if i >= 1:
                        pe.wait_ge(s["probs_t"].sem, s["probs_t"] + i)
                    for k in range(keys[i]):
                        mm = pe.transpose(turned[:, k, :], probs[:, i % 2, k * P:(k + 1) * P], self.c("ident"))
                    mm.then_inc(s["turned"].sem, 1)

                def values(i):
                    h, t = items[i]
                    pe.wait_ge(s["probs_t"].sem, s["probs_t"] + (i + 1))
                    if i >= 2:
                        pe.wait_ge(s["outs"].sem, s["outs"] + (i - 1))
                    for k in range(keys[i]):
                        mm = pe.matmul(self.psum[:, 6 + i % 2, 0:VD], probs_t[:, i % 2, k, :], v[:, k, h, :],
                                       start=(k == 0), stop=(k == keys[i] - 1))
                    mm.then_inc(s["values"].sem, 1)

                for i in range(n_items + 2):
                    if i < n_items:
                        scores(i)
                    if 1 <= i <= n_items:
                        turn(i - 1)
                    if i >= 2:
                        values(i - 2)
                pe.wait_ge(s["outs"].sem, s["outs"] + n_items)
                for n, t in enumerate(tiles):
                    if n >= 2:
                        pe.wait_ge(s["out_t"].sem, s["out_t"] + (n - 1))
                    for a in range(4):
                        mm = pe.transpose(self.psum[:, n % 2, a * P:(a + 1) * P], outs[:, t, a * P:(a + 1) * P], self.c("ident"))
                    mm.then_inc(s["out_turned"].sem, 1)

            @block.scalar
            def _(act):
                for i in range(n_items):
                    act.wait_ge(s["max"].sem, s["max"] + (i + 1))
                    if i >= 2:
                        act.wait_ge(s["turned"].sem, s["turned"] + (i - 1))
                    n = keys[i] * P
                    act.activation(probs[:, i % 2, 0:n], score(i)[:, 0:n], ACT.Exp, bias=stat[:, i % 4, 1:2],
                                   accum_out=stat[:, i % 4, 2:3]).then_inc(s["exp"].sem, 1)
                for n, t in enumerate(tiles):
                    act.wait_ge(s["out_turned"].sem, s["out_turned"] + (n + 1))
                    act.copy(self.mix_t[:, 0:4, t * P:(t + 1) * P],
                             self.psum[:, n % 2, :].rearrange("p (a n) -> p a n", n=P)).then_inc(s["out_t"].sem, 1)

            @block.vector
            def _(dve):
                link = self.dve_chain.on(dve)
                for i in range(n_items + 2):
                    if i < n_items:
                        dve.wait_ge(s["scores"].sem, s["scores"] + (i + 1))
                        dve.tensor_reduce(stat[:, i % 4, 1:2], score(i)[:, 0:keys[i] * P], AX, ALU.max, negate=True
                                          ).then_inc(s["max"].sem, 1)
                    if 1 <= i <= n_items:
                        j = i - 1
                        dve.wait_ge(s["turned"].sem, s["turned"] + (j + 1))
                        if j >= 2:
                            dve.wait_ge(s["values"].sem, s["values"] + (j - 1))
                        dve.tensor_copy(probs_t[:, j % 2, 0:keys[j], :], turned[:, 0:keys[j], :]).then_inc(s["probs_t"].sem, 1)
                    if i >= 2:
                        j = i - 2
                        h, t = items[j]
                        dve.wait_ge(s["values"].sem, s["values"] + (j + 1))
                        link(dve.reciprocal(stat[:, j % 4, 3:4], stat[:, j % 4, 2:3]))
                        dve.tensor_scalar(outs[:, t, h * VD:(h + 1) * VD], self.psum[:, 6 + j % 2, 0:VD],
                                          stat[:, j % 4, 3:4], None, ALU.mult).then_inc(s["outs"].sem, 1)
        for n in names:
            s[n].advance(len(tiles) if n.startswith("out_") else n_items)

    def retention(self, l, last):
        nc, io = self.nc, self.io
        landed, w_landed = self.count("ret_const_landed", 16), self.count("ret_weights_landed", 16)
        tiles = list(range(CT if last else 0, NT))
        names = ("projected", "rotated", "v_copied", "gate", "gated", "turned", "turned_t", "rows_read",
                 "decay_exp", "decay_ln", "log_decay", "powers", "strips",
                 "scores", "weighted", "head_done", "centred", "var", "root", "normed", "out_turned", "out_t")
        s = {n: self.count("ret_" + n) for n in names}
        n_scores = HEADS // 2 * NT
        with ExitStack() as scope:
            sb = lambda name, shape: self.sbuf(scope, name, shape)
            cst = sb("ret_const", [P, RETC_N])
            cc = lambda n: cst[:, RETC[n][0]:RETC[n][1]]
            w = self.w_in
            qk = sb("ret_qk", [P, 2, 8, 64])
            turn = sb("ret_turn", [P, 4, 8, 32])
            v, g = sb("ret_v", [P, NT, 256]), sb("ret_gate", [P, NT, 256])
            qk_t = sb("ret_qk_t", [P, 6, TOK])
            strip_a, strip_b = sb("strip_a", [P, 4, 896]), sb("strip_b", [P, 4, 640])
            parts = self.mix_t[:, 6:8, :].rearrange("p k n -> p (k n)")
            part_a, part_b = parts[:, 0:896], parts[:, 896:1536]
            spare = w[:, :, :].rearrange("p k n -> p (k n)")
            att = spare[:, 0:NT * 512].rearrange("p (t n) -> p t n", t=NT)
            att_c = spare[:, 3072:3072 + CT * 256].rearrange("p (t n) -> p t n", t=CT)
            out = spare[:, 4096:4096 + NT * 256].rearrange("p (t n) -> p t n", t=NT)
            dec = sb("ret_decay", [P, 4, 8])
            st = sb("ret_stat", [P, 4, 4, NT])
            head_sq = spare[:, 5632:5632 + NT * 64]
            block = scope.enter_context(nc.Block())
            proj = lambda t: self.flat[:, 1024 * (t % 2):1024 * (t % 2) + 1024]
            o = self.flat[:, 2048 + 512:2048 + 512 + NT * 256].rearrange("p (t n) -> p t n", t=NT)

            @block.sync
            def _(sp):
                sp.dma_start(cst[:, :], io["retc"]).then_inc(landed.sem, 16)

            @block.tensor
            def _(pe):
                pe.wait_ge(w_landed.sem, w_landed + 1)

                def turn_tile(t):
                    pe.wait_ge(s["rotated"].sem, s["rotated"] + (t + 1))
                    if t >= 1:
                        pe.wait_ge(s["turned_t"].sem, s["turned_t"] + t)
                    for a in range(4):
                        mm = pe.transpose(self.psum[:, 4, a * P:(a + 1) * P],
                                          qk[:, t % 2, 2 * a:2 * a + 2, :].rearrange("p a d -> p (a d)"), self.c("ident"))
                    mm.then_inc(s["turned"].sem, 1)

                for t in range(NT):
                    if t >= 2:
                        pe.wait_ge(s["rotated"].sem, s["rotated"] + (t - 1))
                        pe.wait_ge(s["gated"].sem, s["gated"] + (t - 1))
                        pe.wait_ge(s["v_copied"].sem, s["v_copied"] + (t - 1))
                    for b in range(2):
                        for k in range(KD):
                            mm = pe.matmul(proj(t)[:, b * 512:(b + 1) * 512], self.u_t[:, k, t * P:(t + 1) * P],
                                           w[:, k, b * 512:(b + 1) * 512], start=(k == 0), stop=(k == KD - 1))
                    mm.then_inc(s["projected"].sem, 1)
                    if t >= 1:
                        turn_tile(t - 1)
                turn_tile(NT - 1)
                pe.wait_ge(s["turned_t"].sem, s["turned_t"] + NT)
                pe.wait_ge(s["gated"].sem, s["gated"] + NT)
                pe.wait_ge(s["v_copied"].sem, s["v_copied"] + NT)
                n = 0
                for h in range(4):
                    f = h // 2
                    for j in range(NT):
                        if n >= 2:
                            pe.wait_ge(s["weighted"].sem, s["weighted"] + (n - 1))
                        key = qk_t[:, 2 + 2 * (h % 2) + f, j * P:(j + 1) * P]
                        if j < CT and not last:
                            pe.matmul(proj(n)[:, 0:CTX], key, qk_t[:, f, 0:CTX], start=True, stop=True)
                        pe.matmul(proj(n)[:, 512:1024], key, qk_t[:, f, CTX:TOK], start=True, stop=True
                                  ).then_inc(s["scores"].sem, 1)
                        n += 1
                    pe.wait_ge(s["weighted"].sem, s["weighted"] + n)
                    if h >= 1:
                        pe.wait_ge(s["centred"].sem, s["centred"] + h)
                    for t in tiles:
                        keys = list(range(CT if t < CT else NT))
                        for j in keys:
                            a = att_c[:, j, t * P:(t + 1) * P] if t < CT else att[:, j, (t - CT) * P:(t - CT + 1) * P]
                            mm = pe.matmul(o[:, t, h * 64:(h + 1) * 64], a, v[:, j, h * 64:(h + 1) * 64],
                                           start=(j == keys[0]), stop=(j == keys[-1]))
                    mm.then_inc(s["head_done"].sem, 1)
                pe.wait_ge(s["normed"].sem, s["normed"] + 4)
                for n, t in enumerate(tiles):
                    if n >= 2:
                        pe.wait_ge(s["out_t"].sem, s["out_t"] + (n - 1))
                    for a in range(2):
                        mm = pe.transpose(self.psum[:, n % 2, a * P:(a + 1) * P], out[:, t, a * P:(a + 1) * P], self.c("ident"))
                    mm.then_inc(s["out_turned"].sem, 1)

            @block.scalar
            def _(act):
                act.wait_ge(s["log_decay"].sem, s["log_decay"] + 1)
                act.activation(dec[:, 1, :], dec[:, 0, :], ACT.Exp, scale=-1.0).then_inc(s["decay_exp"].sem, 1)
                act.wait_ge(s["decay_exp"].sem, s["decay_exp"] + 1)
                act.activation(dec[:, 2, :], dec[:, 1, :], ACT.Ln, bias=1.0).then_inc(s["decay_ln"].sem, 1)
                act.wait_ge(s["log_decay"].sem, s["log_decay"] + 2)
                act.wait_ge(landed.sem, landed + 1)
                for t in range(NT):
                    act.wait_ge(s["projected"].sem, s["projected"] + (t + 1))
                    act.copy(v[:, t, :], proj(t)[:, 512:768]).then_inc(s["v_copied"].sem, 1)
                    act.activation(g[:, t, :], proj(t)[:, 768:1024], ACT.Sigmoid).then_inc(s["gate"].sem, 1)
                    if t < 4:
                        if t >= 1:
                            act.wait_ge(s["strips"].sem, s["strips"] + t)
                        forward, backward = dec[:, 3, t:t + 1], dec[:, 3, 4 + t:5 + t]
                        act.activation(strip_a[:, t, :], cc("dist"), ACT.Exp, scale=forward)
                        act.activation(part_a, cc("dist"), ACT.Exp, scale=backward)
                        act.activation(strip_b[:, t, :], cc("dist_f"), ACT.Exp, scale=forward)
                        act.activation(part_b, cc("dist_b"), ACT.Exp, scale=backward).then_inc(s["powers"].sem, 1)
                for h in range(4):
                    act.wait_ge(s["var"].sem, s["var"] + (h + 1))
                    act.activation(st[:, h, 2, :], st[:, h, 1, :], ACT.Sqrt).then_inc(s["root"].sem, 1)
                for n, t in enumerate(tiles):
                    act.wait_ge(s["out_turned"].sem, s["out_turned"] + (n + 1))
                    act.copy(self.mix_t[:, 4:6, t * P:(t + 1) * P],
                             self.psum[:, n % 2, 0:256].rearrange("p (a n) -> p a n", n=P)).then_inc(s["out_t"].sem, 1)

            @block.vector
            def _(dve):
                link = self.dve_chain.on(dve)
                dve.memset(qk_t[64:128, 2:4, :], 0.0)
                dve.memset(qk_t[0:64, 4:6, :], 0.0)
                link(dve.tensor_scalar(dec[:, 3, :], self.row("decay"), -1.0, None, ALU.mult))
                dve.tensor_tensor(dec[:, 0, :], dec[:, 3, :], self.row("decay"), ALU.max).then_inc(s["log_decay"].sem, 1)
                dve.wait_ge(s["decay_ln"].sem, s["decay_ln"] + 1)
                link(dve.tensor_scalar(dec[:, 3, :], self.row("decay"), 0.0, None, ALU.min))
                dve.tensor_tensor(dec[:, 3, :], dec[:, 3, :], dec[:, 2, :], ALU.subtract).then_inc(s["log_decay"].sem, 1)
                dve.wait_ge(landed.sem, landed + 1)
                for t in range(NT):
                    dve.wait_ge(s["projected"].sem, s["projected"] + (t + 1))
                    rows = proj(t)[:, 0:512].rearrange("p (a d) -> p a d", d=64)
                    x1, x2 = rows[:, :, 0:32], rows[:, :, 32:64]
                    cos = spread(cc("seq_cos")[:, t * 32:(t + 1) * 32], 1, 8)
                    sin = spread(cc("seq_sin")[:, t * 32:(t + 1) * 32], 1, 8)
                    link(dve.tensor_tensor(turn[:, 0], x1, cos, ALU.mult))
                    link(dve.tensor_tensor(turn[:, 1], x2, sin, ALU.mult))
                    link(dve.tensor_tensor(turn[:, 2], x1, sin, ALU.mult))
                    link(dve.tensor_tensor(turn[:, 3], x2, cos, ALU.mult))
                    if t >= 2:
                        dve.wait_ge(s["turned"].sem, s["turned"] + (t - 1))
                    link(dve.tensor_tensor(qk[:, t % 2, :, 0:32], turn[:, 0], turn[:, 1], ALU.subtract))
                    dve.tensor_tensor(qk[:, t % 2, :, 32:64], turn[:, 2], turn[:, 3], ALU.add).then_inc(s["rotated"].sem, 1)
                    dve.wait_ge(s["gate"].sem, s["gate"] + (t + 1))
                    dve.tensor_tensor(g[:, t, :], g[:, t, :], proj(t)[:, 768:1024], ALU.mult).then_inc(s["gated"].sem, 1)
                    dve.wait_ge(s["turned"].sem, s["turned"] + (t + 1))
                    by_feature = self.psum[:, 4, :].rearrange("p (a n) -> p a n", n=P)
                    cut = slice(t * P, (t + 1) * P)
                    dve.tensor_copy(qk_t[:, 0:2, cut], by_feature[:, 0:2])
                    dve.tensor_copy(qk_t[0:64, 2:4, cut], by_feature[0:64, 2:4])
                    dve.tensor_copy(qk_t[64:128, 4:6, cut], by_feature[64:128, 2:4]).then_inc(s["turned_t"].sem, 1)
                    if t < 4:
                        dve.wait_ge(s["powers"].sem, s["powers"] + (t + 1))
                        dve.tensor_tensor(strip_a[:, t, :], strip_a[:, t, :], cc("after"), ALU.mult)
                        link(dve.tensor_tensor(part_a, part_a, cc("before"), ALU.mult))
                        dve.tensor_tensor(strip_a[:, t, :], strip_a[:, t, :], part_a, ALU.add)
                        dve.tensor_tensor(strip_b[:, t, :], strip_b[:, t, :], part_b, ALU.add).then_inc(s["strips"].sem, 1)
                lo = tiles[0]
                count = NT - lo

                def normalise_head(h):
                    src, dst = (a[:, lo:NT, h * 64:(h + 1) * 64] for a in (o, out))
                    mean, var, inverse = (st[:, h, i, lo:NT] for i in (0, 1, 3))
                    dve.wait_ge(s["head_done"].sem, s["head_done"] + (h + 1))
                    link(dve.tensor_reduce(mean, src, AX, ALU.add))
                    link(dve.tensor_scalar(mean, mean, 1.0 / 64, None, ALU.mult))
                    dve.tensor_tensor(dst, src, spread(mean, 2, 64), ALU.subtract).then_inc(s["centred"].sem, 1)
                    dve.wait_ge(s["centred"].sem, s["centred"] + (h + 1))
                    squares = head_sq[:, 0:count * 64].rearrange("p (t d) -> p t d", d=64)
                    link(dve.tensor_tensor(squares, dst, dst, ALU.mult))
                    link(dve.tensor_reduce(var, squares, AX, ALU.add))
                    dve.tensor_scalar(var, var, 1.0 / 64, 1e-5, ALU.mult, ALU.add).then_inc(s["var"].sem, 1)
                    gain = spread(self.row("gn_w")[:, h * 64:(h + 1) * 64], 1, count)
                    link(dve.tensor_tensor(dst, dst, gain, ALU.mult))
                    link(dve.tensor_tensor(dst, dst, g[:, lo:NT, h * 64:(h + 1) * 64], ALU.mult))
                    dve.wait_ge(s["root"].sem, s["root"] + (h + 1))
                    link(dve.reciprocal(inverse, st[:, h, 2, lo:NT]))
                    dve.tensor_tensor(dst, dst, spread(inverse, 2, 64), ALU.mult).then_inc(s["normed"].sem, 1)

                link(dve.memset(st[:, :, :, :], 1.0))
                dve.wait_ge(s["strips"].sem, s["strips"] + 4)
                n = 0
                for h in range(4):
                    if h >= 1:
                        normalise_head(h - 1)
                    for j in range(NT):
                        dve.wait_ge(s["scores"].sem, s["scores"] + (n + 1))
                        if j < CT:
                            if not last:
                                dve.scalar_tensor_tensor(att_c[:, j, :], proj(n)[:, 0:CTX], 0.125,
                                                         strip_a[:, h, 384 - j * P:384 - j * P + CTX], ALU.mult, ALU.mult)
                            strip = strip_b[:, h, P - j * P:P - j * P + LAT]
                        else:
                            strip = strip_a[:, h, 384 - (j - CT) * P:384 - (j - CT) * P + LAT]
                        dve.scalar_tensor_tensor(att[:, j, :], proj(n)[:, 512:1024], 0.125, strip,
                                                 ALU.mult, ALU.mult).then_inc(s["weighted"].sem, 1)
                        n += 1
                normalise_head(3)
        landed.advance(1)
        w_landed.advance(1)
        once = {"decay_exp": 1, "decay_ln": 1, "log_decay": 2, "powers": 4, "strips": 4, "head_done": 4, "centred": 4, "var": 4,
                "root": 4, "normed": 4, "scores": n_scores, "weighted": n_scores,
                "out_turned": len(tiles), "out_t": len(tiles)}
        for n in names:
            s[n].advance(once.get(n, NT))

    def rwkv(self, l, last):
        with ExitStack() as scope:
            sb = lambda name, shape: self.sbuf(scope, name, shape)
            cst = sb("rwkv_const", [P, RWKVC_N])
            self.cc = lambda n: cst[:, RWKVC[n][0]:RWKVC[n][1]]
            g, bonus = sb("rwkv_g", [P, 2, TOK]), sb("rwkv_bonus", [P, 2, TOK])
            v = sb("rwkv_v", [P, 2, TOK])
            queries = self.u_t[:, :, :].rearrange("p k n -> p (k n)").rearrange("p (q c a t) -> p q c a t", q=4, c=NCH, a=2)
            updates = sb("updates", [P, 4, NCH, 2, C])
            half = sb("half_decay", [P, 4, NCH])
            self.rwkv_features(l, cst, g, bonus, v, queries, updates, half)
            self.rwkv_chunks(l, last, g, bonus, v, queries, updates, half)

    def rwkv_features(self, l, cst, g, bonus, v, queries, updates, half):
        nc, io, cc = self.nc, self.io, self.cc
        landed = self.count("rwkv_const_landed", 16)
        w_landed = [self.count(f"rwkv_w_landed{i}", 16) for i in range(2)]
        names = ("projected", "tile_read", "shifted", "low_ready", "wide", "kept", "summed", "table", "root",
                 "decay_in", "decay_exp")
        s = {n: self.count("rwkv_" + n) for n in names}
        order = (6, 7, 8, 2, 3, 0, 1, 4, 5)
        at = [(n * P, P) for n in range(7)] + [(896, 64), (960, P)]
        jobs = [("w", q) for q in range(4)] + [("a", f) for f in range(2)] + [("g", f) for f in range(2)] + \
               [("kk", f) for f in range(2)] + [("bonus", f) for f in range(2)]
        jobs_after = {2: (0, 1), 3: (2, 3, 4, 5), 4: (6, 7), 5: (8, 9), 8: (10, 11)}
        halves = ((0, CTX), (CTX, TOK))
        with ExitStack() as scope:
            sb = lambda name, shape: self.sbuf(scope, name, shape)
            feat = sb("rwkv_feat", [P, 4, TOK])
            low = sb("rwkv_low", [P, 3, TOK])
            raw = sb("rwkv_raw", [P, TOK + 4])
            lw, inc = sb("log_w", [P, 4, TOK]), sb("decay_sums", [P, 4, TOK])
            a = sb("rwkv_a", [P, 2, TOK])
            small = sb("rwkv_small", [P, 3, 256])
            tot = sb("chunk_total", [P, 4, NCH])
            kk, squares = self.mix_t[:, 6:8, :], bonus
            late = RWKVC["restart"][0]
            w = cst[:, 0:KD * 2 * P].rearrange("p (k a n) -> p k a n", k=KD, a=2)
            assert KD * 2 * P <= late
            block = scope.enter_context(nc.Block())
            wide = lambda n: self.psum[:, 4 + 2 * (n % 2):6 + 2 * (n % 2), :]
            each_half = lambda n: [(wide(n)[:, b, 0:hi - lo], slice(lo, hi)) for b, (lo, hi) in enumerate(halves)]
            chunks = lambda ap: ap.rearrange("p (c t) -> p c t", t=C)
            sums = lambda q: (lw[:, q, :], inc[:, q, :]) if q < 2 else (inc[:, q, :], lw[:, q, :])

            @block.sync
            def _(sp):
                sp.dma_start(cst[:, late:RWKVC_N], io["rwkvc"][:, late:RWKVC_N]).then_inc(landed.sem, 16)
                for n, f in enumerate(order):
                    lo, width = at[f]
                    if n >= 2:
                        sp.wait_ge(s["projected"].sem, s["projected"] + (n - 1))
                    c0 = MLA_COLS + RET_COLS + lo
                    sp.dma_start(w[:, :, n % 2, 0:width], io["w_in"][l, :, c0:c0 + width].rearrange("(k p) n -> p k n", p=P)
                                 ).then_inc(w_landed[n % 2].sem, 16)
                    if n == 1:
                        sp.dma_start(small[:, 0, :], io["rwkv_w2"][l].rearrange("d k n -> (d k) n")).then_inc(landed.sem, 16)
                        sp.dma_start(small[0:64, 1, :], io["rwkv_a2"][l]).then_inc(landed.sem, 16)
                        sp.dma_start(small[:, 2, :], io["rwkv_g2"][l]).then_inc(landed.sem, 16)
                sp.wait_ge(s["projected"].sem, s["projected"] + len(order))
                sp.dma_start(cst[:, 0:late], io["rwkvc"][:, 0:late]).then_inc(landed.sem, 16)
                sp.wait_ge(landed.sem, landed + 5)

            @block.tensor
            def _(pe):
                def job_products(n):
                    job, q = jobs[n]
                    if 2 <= n < 10:
                        pe.wait_ge(s["kept"].sem, s["kept"] + (n - 1))
                    elif n >= 10:
                        pe.wait_ge(s["summed"].sem, s["summed"] + (n - 9))
                    if n == 0:
                        pe.wait_ge(landed.sem, landed + 4)
                        pe.wait_ge(s["low_ready"].sem, s["low_ready"] + 1)
                    if n == 4:
                        pe.wait_ge(s["shifted"].sem, s["shifted"] + 2)
                    if n == 6:
                        pe.wait_ge(s["low_ready"].sem, s["low_ready"] + 2)
                    if n >= 8:
                        pe.wait_ge(s["table"].sem, s["table"] + (n - 7))
                    for b, (lo, hi) in enumerate(halves):
                        d, f = divmod(q, 2)
                        lhs, rhs = {
                            "w": lambda: (small[64 * d:64 * d + 64, 0, f * P:(f + 1) * P], low[64 * d:64 * d + 64, 0, lo:hi]),
                            "a": lambda: (small[0:64, 1, q * P:(q + 1) * P], low[0:64, 1, lo:hi]),
                            "g": lambda: (small[:, 2, q * P:(q + 1) * P], low[:, 2, lo:hi]),
                            "kk": lambda: (self.c("pair_ones"), squares[:, q, lo:hi]),
                            "bonus": lambda: (self.c("pair_ones"), squares[:, q, lo:hi])}[job]()
                        mm = pe.matmul(wide(n)[:, b, 0:hi - lo], lhs, rhs, start=True, stop=True)
                    mm.then_inc(s["wide"].sem, 1)

                for n, f in enumerate(order):
                    width = at[f][1]
                    pe.wait_ge(w_landed[n % 2].sem, w_landed[n % 2] + (n // 2 + 1))
                    if n >= 2:
                        pe.wait_ge(s["tile_read"].sem, s["tile_read"] + (n - 1))
                    for lo, hi in halves:
                        b = 2 * (n % 2) + (lo > 0)
                        for k in range(KD):
                            mm = pe.matmul(self.psum[0:width, b, 0:hi - lo], w[:, k, n % 2, 0:width],
                                           self.u_t[:, k, lo:hi], start=(k == 0), stop=(k == KD - 1))
                    mm.then_inc(s["projected"].sem, 1)
                    for job in jobs_after.get(n, ()):
                        job_products(job)

            @block.scalar
            def _(act):
                link = self.act_chain.on(act)

                def keep(n):
                    job, q = jobs[n]
                    act.wait_ge(s["wide"].sem, s["wide"] + (n + 1))
                    for src, cut in each_half(n):
                        if job == "w":
                            ins = act.activation(lw[:, q, cut], src, ACT.Sigmoid, bias=self.col("w0")[:, q:q + 1])
                        elif job == "a":
                            ins = act.activation(a[:, q, cut], src, ACT.Sigmoid, bias=self.col("a0")[:, q:q + 1])
                        else:
                            ins = act.copy(g[:, q, cut], src)
                    ins.then_inc(s["kept"].sem, 1)

                def powers(q):
                    act.wait_ge(s["decay_in"].sem, s["decay_in"] + (q + 1))
                    rate = DECAY * (1.0, -1.0)[q // 2]
                    by_query, by_update = sums(q)
                    link(act.activation(updates[:, q, :, 1, :], chunks(by_update), ACT.Exp, scale=-rate))
                    act.activation(by_query, by_query, ACT.Exp, scale=rate)
                    act.activation(by_update, by_update, ACT.Exp, scale=rate)
                    act.activation(half[:, q, :], tot[:, q, :], ACT.Exp, scale=0.5 * DECAY).then_inc(s["decay_exp"].sem, 1)

                act.wait_ge(s["shifted"].sem, s["shifted"] + 1)
                act.activation(low[:, 0, :], low[:, 0, :], ACT.Tanh).then_inc(s["low_ready"].sem, 1)
                keep(0)
                keep(1)
                act.wait_ge(s["shifted"].sem, s["shifted"] + 3)
                act.activation(low[:, 2, :], low[:, 2, :], ACT.Sigmoid).then_inc(s["low_ready"].sem, 1)
                for n in range(2, 8):
                    keep(n)
                for f in range(2):
                    act.wait_ge(s["summed"].sem, s["summed"] + (f + 1))
                    act.activation(squares[:, f, :], squares[:, f, :], ACT.Sqrt).then_inc(s["root"].sem, 1)
                for q in range(4):
                    powers(q)

            @block.vector
            def _(dve):
                link = self.dve_chain.on(dve)

                def shift(n):
                    f = order[n]
                    width = at[f][1]
                    dst = {6: low[:, 0], 7: low[:, 1], 8: low[:, 2], 4: v[:, 0], 5: v[:, 1]}.get(f)
                    if dst is None:
                        dst = feat[:, f]
                    dve.wait_ge(s["projected"].sem, s["projected"] + (n + 1))
                    dve.tensor_copy(raw[0:width, 1:1 + CTX], self.psum[0:width, 2 * (n % 2), 0:CTX])
                    dve.tensor_copy(raw[0:width, 3 + CTX:3 + TOK], self.psum[0:width, 2 * (n % 2) + 1, 0:LAT]
                                    ).then_inc(s["tile_read"].sem, 1)
                    dve.wait_ge(s["tile_read"].sem, s["tile_read"] + (n + 1))
                    parts = []
                    for lo, hi in halves:
                        off = 1 if lo == 0 else 3
                        now, before, after = (raw[0:width, lo + off + d:hi + off + d] for d in (0, -1, 1))
                        parts.append((dst[0:width, lo:hi], now, before, after))
                    for to, now, before, after in parts:
                        ins = dve.tensor_tensor(to, before, after, ALU.add)
                    link(ins)
                    for to, now, before, after in parts:
                        ins = dve.scalar_tensor_tensor(to, to, 0.5, now, ALU.mult, ALU.subtract)
                    link(ins)
                    for to, now, before, after in parts:
                        ins = dve.scalar_tensor_tensor(to, to, self.col("mu")[0:width, f:f + 1], now, ALU.mult, ALU.add)
                    ins.then_inc(s["shifted"].sem, 1)
                    dve.wait_ge(s["shifted"].sem, s["shifted"] + (n + 1))

                def square_keys(f):
                    link(dve.tensor_scalar(kk[:, f, :], feat[:, 2 + f, :], self.col("k_k")[:, f:f + 1], None, ALU.mult))
                    dve.tensor_tensor(squares[:, f, :], kk[:, f, :], kk[:, f, :], ALU.mult).then_inc(s["table"].sem, 1)

                def sum_decays(q):
                    dve.wait_ge(s["kept"].sem, s["kept"] + (q + 1))
                    link(dve.tensor_tensor_scan(inc[:, q, :], cc("restart"), lw[:, q, :], 0.0, ALU.mult, ALU.add))
                    link(dve.tensor_copy(tot[:, q, :], chunks(inc[:, q, :])[:, :, C - 1]))
                    link(dve.scalar_tensor_tensor(chunks(inc[:, q, :]), spread(tot[:, q, :], 2, C), -0.5, chunks(inc[:, q, :]),
                                                  ALU.mult, ALU.add))
                    dve.tensor_tensor(lw[:, q, :], inc[:, q, :], lw[:, q, :], ALU.subtract).then_inc(s["decay_in"].sem, 1)

                def mix_keys(f):
                    dve.wait_ge(s["kept"].sem, s["kept"] + 6)
                    scratch = low[:, 1, :]
                    link(dve.tensor_scalar(scratch, a[:, f, :], -1.0, self.col("k_a")[:, f:f + 1], ALU.add, ALU.mult))
                    link(dve.scalar_tensor_tensor(feat[:, 2 + f, :], scratch, 1.0, feat[:, 2 + f, :], ALU.add, ALU.mult))

                def bound_norms(f):
                    dve.wait_ge(s["wide"].sem, s["wide"] + (9 + f))
                    for src, cut in each_half(8 + f):
                        ins = dve.tensor_scalar(squares[:, f, cut], src, 1e-24, None, ALU.max)
                    ins.then_inc(s["summed"].sem, 1)

                link(dve.memset(raw[:, :], 0.0))
                dve.wait_ge(landed.sem, landed + 4)
                for n in range(len(order)):
                    shift(n)
                    if n == 3:
                        square_keys(0)
                        sum_decays(0)
                    elif n == 4:
                        square_keys(1)
                        sum_decays(1)
                    elif n == 5:
                        mix_keys(0)
                        sum_decays(2)
                    elif n == 6:
                        mix_keys(1)
                        bound_norms(0)
                        bound_norms(1)
                        sum_decays(3)
                    elif n == 7:
                        for f in range(2):
                            dve.wait_ge(s["root"].sem, s["root"] + (f + 1))
                            link(dve.reciprocal(squares[:, f, :], squares[:, f, :]))
                            link(dve.tensor_tensor(kk[:, f, :], kk[:, f, :], squares[:, f, :], ALU.mult))
                            link(dve.tensor_tensor(a[:, f, :], a[:, f, :], kk[:, f, :], ALU.mult))
                            dve.scalar_tensor_tensor(squares[:, f, :], feat[:, f, :], self.col("r_k")[:, f:f + 1],
                                                     feat[:, 2 + f, :], ALU.mult, ALU.mult).then_inc(s["table"].sem, 1)
                for q in range(4):
                    f = q % 2
                    dve.wait_ge(s["decay_exp"].sem, s["decay_exp"] + (q + 1))
                    ins = dve.scalar_tensor_tensor(updates[:, q, :, 0, :], chunks(a[:, f, :]), -1.0, updates[:, q, :, 1, :],
                                                   ALU.mult, ALU.mult)
                link(ins)
                for q in range(4):
                    dve.tensor_tensor(updates[:, q, :, 1, :], chunks(feat[:, 2 + q % 2, :]), updates[:, q, :, 1, :], ALU.mult)
                dve.wait_ge(s["projected"].sem, s["projected"] + len(order))
                for q in range(4):
                    f = q % 2
                    by_query, by_update = sums(q)
                    dve.tensor_tensor(queries[:, q, :, 0, :], chunks(kk[:, f, :]), chunks(by_query), ALU.mult)
                    dve.tensor_tensor(queries[:, q, :, 1, :], chunks(feat[:, f, :]), chunks(by_update), ALU.mult)
                for f in range(2):
                    dve.wait_ge(s["wide"].sem, s["wide"] + (11 + f))
                    for src, cut in each_half(10 + f):
                        ins = dve.tensor_tensor(bonus[:, f, cut], src, v[:, f, cut], ALU.mult)
                    ins.then_inc(s["summed"].sem, 1)
        landed.advance(5)
        w_landed[0].advance(5)
        w_landed[1].advance(4)
        per = {"low_ready": 2, "wide": 12, "kept": 8, "summed": 4, "table": 4, "root": 2, "decay_in": 4, "decay_exp": 4}
        for n in names:
            s[n].advance(per.get(n, len(order)))

    def rwkv_chunks(self, l, last, g, bonus, v, queries, updates, half):
        nc, cc = self.nc, self.cc
        back = list(range(CCH - 1, -1, -1)) + list(range(NCH - 1, CCH - 1, -1))
        ch = lambda q, i: i if q < 2 else back[i]
        names = ("prep", "masked_b", "masked_k", "blocks", "copied", "inner", "inner_copied", "grown", "added",
                 "rest", "rest_copied", "removed", "removed_copied", "moved", "state", "y_copied",
                 "var", "root", "normed", "turned")
        s = {n: self.count("chunk_" + n) for n in names}
        NL = len(LEVELS)
        chain_at = {(0, 0): ("rest", 0), (0, 1): ("removed", 0), (1, 0): ("move", 0),
                    (2, 0): ("rest", 1), (2, 1): ("removed", 1), (3, 0): ("move", 1)}
        nth = lambda i, n: 2 * NL * (i // 2) + 2 * n + i % 2
        with ExitStack() as scope:
            sb = lambda name, shape: self.sbuf(scope, name, shape)
            m_b, m_k = sb("queries_b", [P, 4, 4, 2, C]), sb("queries_k", [P, 4, 4, 2, C])
            inv = sb("inverse", [P, 4, 2, 4, C])
            steps = sb("level_blocks", [P, 2, NL, 4, C])
            inner = sb("inner", [P, 2, 4, C])
            rows = sb("update_rows", [P, 4, 3, 4, C])
            state, rest, removed = sb("state", [P, 4, C]), sb("rest", [P, 4, C]), sb("removed", [P, 4, C])
            move = sb("state_decay", [P, 4])
            y = [self.mix_t[:, 6:8, :].rearrange("p k n -> p (k n)").rearrange("p (c f t) -> p c f t", c=NCH, f=2),
                 sb("rwkv_y", [P, NCH, 2, C])[:, :, :, :]]
            st = sb("rwkv_stat", [P, 4, 2 * NCH])
            block = scope.enter_context(nc.Block())
            ps = lambda bank, half_: self.psum[:, bank, 256 * half_:256 * half_ + 256].rearrange("p (q t) -> p q t", q=4)
            heads = [(q, slice(64 * e, 64 * e + 64)) for q in range(4) for e in range(2)]

            @block.tensor
            def _(pe):
                def masked_products(i):
                    for bank, what in ((0, "masked_b"), (1, "masked_k")):
                        if i >= 1:
                            pe.wait_ge(s[what].sem, s[what] + i)
                        for q, r in heads:
                            c = ch(q, i)
                            mm = pe.matmul(self.psum[r, bank, q * 128:q * 128 + 128], updates[r, q, c, bank, :],
                                           queries[r, q, c, :, :].rearrange("p a t -> p (a t)"), start=True, stop=True)
                        mm.then_inc(s["prep"].sem, 1)

                def turn_updates(i):
                    b_bank, k_bank = (6, 7) if i % 2 == 0 else (7, 6)
                    if i >= 2:
                        last_pair = nth(i // 2 * 2 - 1, NL - 1) + 1
                        pe.wait_ge(s["inner_copied"].sem, s["inner_copied"] + last_pair)
                        pe.wait_ge(s["added"].sem, s["added"] + last_pair)
                    if i % 2:
                        pe.wait_ge(s["copied"].sem, s["copied"] + 2 * i)
                    for bank, of in ((4 + i % 2, lambda q, c: v[:, q % 2, c * C:(c + 1) * C]),
                                     (b_bank, lambda q, c: updates[:, q, c, 0, :]), (k_bank, lambda q, c: updates[:, q, c, 1, :])):
                        for q in range(4):
                            mm = pe.transpose(self.psum[0:C, bank, q * P:(q + 1) * P], of(q, ch(q, i)), self.c("ident"))
                        mm.then_inc(s["prep"].sem, 1)

                def inner_part(i, n):
                    if n == 0:
                        pe.wait_ge(s["blocks"].sem, s["blocks"] + (i + 1))
                    else:
                        pe.wait_ge(s["added"].sem, s["added"] + (nth(i, n - 1) + 1))
                    for q, r in heads:
                        mm = pe.matmul(ps(4 + i % 2, 0)[r, q, :], steps[r, i % 2, n, q, :], inv[r, i % 4, 1, q, :], start=True, stop=True)
                    mm.then_inc(s["inner"].sem, 1)

                def grow(i, n):
                    if n == 0:
                        pe.wait_ge(s["copied"].sem, s["copied"] + 2 * (i // 2 * 2 + 2))
                    pe.wait_ge(s["inner_copied"].sem, s["inner_copied"] + (nth(i, n) + 1))
                    for q, r in heads:
                        mm = pe.matmul(ps(6 + i % 2, 0)[r, q, :], inner[r, i % 2, q, :], inv[r, i % 4, 0, q, :], start=True, stop=True)
                    mm.then_inc(s["grown"].sem, 1)

                def rest_part(i):
                    pe.wait_ge(s["state"].sem, s["state"] + (i + 1))
                    for q, r in heads:
                        pe.matmul(ps(2, 0)[r, q, :], queries[r, q, ch(q, i), 0, :], state[r, q, :], start=True, stop=False)
                        mm = pe.matmul(ps(2, 0)[r, q, :], m_k[r, i % 4, q, 0, :], rows[r, i % 4, 2, q, :], start=False, stop=True)
                    mm.then_inc(s["rest"].sem, 1)

                def removed_part(i):
                    pe.wait_ge(s["rest_copied"].sem, s["rest_copied"] + (i + 1))
                    pe.wait_ge(s["added"].sem, s["added"] + (nth(i, NL - 1) + 1))
                    for q, r in heads:
                        mm = pe.matmul(ps(2, 1)[r, q, :], inv[r, i % 4, 0, q, :], rest[r, q, :], start=True, stop=True)
                    mm.then_inc(s["removed"].sem, 1)

                def move_part(i):
                    pe.wait_ge(s["removed_copied"].sem, s["removed_copied"] + (i + 1))
                    if i >= 1:
                        pe.wait_ge(s["y_copied"].sem, s["y_copied"] + i)
                    for q, r in heads:
                        pe.matmul(ps(3, 0)[r, q, :], queries[r, q, ch(q, i), 1, :], state[r, q, :], start=True, stop=False)
                        pe.matmul(ps(3, 0)[r, q, :], m_b[r, i % 4, q, 1, :], removed[r, q, :], start=False, stop=False)
                        pe.matmul(ps(3, 0)[r, q, :], m_k[r, i % 4, q, 1, :], rows[r, i % 4, 2, q, :], start=False, stop=True)
                        pe.matmul(ps(3, 1)[r, q, :], rows[r, i % 4, 0, q, :], removed[r, q, :], start=True, stop=False)
                        mm = pe.matmul(ps(3, 1)[r, q, :], rows[r, i % 4, 1, q, :], rows[r, i % 4, 2, q, :], start=False, stop=True)
                    mm.then_inc(s["moved"].sem, 1)

                parts = {"rest": rest_part, "removed": removed_part, "move": move_part}
                for i in range(0, NCH + 2, 2):
                    if i < NCH:
                        for j in (i, i + 1):
                            masked_products(j)
                            turn_updates(j)
                    for n in range(NL):
                        for a in range(2):
                            if i < NCH:
                                inner_part(i + a, n)
                            if i >= 2 and (n, a) in chain_at:
                                part, b = chain_at[n, a]
                                parts[part](i - 2 + b)
                        if i < NCH:
                            grow(i, n)
                            grow(i + 1, n)
                pe.wait_ge(s["normed"].sem, s["normed"] + 1)
                for f in range(2):
                    for c in range(NCH):
                        for r in (slice(0, 64), slice(64, 128)):
                            mm = pe.matmul(self.flat[r, 1024 * f + c * C:1024 * f + (c + 1) * C], y[0][r, c, f, :],
                                           self.c("ident64")[r, :], start=True, stop=True)
                mm.then_inc(s["turned"].sem, 1)

            @block.scalar
            def _(act):
                def copy_rows(i):
                    if i >= 4:
                        act.wait_ge(s["moved"].sem, s["moved"] + (i - 3))
                    for a, bank in enumerate((6, 7) if i % 2 == 0 else (7, 6)):
                        act.wait_ge(s["prep"].sem, s["prep"] + (5 * i + 4 + a))
                        for e in range(2):
                            turned = self.psum[0:C, bank, :].rearrange("p (q e d) -> p q e d", q=4, e=2)[:, :, e, :]
                            ins = act.copy(rows[64 * e:64 * e + 64, i % 4, a], turned)
                        ins.then_inc(s["copied"].sem, 1)

                for i in range(0, NCH + 2, 2):
                    if i < NCH:
                        copy_rows(i)
                        copy_rows(i + 1)
                    for n in range(NL):
                        for a in range(2):
                            if i < NCH:
                                act.wait_ge(s["inner"].sem, s["inner"] + (nth(i + a, n) + 1))
                                if n >= 1:
                                    act.wait_ge(s["grown"].sem, s["grown"] + (nth(i + a, n - 1) + 1))
                                act.copy(inner[:, a, :, :], ps(4 + a, 0)).then_inc(s["inner_copied"].sem, 1)
                            part, b = chain_at.get((n, a), ("", 0))
                            if i >= 2 and part == "rest":
                                act.wait_ge(s["rest"].sem, s["rest"] + (i - 2 + b + 1))
                                act.copy(rest[:, :, :], ps(2, 0)).then_inc(s["rest_copied"].sem, 1)
                            if i >= 2 and part == "removed":
                                act.wait_ge(s["removed"].sem, s["removed"] + (i - 2 + b + 1))
                                act.copy(removed[:, :, :], ps(2, 1)).then_inc(s["removed_copied"].sem, 1)
                act.wait_ge(s["var"].sem, s["var"] + 1)
                act.activation(st[:, 2, :], st[:, 1, :], ACT.Sqrt).then_inc(s["root"].sem, 1)

            @block.vector
            def _(dve):
                link = self.dve_chain.on(dve)

                def plain(a):
                    flat = lambda x: inv[:, a, x].rearrange("p q t -> p (q t)")
                    return dve.transpose(flat(1), flat(0))

                def mask(i):
                    full = lambda b: self.psum[:, b, :].rearrange("p (q a t) -> p q a t", q=4, a=2)
                    m = cc("mask").rearrange("p (q a t) -> p q a t", q=4, a=2)
                    quarter = lambda ap: ap.rearrange("p (q t) -> p q t", q=4)
                    a = i % 4
                    dve.wait_ge(s["prep"].sem, s["prep"] + (5 * i + 1))
                    if i >= 4:
                        dve.wait_ge(s["moved"].sem, s["moved"] + (i - 3))
                    dve.tensor_tensor(m_b[:, a], full(0), m, ALU.mult).then_inc(s["masked_b"].sem, 1)
                    dve.wait_ge(s["prep"].sem, s["prep"] + (5 * i + 2))
                    dve.tensor_tensor(m_k[:, a], full(1), m, ALU.mult).then_inc(s["masked_k"].sem, 1)
                    dve.wait_ge(s["masked_b"].sem, s["masked_b"] + (i + 1))
                    if i >= 2:
                        dve.wait_ge(s["grown"].sem, s["grown"] + (nth(i - 2, NL - 1) + 1))
                    dve.tensor_tensor(steps[:, i % 2, :, :, :], spread(m_b[:, a, :, 0, :], 1, NL),
                                      cc("level").rearrange("p (n q t) -> p n q t", n=NL, q=4), ALU.mult)
                    link(dve.tensor_tensor(inv[:, a, 0], m_b[:, a, :, 0, :], quarter(cc("first_t")), ALU.mult))
                    link(dve.tensor_tensor(inv[:, a, 0], inv[:, a, 0], spread(self.c("ident64"), 1, 4), ALU.add))
                    dve.wait_ge(s["prep"].sem, s["prep"] + (5 * i + 3))
                    for e in range(2):
                        turned = self.psum[0:C, 4 + i % 2, :].rearrange("p (q e d) -> p q e d", q=4, e=2)[:, :, e, :]
                        dve.tensor_copy(rows[64 * e:64 * e + 64, a, 2], turned)
                    plain(a).then_inc(s["blocks"].sem, 1)

                def move_state(j):
                    for d in range(2):
                        now, then = ch(2 * d, j), ch(2 * d, min(j + 1, NCH - 1))
                        link(dve.tensor_tensor(move[:, 2 * d:2 * d + 2], half[:, 2 * d:2 * d + 2, now],
                                               half[:, 2 * d:2 * d + 2, then], ALU.mult))
                    dve.wait_ge(s["moved"].sem, s["moved"] + (j + 1))
                    link(dve.tensor_tensor(state[:, :, :], state[:, :, :], ps(3, 1), ALU.add))
                    dve.tensor_tensor(state[:, :, :], state[:, :, :], spread(move[:, :], 2, C), ALU.mult).then_inc(s["state"].sem, 1)
                    dve.tensor_copy(y[0][:, ch(0, j), :, :], ps(3, 0)[:, 0:2, :])
                    dve.tensor_copy(y[1][:, ch(2, j), :, :], ps(3, 0)[:, 2:4, :]).then_inc(s["y_copied"].sem, 1)
                    dve.wait_ge(s["state"].sem, s["state"] + (j + 2))

                dve.memset(state[:, :, :], 0.0).then_inc(s["state"].sem, 1)
                for i in range(0, NCH + 2, 2):
                    if i < NCH:
                        mask(i)
                        mask(i + 1)
                    for n in range(NL):
                        part, b = chain_at.get((n, 0), ("", 0))
                        if i >= 2 and part == "move":
                            move_state(i - 2 + b)
                        if i < NCH:
                            for j in (i, i + 1):
                                dve.wait_ge(s["grown"].sem, s["grown"] + (nth(j, n) + 1))
                                if n == 0:
                                    dve.wait_ge(s["blocks"].sem, s["blocks"] + (j + 1))
                                else:
                                    dve.wait_ge(s["added"].sem, s["added"] + (nth(j, n - 1) + 1))
                                ins = dve.tensor_tensor(inv[:, j % 4, 0], inv[:, j % 4, 0], ps(6 + j % 2, 0), ALU.add)
                                if n < NL - 1:
                                    link(ins)
                                    ins = plain(j % 4)
                                ins.then_inc(s["added"].sem, 1)
                dve.wait_ge(s["y_copied"].sem, s["y_copied"] + NCH)
                sq = m_b[:, 0:3].rearrange("p a q b t -> p (a q b) t")
                y0, y1 = (a.rearrange("p c f t -> p (c f) t") for a in y)
                link(dve.tensor_tensor(y0, y0, y1, ALU.add))
                link(dve.tensor_reduce(st[:, 0, :], y0, AX, ALU.add))
                link(dve.tensor_scalar(st[:, 0, :], st[:, 0, :], 1.0 / 64, None, ALU.mult))
                link(dve.tensor_tensor(y0, y0, spread(st[:, 0, :], 2, C), ALU.subtract))
                link(dve.tensor_tensor(sq, y0, y0, ALU.mult))
                link(dve.tensor_reduce(st[:, 1, :], sq, AX, ALU.add))
                dve.tensor_scalar(st[:, 1, :], st[:, 1, :], 1.0 / 64, 64e-5, ALU.mult, ALU.add).then_inc(s["var"].sem, 1)
                dve.wait_ge(s["root"].sem, s["root"] + 1)
                link(dve.reciprocal(st[:, 3, :], st[:, 2, :]))
                link(dve.tensor_tensor(y0, y0, spread(st[:, 3, :], 2, C), ALU.mult))
                lnw = spread(self.row("ln_w").rearrange("p (f t) -> p f t", f=2), 1, NCH)
                dve.tensor_tensor(y[0], y[0], lnw, ALU.mult).then_inc(s["normed"].sem, 1)
                dve.wait_ge(s["turned"].sem, s["turned"] + 1)
                for f in range(2):
                    to = self.mix_t[:, 6 + f, :]
                    link(dve.tensor_tensor(to, self.flat[:, 1024 * f:1024 * f + TOK], bonus[:, f, :], ALU.add))
                    link(dve.tensor_tensor(to, to, g[:, f, :], ALU.mult))
        per = {"state": NCH + 1, "prep": 5 * NCH, "copied": 2 * NCH, **{n: NL * NCH for n in ("inner", "inner_copied", "grown", "added")},
               **{n: 1 for n in ("var", "root", "normed", "turned")}}
        for n in names:
            s[n].advance(per.get(n, NCH))

    def project_out(self, l, last, tiles):
        nc, io = self.nc, self.io
        landed = [self.count(f"w_out_landed{b}", 16) for b in range(2)]
        made, added = self.count("out_made"), self.count("out_added")
        with ExitStack() as scope:
            w = self.sbuf(scope, "w_out", [P, KD, D])
            tmp, junk = self.sbuf(scope, "gated", [P, D]), self.sbuf(scope, "squares", [P, D])
            block = scope.enter_context(nc.Block())

            @block.sync
            def _(sp):
                for b in range(2):
                    sp.dma_start(w[:, :, b * 512:(b + 1) * 512], io["w_out"][l, :, b * 512:(b + 1) * 512].rearrange(
                        "(k p) n -> p k n", p=P)).then_inc(landed[b].sem, 16)

            @block.tensor
            def _(pe):
                for n, t in enumerate(tiles):
                    if n >= 2:
                        pe.wait_ge(added.sem, added + (n - 1))
                    for b in range(2):
                        if n == 0:
                            pe.wait_ge(landed[b].sem, landed[b] + 1)
                        for k in range(KD):
                            mm = pe.matmul(self.psum[:, 2 * (n % 2) + b, :], self.mix_t[:, k, t * P:(t + 1) * P],
                                           w[:, k, b * 512:(b + 1) * 512], start=(k == 0), stop=(k == KD - 1))
                    mm.then_inc(made.sem, 1)

            @block.scalar
            def _(act):
                self.sum_squares(act, junk[:, :], tiles, added)

            @block.vector
            def _(dve):
                self.add_gated(dve, tmp, 0, tiles, made, added)
        for half in landed:
            half.advance(1)
        made.advance(len(tiles))
        added.advance(len(tiles))

    def add_gated(self, dve, tmp, which, tiles, made, added):
        link = self.dve_chain.on(dve)
        for n, t in enumerate(tiles):
            dve.wait_ge(made.sem, made + (n + 1))
            product = self.flat[:, 1024 * (n % 2):1024 * (n % 2) + D]
            if n >= 1:
                dve.wait_ge(added.sem, added + n)
            link(dve.tensor_tensor(tmp[:, :], product, self.gates[:, which, int(t < CT), :], ALU.mult))
            dve.tensor_tensor(self.x[:, t, :], self.x[:, t, :], tmp[:, :], ALU.add).then_inc(added.sem, 1)

    def route(self, l, last, tiles):
        nc, io = self.nc, self.io
        landed = self.count("router_landed", 16)
        names = ("by_expert", "logits_copied", "logits", "shifted", "exp", "affinity", "turned", "placed", "back")
        s = {n: self.count("route_" + n) for n in names}
        lo = tiles[0]
        groups = [(CT, NT, CAP_L)] + ([] if last else [(0, CT, CAP_C)])
        with ExitStack() as scope:
            sb = lambda name, shape: self.sbuf(scope, name, shape)
            w = sb("router_w", [P, KD, E_N])
            st = sb("router_stat", [P, 3, NT])
            work, chosen = sb("affinity_left", [E_N, TOK]), sb("chosen", [E_N, TOK])
            place, ones = sb("place", [E_N, TOK]), sb("scan_ones", [E_N, LAT])
            best = sb("best", [E_N, 8])
            block = scope.enter_context(nc.Block())
            logits = self.psum[:, 0, 0:NT * E_N].rearrange("p (t e) -> p t e", e=E_N)
            back = self.psum[:, 3, 0:NT * E_N].rearrange("p (t e) -> p t e", e=E_N)
            turned = lambda a, b: self.psum[0:E_N, 1 if a < CT else 2, 0:(b - a) * P]

            @block.sync
            def _(sp):
                sp.dma_start(w[:, :, :], io["router_w"][l].rearrange("(k p) n -> p k n", p=P)).then_inc(landed.sem, 16)
                for m in range(W_AHEAD):
                    self.load_expert_part(sp, l, 0, m)

            @block.tensor
            def _(pe):
                pe.wait_ge(landed.sem, landed + 1)
                for a, b, _ in groups:
                    for k in range(KD):
                        mm = pe.matmul(turned(a, b), w[:, k, :], self.u_t[:, k, a * P:b * P],
                                       start=(k == 0), stop=(k == KD - 1))
                    mm.then_inc(s["by_expert"].sem, 1)
                pe.wait_ge(s["logits_copied"].sem, s["logits_copied"] + len(groups))
                for t in tiles:
                    mm = pe.transpose(logits[:, t, :], work[:, t * P:(t + 1) * P], self.c("ident")[0:E_N, 0:E_N])
                mm.then_inc(s["logits"].sem, 1)
                pe.wait_ge(s["affinity"].sem, s["affinity"] + 1)
                for a, b, _ in groups:
                    for t in range(a, b):
                        mm = pe.transpose(turned(a, b)[:, (t - a) * P:(t - a + 1) * P], self.aff[:, t, :], self.c("ident"))
                mm.then_inc(s["turned"].sem, 1)
                pe.wait_ge(s["placed"].sem, s["placed"] + 1)
                for t in tiles:
                    mm = pe.transpose(back[:, t, :], place[:, t * P:(t + 1) * P], self.c("ident")[0:E_N, 0:E_N])
                mm.then_inc(s["back"].sem, 1)

            @block.scalar
            def _(act):
                for n, (a, b, _) in enumerate(groups):
                    act.wait_ge(s["by_expert"].sem, s["by_expert"] + (n + 1))
                    act.copy(work[:, a * P:b * P], turned(a, b)).then_inc(s["logits_copied"].sem, 1)
                act.wait_ge(s["shifted"].sem, s["shifted"] + 1)
                act.activation(self.aff[:, lo:NT, :], self.aff[:, lo:NT, :], ACT.Exp).then_inc(s["exp"].sem, 1)

            @block.vector
            def _(dve):
                link = self.dve_chain.on(dve)
                link(dve.memset(ones[:, :], 1.0))
                dve.wait_ge(s["logits"].sem, s["logits"] + 1)
                aff = self.aff[:, lo:NT, :]
                link(dve.tensor_reduce(st[:, 0, lo:NT], logits[:, lo:NT, :], AX, ALU.max))
                dve.tensor_tensor(aff, logits[:, lo:NT, :], spread(st[:, 0, lo:NT], 2, E_N), ALU.subtract).then_inc(s["shifted"].sem, 1)
                dve.wait_ge(s["exp"].sem, s["exp"] + 1)
                link(dve.tensor_reduce(st[:, 1, lo:NT], aff, AX, ALU.add))
                link(dve.reciprocal(st[:, 2, lo:NT], st[:, 1, lo:NT]))
                dve.tensor_tensor(aff, aff, spread(st[:, 2, lo:NT], 2, E_N), ALU.mult).then_inc(s["affinity"].sem, 1)
                dve.wait_ge(s["turned"].sem, s["turned"] + 1)
                for n, (a, b, cap) in enumerate(groups):
                    cut = slice(a * P, b * P)
                    link(dve.tensor_copy(work[:, cut], turned(a, b)))
                    for _ in range(cap // 8):
                        link(dve.max(best[:, :], work[:, cut]))
                        link(dve.match_replace(work[:, cut], best[:, :], work[:, cut], -1.0))
                    link(dve.tensor_scalar(chosen[:, cut], work[:, cut], -1.0, None, ALU.is_equal))
                    link(dve.tensor_tensor_scan(place[:, cut], ones[:, 0:(b - a) * P], chosen[:, cut], 0.0, ALU.mult, ALU.add))
                    link(dve.tensor_tensor(place[:, cut], place[:, cut], chosen[:, cut], ALU.mult))
                    ins = dve.tensor_scalar(place[:, cut], place[:, cut], 1.0, None, ALU.subtract)
                    if n == len(groups) - 1:
                        ins.then_inc(s["placed"].sem, 1)
                    else:
                        link(ins)
                dve.wait_ge(s["back"].sem, s["back"] + 1)
                link(dve.tensor_copy(self.slot[:, lo:NT, :], back[:, lo:NT, :]))
        landed.advance(1)
        for n in names:
            s[n].advance(len(groups) if n in ("by_expert", "logits_copied") else 1)

    def gather(self, l, last):
        nc = self.nc
        onehot, gathered = self.count("gather_onehot"), self.count("gathered")
        kept = [self.count("gather_kept_dve"), self.count("gather_kept_act")]
        halves = 2
        items = [(CT, NT, CAP_L, 0, g * E_N // halves, (g + 1) * E_N // halves, k) for k in range(KD) for g in range(halves)] + \
                ([] if last else [(0, CT, CAP_C, 1, 0, E_N, k) for k in range(KD)])
        with ExitStack() as scope:
            hot_l = self.sbuf(scope, "onehot_lat", [P, NT - CT, E_N, CAP_L])
            hot_c = self.sbuf(scope, "onehot_ctx", [P, CT, E_N, CAP_C])
            block = scope.enter_context(nc.Block())

            def result(i):
                a, b, cap, v, e0, e1, k = items[i]
                at = 0 if cap == CAP_L else CAP_L
                return (self.chosen[:, e0:e1, k, at:at + cap],
                        self.psum[:, i % 4, 0:(e1 - e0) * cap].rearrange("p (e c) -> p e c", c=cap),
                        self.scale2[:, k, v:v + 1], self.mod[:, 24 + k, v:v + 1])

            @block.tensor
            def _(pe):
                pe.wait_ge(onehot.sem, onehot + 1)
                for i, (a, b, cap, v, e0, e1, k) in enumerate(items):
                    if i >= 4:
                        pe.wait_ge(kept[i % 2].sem, kept[i % 2] + ((i - 4) // 2 + 1))
                    hot = hot_l if cap == CAP_L else hot_c
                    for t in range(a, b):
                        mm = pe.matmul(self.psum[:, i % 4, 0:(e1 - e0) * cap], self.xn[:, t, k * P:(k + 1) * P],
                                       hot[:, t - a, e0:e1, :].rearrange("p e c -> p (e c)"), start=(t == a), stop=(t == b - 1))
                    mm.then_inc(gathered.sem, 1)

            @block.scalar
            def _(act):
                for i in range(1, len(items), 2):
                    to, got, scale, shift = result(i)
                    act.wait_ge(gathered.sem, gathered + (i + 1))
                    act.activation(to, got, ACT.Identity, bias=shift, scale=scale).then_inc(kept[1].sem, 1)

            @block.vector
            def _(dve):
                cuts = [(t, hot_l[:, t - CT], CAP_L) for t in range(CT, NT)] + ([] if last else [(t, hot_c[:, t], CAP_C) for t in range(CT)])
                for t, hot, cap in cuts:
                    ins = dve.tensor_tensor(hot, spread(self.c("iota")[:, 0:cap], 1, E_N), spread(self.slot[:, t, :], 2, cap), ALU.is_equal)
                ins.then_inc(onehot.sem, 1)
                for i in range(0, len(items), 2):
                    to, got, scale, shift = result(i)
                    dve.wait_ge(gathered.sem, gathered + (i + 1))
                    dve.tensor_scalar(to, got, scale, shift, ALU.mult, ALU.add).then_inc(kept[0].sem, 1)
        onehot.advance(1)
        gathered.advance(len(items))
        for side in kept:
            side.advance(len(items) // 2)

    def load_expert_part(self, sp, l, expert, m):
        name, h = W_PARTS[m % len(W_PARTS)]
        src = self.io[name][l].rearrange("e (k p) n -> p e k n", p=P)
        src = src[:, expert, :, h * 512:(h + 1) * 512] if isinstance(expert, int) else \
            src[:, bass.ds(expert, 1), :, h * 512:(h + 1) * 512].rearrange("p e k n -> p (e k) n")
        landed = self.count(f"expert_w_landed{m % W_SLOTS}", 16)
        sp.dma_start(self.expert_w[:, m % W_SLOTS, :, :], src).then_inc(landed.sem, 16)

    def experts(self, l, last, scope):
        nc = self.nc
        UNROLL = 4
        landed = [self.count(f"expert_w_landed{i}", 16) for i in range(W_SLOTS)]
        multiplied = [self.count(f"expert_w_multiplied{i}") for i in range(W_SLOTS)]
        names = ("sigmoid", "gated", "hidden", "stored")
        s = {n: self.count("expert_" + n) for n in names}
        M = CAP_L + (0 if last else CAP_C)
        per_body = UNROLL * len(W_PARTS)
        rounds = per_body // W_SLOTS
        nth = lambda i, m: i * rounds + (m // W_SLOTS + 1)
        for first in (*multiplied, s["hidden"], s["stored"]):
            first.advance(1)
        sb = lambda name, shape: self.sbuf(scope, name, shape)
        w = self.expert_w
        sig, hid = sb("expert_sigmoid", [P, 2, 4 * M]), sb("expert_hidden", [P, 2, 4 * M])
        hidden = hid[:, :, :].rearrange("p h (f m) -> p (h f) m", f=4)
        with nc.Block() as block:
            @block.sync
            def _(sp):
                def load(i, m):
                    slot = m % W_SLOTS
                    sp.wait_ge(multiplied[slot].sem, multiplied[slot] + (nth(i, m) - 1))
                    self.load_expert_part(sp, l, (i + m // per_body) * UNROLL + m % per_body // len(W_PARTS), m)

                with sp.Fori(0, E_N // UNROLL - 1) as i:
                    for m in range(W_AHEAD, per_body + W_AHEAD):
                        load(i, m)
                for m in range(W_AHEAD, per_body):
                    load(E_N // UNROLL - 1, m)

            @block.tensor
            def _(pe):
                def to_features(i, m, bank, tokens):
                    for h in range(2):
                        slot = (m + h) % W_SLOTS
                        pe.wait_ge(landed[slot].sem, landed[slot] + nth(i, m + h))
                        for f in range(4):
                            for k in range(KD):
                                mm = pe.matmul(self.psum[:, bank + h, f * M:(f + 1) * M], w[:, slot, k, f * P:(f + 1) * P],
                                               tokens(k), start=(k == 0), stop=(k == KD - 1))
                        mm.then_inc(multiplied[slot].sem, 1)

                def to_tokens(i, n, m, bank):
                    for h in range(2):
                        slot = (m + h) % W_SLOTS
                        pe.wait_ge(landed[slot].sem, landed[slot] + nth(i, m + h))
                        for k in range(KD):
                            if h == 0 and k % 4 == 0:
                                pe.wait_ge(s["hidden"].sem, s["hidden"] + (n * 2 + (k // 4 + 1)))
                            mm = pe.matmul(self.psum[0:M, bank + h, :], hidden[:, k, :], w[:, slot, k, :],
                                           start=(k == 0), stop=(k == KD - 1))
                        mm.then_inc(multiplied[slot].sem, 1)

                for slot in range(W_SLOTS):
                    pe.matmul(self.psum[0:1, 2, 511:512], self.c("ident")[:, 0:1], self.c("ident")[:, 0:1],
                              start=True, stop=True).then_inc(multiplied[slot].sem, 1)
                with pe.Fori(0, E_N // UNROLL) as i:
                    for j in range(UNROLL):
                        n, m = i * UNROLL + j, j * len(W_PARTS)
                        tokens = lambda k: self.chosen[:, bass.ds(n, 1), k, :].rearrange("p e m -> p (e m)")
                        to_features(i, m, 2, tokens)
                        to_features(i, m + 2, 4, tokens)
                        pe.wait_ge(s["stored"].sem, s["stored"] + n)
                        to_tokens(i, n, m + 4, 6)

            @block.scalar
            def _(act):
                act.copy(self.stat[0:1, 0:1], self.c("iota")[0:1, 0:1]).then_inc(s["stored"].sem, 1)
                with act.Fori(0, E_N // UNROLL) as i:
                    for j in range(UNROLL):
                        n, m = i * UNROLL + j, j * len(W_PARTS)
                        act.wait_ge(s["hidden"].sem, s["hidden"] + n * 2)
                        for h in range(2):
                            gate = multiplied[(m + h) % W_SLOTS]
                            act.wait_ge(gate.sem, gate + nth(i, m + h))
                            act.activation(sig[:, h, :], self.psum[:, 2 + h, 0:4 * M], ACT.Sigmoid).then_inc(s["sigmoid"].sem, 1)
                        down = multiplied[(m + 5) % W_SLOTS]
                        act.wait_ge(down.sem, down + nth(i, m + 5))
                        y, e = self.flat[:, 3072:4096], j % 2
                        ins = act.copy(self.y_lat[64 * e:64 * e + 64, bass.ds(i * 2 + j // 2, 1), :].rearrange("p a n -> p (a n)"),
                                       y[0:CAP_L, :])
                        if not last:
                            ins = act.copy(self.y_ctx[32 * j:32 * j + 32, bass.ds(i, 1), :].rearrange("p a n -> p (a n)"),
                                           y[CAP_L:M, :])
                        ins.then_inc(s["stored"].sem, 1)

            @block.vector
            def _(dve):
                dve.memset(self.stat[0:1, 1:2], 0.0).then_inc(s["hidden"].sem, 1)
                with dve.Fori(0, E_N // UNROLL) as i:
                    for j in range(UNROLL):
                        n, m = i * UNROLL + j, j * len(W_PARTS)
                        for h in range(2):
                            dve.wait_ge(s["sigmoid"].sem, s["sigmoid"] + (n * 2 + (h + 1)))
                            dve.tensor_tensor(sig[:, h, :], sig[:, h, :], self.psum[:, 2 + h, 0:4 * M], ALU.mult).then_inc(s["gated"].sem, 1)
                        for h in range(2):
                            dve.wait_ge(s["gated"].sem, s["gated"] + (n * 2 + (h + 1)))
                            up = multiplied[(m + 2 + h) % W_SLOTS]
                            dve.wait_ge(up.sem, up + nth(i, m + 2 + h))
                            dve.tensor_tensor(hid[:, h, :], sig[:, h, :], self.psum[:, 4 + h, 0:4 * M], ALU.mult).then_inc(s["hidden"].sem, 1)
        for slot in range(W_SLOTS):
            landed[slot].advance(rounds * E_N // UNROLL)
            multiplied[slot].advance(rounds * E_N // UNROLL)
        for n in names:
            s[n].advance(E_N * (1 if n == "stored" else 2))

    def combine(self, l, last, tiles):
        nc = self.nc
        names = ("weights", "turned", "copied", "made", "added")
        s = {n: self.count("combine_" + n) for n in names}
        groups = [(CT, NT, g, 2, CAP_L) for g in range(E_N // 2)] + \
                 ([] if last else [(0, CT, g, 4, CAP_C) for g in range(E_N // 4)])
        with ExitStack() as scope:
            sb = lambda name, shape: self.sbuf(scope, name, shape)
            hot = sb("weighted_onehot", [P, 2, LAT])
            spare = self.expert_w[:, :, :, :].rearrange("p s k n -> p (s k n)")
            back_l = spare[:, 0:E_N // 2 * LAT].rearrange("p (g t) -> p g t", t=LAT)
            back_c = spare[:, 4096:4096 + E_N // 4 * CTX].rearrange("p (g t) -> p g t", t=CTX)
            tmp = sb("gated_experts", [P, D])
            block = scope.enter_context(nc.Block())

            @block.tensor
            def _(pe):
                for n, (a, b, g, per, cap) in enumerate(groups):
                    pe.wait_ge(s["weights"].sem, s["weights"] + (n + 1))
                    if n >= 2:
                        pe.wait_ge(s["copied"].sem, s["copied"] + (n - 1))
                    for t in range(b - a):
                        mm = pe.transpose(self.psum[:, 4 + n % 2, t * P:(t + 1) * P], hot[:, n % 2, t * P:(t + 1) * P], self.c("ident"))
                    mm.then_inc(s["turned"].sem, 1)
                pe.wait_ge(s["copied"].sem, s["copied"] + len(groups))
                for n, t in enumerate(tiles):
                    if n >= 2:
                        pe.wait_ge(s["added"].sem, s["added"] + (n - 1))
                    back, y, k, t0 = (back_c, self.y_ctx, E_N // 4, t) if t < CT else (back_l, self.y_lat, E_N // 2, t - CT)
                    for b in range(2):
                        for g in range(k):
                            mm = pe.matmul(self.psum[:, 2 * (n % 2) + b, :], back[:, g, t0 * P:(t0 + 1) * P],
                                           y[:, g, b * 512:(b + 1) * 512], start=(g == 0), stop=(g == k - 1))
                    mm.then_inc(s["made"].sem, 1)

            @block.scalar
            def _(act):
                for n, (a, b, g, per, cap) in enumerate(groups):
                    act.wait_ge(s["turned"].sem, s["turned"] + (n + 1))
                    to = (back_c if a < CT else back_l)[:, g, :]
                    act.copy(to, self.psum[:, 4 + n % 2, 0:(b - a) * P]).then_inc(s["copied"].sem, 1)
                if not last:
                    self.sum_squares(act, spare[:, 6144:6144 + D], tiles, s["added"])

            @block.vector
            def _(dve):
                link = self.dve_chain.on(dve)
                for n, (a, b, g, per, cap) in enumerate(groups):
                    if n >= 2:
                        dve.wait_ge(s["turned"].sem, s["turned"] + (n - 1))
                    to = hot[:, n % 2, 0:(b - a) * P].rearrange("p (t e c) -> p t e c", e=per, c=cap)
                    of = lambda x: spread(x[:, a:b, g * per:(g + 1) * per], 3, cap)
                    iota = spread(spread(self.c("iota")[:, 0:cap], 1, per), 1, b - a)
                    link(dve.tensor_tensor(to, iota, of(self.slot), ALU.is_equal))
                    dve.tensor_tensor(to, to, of(self.aff), ALU.mult).then_inc(s["weights"].sem, 1)
                self.add_gated(dve, tmp, 1, tiles, s["made"], s["added"])
        for n in names:
            s[n].advance(len(tiles) if n in ("made", "added") else len(groups))

    def store(self):
        nc, io = self.nc, self.io
        stored = self.count("output_stored", 16)
        with nc.Block() as block:
            @block.sync
            def _(sp):
                sp.dma_start(io["out"].rearrange("(t p) d -> p t d", p=P), self.x[:, CT:NT, :]).then_inc(stored.sem, 16)
                sp.wait_ge(stored.sem, stored + 1)


_WHOLE = ["mod_w", "w_in", "mla_w_uq", "mla_w_ukv", "rwkv_w2", "rwkv_a2", "rwkv_g2", "w_out", "router_w",
          "exp_w_gate", "exp_w_up", "exp_w_down"]


def _by_feature(a):
    return np.asarray(a).reshape(-1, P).T


def kernel(**inputs):
    import concourse.bacc as bacc
    from concourse.bass_utils import run_bass_kernel_spmd

    a = {k: np.asarray(v) for k, v in inputs.items()}
    cols, rows = [], []
    for l in range(DEPTH):
        mu = np.zeros(9 * P, np.float32)
        mu[0:896], mu[896:960], mu[1024:1152] = a["rwkv_mu"][l, 0:896], a["rwkv_mu"][l, 896:960], a["rwkv_mu"][l, 960:1088]
        cols.append(np.concatenate([_by_feature(x) for x in (
            a["mod_b"][l], a["norm1_w"][l], a["norm2_w"][l],
            np.concatenate([a["mla_q_norm_w"][l], a["mla_kv_norm_w"][l]]), mu, a["rwkv_w0"][l], a["rwkv_a0"][l],
            a["rwkv_k_k"][l], a["rwkv_k_a"][l], a["rwkv_r_k"][l])], 1))
        ln = a["rwkv_ln_w"][l].reshape(2, 2, 64)
        row = [a["mla_q_gain"][l], a["mla_k_gain"][l], a["ret_decay"][l].reshape(-1), a["ret_gn_w"][l]]
        rows.append(np.concatenate(
            [np.broadcast_to(np.concatenate(row), (P, ROWS_N - 128)),
             np.concatenate([np.broadcast_to(ln[:, e].reshape(-1), (64, 128)) for e in range(2)], 0)], 1))
    base, retc, rwkvc = constants()
    arrays = {"x": a["x"][0], "ctx": a["ctx"][0],
              "cvec": np.stack([_by_feature(a["c"][0]), _by_feature(a["c_ctx"])], 2),
              "cols": np.stack(cols), "rows": np.stack(rows), "base": base, "retc": retc, "rwkvc": rwkvc}
    for name in _WHOLE:
        arrays[name] = a[name]
    nc = bacc.Bacc("TRN2", target_bir_lowering=False, num_devices=1)
    io, fed = {}, {}
    for name, x in arrays.items():
        x = np.ascontiguousarray(x)
        fed[f"in_{name}"] = x
        io[name] = nc.dram_tensor(f"in_{name}", x.shape, mybir.dt.from_np(x.dtype), kind="ExternalInput").ap()
    io["out"] = nc.dram_tensor("out_0", (LAT, D), F32, kind="ExternalOutput").ap()
    build(nc, io)
    r = run_bass_kernel_spmd(nc, [fed], core_ids=[0])
    return r.results[0]["out_0"].reshape(1, LAT, D)
```
